# Optimizing a Trainium2 kernel written in Bass

```python
import math
import jax, jax.numpy as jnp
from jax import lax
import numpy as np

D_MODEL = 1024
BATCH = 1
SEQ = 512
DEPTH = 1

N_META = 16
SSM_WIDTH = D_MODEL // 2
SSM_GROUP = 16
SSM_GROUPS = SSM_WIDTH // SSM_GROUP
SSM_STATE = 64
MLSTM_WIDTH = D_MODEL // 2
MLSTM_HEADS = 4
MLSTM_HEAD_DIM = MLSTM_WIDTH // MLSTM_HEADS
MLSTM_CHUNK = 64
QK_CONV = 4
FFN_DIM = 2816
FFN_CONV = 3
NORM_EPS = 1e-6
PAD_LOG_INPUT_GATE = -1e4
IN_WIDTHS = (SSM_WIDTH, MLSTM_WIDTH, MLSTM_WIDTH, MLSTM_WIDTH, MLSTM_WIDTH, MLSTM_HEADS, MLSTM_HEADS, D_MODEL, D_MODEL)
IN_SPLITS = tuple(int(s) for s in np.cumsum(IN_WIDTHS)[:-1])
N_IN = int(sum(IN_WIDTHS))


def rmsnorm(x, g):
    xf = x.astype(jnp.float32)
    y = xf * lax.rsqrt(jnp.mean(xf * xf, axis=-1, keepdims=True) + NORM_EPS)
    return (y * g.astype(jnp.float32)).astype(x.dtype)

def causal_dwconv(x, w, b):
    k = w.shape[0]
    y = lax.conv_general_dilated(x, w[:, None, :].astype(x.dtype), (1,), [(k - 1, 0)],
                                 dimension_numbers=('NWC', 'WIO', 'NWC'),
                                 feature_group_count=x.shape[-1])
    return y + b.astype(x.dtype)

def _complex_affine_combine(e1, e2):
    a1r, a1i, b1r, b1i = e1
    a2r, a2i, b2r, b2i = e2
    return (a2r * a1r - a2i * a1i,
            a2r * a1i + a2i * a1r,
            a2r * b1r - a2i * b1i + b2r,
            a2r * b1i + a2i * b1r + b2i)

def s5_ssm(u, lam_re, lam_im, b_re, b_im, c_re, c_im, d, log_dt):
    bsz, L, _ = u.shape
    u = u.astype(jnp.float32).reshape(bsz, L, SSM_GROUPS, SSM_GROUP)
    lam_re = lam_re.astype(jnp.float32)
    lam_im = lam_im.astype(jnp.float32)
    dt = jnp.exp(log_dt.astype(jnp.float32))[:, None]
    mag = jnp.exp(lam_re * dt)
    ab_re = mag * jnp.cos(lam_im * dt)
    ab_im = mag * jnp.sin(lam_im * dt)
    nr, ni = ab_re - 1.0, ab_im
    den = lam_re * lam_re + lam_im * lam_im
    z_re = (nr * lam_re + ni * lam_im) / den
    z_im = (ni * lam_re - nr * lam_im) / den
    b_re = b_re.astype(jnp.float32)
    b_im = b_im.astype(jnp.float32)
    bb_re = z_re[..., None] * b_re - z_im[..., None] * b_im
    bb_im = z_re[..., None] * b_im + z_im[..., None] * b_re
    bu_re = jnp.einsum('blgh,gph->blgp', u, bb_re)
    bu_im = jnp.einsum('blgh,gph->blgp', u, bb_im)
    a_re = jnp.broadcast_to(ab_re, bu_re.shape)
    a_im = jnp.broadcast_to(ab_im, bu_im.shape)
    _, _, x_re, x_im = lax.associative_scan(_complex_affine_combine, (a_re, a_im, bu_re, bu_im), axis=1)
    y = (jnp.einsum('blgp,ghp->blgh', x_re, c_re.astype(jnp.float32))
         - jnp.einsum('blgp,ghp->blgh', x_im, c_im.astype(jnp.float32))
         + d.astype(jnp.float32) * u)
    return y.reshape(bsz, L, SSM_WIDTH)

def mlstm_chunkwise(q, k, v, log_i, log_f):
    bsz, lp, nh, dh = q.shape
    nc = lp // MLSTM_CHUNK

    def to_chunks(t):
        return jnp.moveaxis(t.reshape(bsz, nc, MLSTM_CHUNK, nh, -1), 3, 1)

    q, k, v = to_chunks(q), to_chunks(k), to_chunks(v)
    log_i = to_chunks(log_i[..., None])[..., 0]
    log_f = to_chunks(log_f[..., None])[..., 0]
    b = jnp.cumsum(log_f, axis=-1)
    g = b[..., -1]
    causal = jnp.tril(jnp.ones((MLSTM_CHUNK, MLSTM_CHUNK), dtype=bool))
    log_d = jnp.where(causal, b[..., :, None] - b[..., None, :] + log_i[..., None, :], -jnp.inf)
    a = g[..., None] - b + log_i

    def step(carry, xs):
        c_st, n_st, m_st = carry
        k_c, v_c, a_c, g_c = xs
        m_new = jnp.maximum(g_c + m_st, jnp.max(a_c, axis=-1))
        decay = jnp.exp(g_c + m_st - m_new)
        w = jnp.exp(a_c - m_new[..., None])
        c_new = decay[..., None, None] * c_st + jnp.einsum('bhs,bhsd,bhse->bhde', w, v_c, k_c)
        n_new = decay[..., None] * n_st + jnp.einsum('bhs,bhse->bhe', w, k_c)
        return (c_new, n_new, m_new), (c_st, n_st, m_st)

    init = (jnp.zeros((bsz, nh, dh, dh), jnp.float32),
            jnp.zeros((bsz, nh, dh), jnp.float32),
            jnp.zeros((bsz, nh), jnp.float32))
    xs = (jnp.moveaxis(k, 2, 0), jnp.moveaxis(v, 2, 0), jnp.moveaxis(a, 2, 0), jnp.moveaxis(g, 2, 0))
    _, (c_prev, n_prev, m_prev) = lax.scan(step, init, xs)
    c_prev = jnp.moveaxis(c_prev, 0, 2)
    n_prev = jnp.moveaxis(n_prev, 0, 2)
    m_prev = jnp.moveaxis(m_prev, 0, 2)
    log_inter = b + m_prev[..., None]
    m_t = jnp.maximum(log_inter, jnp.max(log_d, axis=-1))
    s = jnp.einsum('bhnte,bhnse->bhnts', q, k) * jnp.exp(log_d - m_t[..., None])
    w_inter = jnp.exp(log_inter - m_t)
    num = (jnp.einsum('bhnts,bhnsd->bhntd', s, v)
           + w_inter[..., None] * jnp.einsum('bhnde,bhnte->bhntd', c_prev, q))
    den = jnp.sum(s, axis=-1) + w_inter * jnp.einsum('bhne,bhnte->bhnt', n_prev, q)
    h = num / jnp.maximum(jnp.abs(den), jnp.exp(-m_t))[..., None]
    return jnp.moveaxis(h, 1, 3).reshape(bsz, lp, nh, dh)

def token_mixer(x, g_pre, g_post, w_in, b_gates, lam_re, lam_im, b_re, b_im, c_re, c_im, d, log_dt,
                w_glu, w_qk, b_qk, g_head, w_a, w_b, w_out):
    bsz, L, _ = x.shape
    dtype = x.dtype
    h = rmsnorm(x, g_pre)
    proj = h @ w_in
    u, q, k, v, o, gi, gf, ga, gb = jnp.split(proj, IN_SPLITS, axis=-1)

    y_a = jax.nn.gelu(s5_ssm(u, lam_re, lam_im, b_re, b_im, c_re, c_im, d, log_dt))
    y_a = y_a * jax.nn.sigmoid(y_a @ w_glu.astype(jnp.float32))

    qk = jax.nn.silu(causal_dwconv(jnp.concatenate([q, k], axis=-1), w_qk, b_qk)).astype(jnp.float32)
    q, k = jnp.split(qk, 2, axis=-1)
    heads = lambda t: t.reshape(bsz, L, MLSTM_HEADS, MLSTM_HEAD_DIM)
    q = heads(q)
    k = heads(k) * (MLSTM_HEAD_DIM ** -0.5)
    v = heads(v.astype(jnp.float32))
    gates = (jnp.concatenate([gi, gf], axis=-1) + b_gates.astype(dtype)).astype(jnp.float32)
    log_i, f_pre = jnp.split(gates, 2, axis=-1)
    log_f = jax.nn.log_sigmoid(f_pre)
    pad = MLSTM_CHUNK - N_META
    padseq = lambda t, val: jnp.pad(t, [(0, 0), (pad, 0)] + [(0, 0)] * (t.ndim - 2), constant_values=val)
    hb = mlstm_chunkwise(padseq(q, 0.0), padseq(k, 0.0), padseq(v, 0.0),
                         padseq(log_i, PAD_LOG_INPUT_GATE), padseq(log_f, 0.0))[:, pad:]
    hb = hb * lax.rsqrt(jnp.mean(hb * hb, axis=-1, keepdims=True) + NORM_EPS)
    hb = hb * g_head.astype(jnp.float32).reshape(MLSTM_HEADS, MLSTM_HEAD_DIM)
    y_b = hb.reshape(bsz, L, MLSTM_WIDTH) * jax.nn.sigmoid(o.astype(jnp.float32))

    merged = (jax.nn.sigmoid(ga) * (y_a.astype(dtype) @ w_a)
              + jax.nn.sigmoid(gb) * (y_b.astype(dtype) @ w_b))
    return x + rmsnorm(merged @ w_out, g_post)

def channel_mixer(x, g_pre, g_post, w_gate, w_up, w_conv, b_conv, w_down):
    h = rmsnorm(x, g_pre)
    a = causal_dwconv(h @ w_gate, w_conv, b_conv)
    y = (jax.nn.gelu(a, approximate=True) * (h @ w_up)) @ w_down
    return x + rmsnorm(y, g_post)

def first_inputs(seed: int = 0) -> dict:
    key = jax.random.key(seed)
    ks = iter(jax.random.split(key, 40))
    f32 = jnp.float32
    nrm = lambda shape, scale: scale * jax.random.normal(next(ks), shape, f32)
    gain = lambda: 1.0 + nrm((DEPTH, D_MODEL), 0.02)
    G, P, GH, H = SSM_GROUPS, SSM_STATE, SSM_GROUP, MLSTM_HEADS
    x = nrm((BATCH, SEQ, D_MODEL), 1.0)
    meta_tokens = nrm((N_META, D_MODEL), 1.0)
    g_mix_pre = gain()
    g_mix_post = gain()
    w_in = nrm((DEPTH, D_MODEL, N_IN), D_MODEL ** -0.5)
    b_gates = jnp.concatenate([nrm((DEPTH, H), 0.1),
                               jnp.linspace(3.0, 6.0, H, dtype=f32)[None, :] + nrm((DEPTH, H), 0.1)], axis=-1)
    n_idx = jnp.arange(P, dtype=f32)
    ssm_lambda_re = -0.5 + nrm((DEPTH, G, P), 0.01)
    ssm_lambda_im = jnp.pi * n_idx[None, None, :] + nrm((DEPTH, G, P), 0.01)
    ssm_b_re = nrm((DEPTH, G, P, GH), (2 * GH) ** -0.5)
    ssm_b_im = nrm((DEPTH, G, P, GH), (2 * GH) ** -0.5)
    ssm_c_re = nrm((DEPTH, G, GH, P), P ** -0.5)
    ssm_c_im = nrm((DEPTH, G, GH, P), P ** -0.5)
    ssm_d = nrm((DEPTH, G, GH), 1.0)
    ssm_log_dt = jax.random.uniform(next(ks), (DEPTH, G), f32, math.log(1e-3), math.log(1e-1))
    w_ssm_glu = nrm((DEPTH, SSM_WIDTH, SSM_WIDTH), SSM_WIDTH ** -0.5)
    w_qk_conv = nrm((DEPTH, QK_CONV, 2 * MLSTM_WIDTH), QK_CONV ** -0.5)
    b_qk_conv = nrm((DEPTH, 2 * MLSTM_WIDTH), 0.02)
    g_head_norm = 1.0 + nrm((DEPTH, MLSTM_WIDTH), 0.02)
    w_branch_ssm = nrm((DEPTH, SSM_WIDTH, D_MODEL), SSM_WIDTH ** -0.5)
    w_branch_mlstm = nrm((DEPTH, MLSTM_WIDTH, D_MODEL), MLSTM_WIDTH ** -0.5)
    w_out = nrm((DEPTH, D_MODEL, D_MODEL), D_MODEL ** -0.5)
    g_ffn_pre = gain()
    g_ffn_post = gain()
    w_ffn_gate = nrm((DEPTH, D_MODEL, FFN_DIM), D_MODEL ** -0.5)
    w_ffn_up = nrm((DEPTH, D_MODEL, FFN_DIM), D_MODEL ** -0.5)
    w_ffn_conv = nrm((DEPTH, FFN_CONV, FFN_DIM), FFN_CONV ** -0.5)
    b_ffn_conv = nrm((DEPTH, FFN_DIM), 0.02)
    w_ffn_down = nrm((DEPTH, FFN_DIM, D_MODEL), FFN_DIM ** -0.5)
    return {'x': x, 'meta_tokens': meta_tokens, 'g_mix_pre': g_mix_pre, 'g_mix_post': g_mix_post,
            'w_in': w_in, 'b_gates': b_gates, 'ssm_lambda_re': ssm_lambda_re, 'ssm_lambda_im': ssm_lambda_im,
            'ssm_b_re': ssm_b_re, 'ssm_b_im': ssm_b_im, 'ssm_c_re': ssm_c_re, 'ssm_c_im': ssm_c_im,
            'ssm_d': ssm_d, 'ssm_log_dt': ssm_log_dt, 'w_ssm_glu': w_ssm_glu, 'w_qk_conv': w_qk_conv,
            'b_qk_conv': b_qk_conv, 'g_head_norm': g_head_norm, 'w_branch_ssm': w_branch_ssm,
            'w_branch_mlstm': w_branch_mlstm, 'w_out': w_out, 'g_ffn_pre': g_ffn_pre, 'g_ffn_post': g_ffn_post,
            'w_ffn_gate': w_ffn_gate, 'w_ffn_up': w_ffn_up, 'w_ffn_conv': w_ffn_conv, 'b_ffn_conv': b_ffn_conv,
            'w_ffn_down': w_ffn_down}

def first_block(x, meta_tokens, g_mix_pre, g_mix_post, w_in, b_gates, ssm_lambda_re, ssm_lambda_im,
              ssm_b_re, ssm_b_im, ssm_c_re, ssm_c_im, ssm_d, ssm_log_dt, w_ssm_glu, w_qk_conv,
              b_qk_conv, g_head_norm, w_branch_ssm, w_branch_mlstm, w_out, g_ffn_pre, g_ffn_post,
              w_ffn_gate, w_ffn_up, w_ffn_conv, b_ffn_conv, w_ffn_down):
    bsz = x.shape[0]
    meta = jnp.broadcast_to(meta_tokens.astype(x.dtype)[None], (bsz, N_META, D_MODEL))
    h = jnp.concatenate([meta, x], axis=1)
    for l in range(DEPTH):
        h = token_mixer(h, g_mix_pre[l], g_mix_post[l], w_in[l], b_gates[l],
                        ssm_lambda_re[l], ssm_lambda_im[l], ssm_b_re[l], ssm_b_im[l],
                        ssm_c_re[l], ssm_c_im[l], ssm_d[l], ssm_log_dt[l], w_ssm_glu[l],
                        w_qk_conv[l], b_qk_conv[l], g_head_norm[l],
                        w_branch_ssm[l], w_branch_mlstm[l], w_out[l])
        h = channel_mixer(h, g_ffn_pre[l], g_ffn_post[l], w_ffn_gate[l], w_ffn_up[l],
                          w_ffn_conv[l], b_ffn_conv[l], w_ffn_down[l])
    return h[:, N_META:]


HEAD_DIM = 64
N_HEADS = D_MODEL // HEAD_DIM
N_MOBA = N_HEADS // 4
N_FOX = (N_HEADS - N_MOBA) // 2
N_DIL = N_HEADS - N_MOBA - N_FOX
N_ALIBI = N_MOBA + N_DIL
MOBA_BLOCK = 256
MOBA_TOPK = 3
MOBA_QCHUNK = 32
FOX_QBLOCK = 128
DIL_PAIRS = ((128, 1), (512, 4), (2048, 16))
DIL_BLOCK = 128
D_FF = 4 * D_MODEL
QKV_COLS = 3 * D_MODEL
FOX_GATE_COLS = N_FOX * HEAD_DIM
N_IN_COLS = QKV_COLS + N_FOX + FOX_GATE_COLS
W_MOBA = N_MOBA * HEAD_DIM
W_FOX = N_FOX * HEAD_DIM
ATTN_SCALE = HEAD_DIM ** -0.5
EPS = 1e-6
NEG_INF = -1e30


def rms_norm(x, gain):
    xf = x.astype(jnp.float32)
    y = xf * lax.rsqrt(jnp.mean(xf * xf, axis=-1, keepdims=True) + EPS)
    return (y * gain.astype(jnp.float32)).astype(x.dtype)

def alibi_slopes():
    return jnp.exp2(-8.0 * jnp.arange(1, N_ALIBI + 1, dtype=jnp.float32) / N_ALIBI)

def moba_attention(q, k, v, slopes):
    b, h, s, dh = q.shape
    n_blk = -(-s // MOBA_BLOCK)
    s_pad = n_blk * MOBA_BLOCK
    pad = ((0, 0), (0, 0), (0, s_pad - s), (0, 0))
    q, k, v = jnp.pad(q, pad), jnp.pad(k, pad), jnp.pad(v, pad)
    k_blocks = k.reshape(b, h, n_blk, MOBA_BLOCK, dh)
    v_blocks = v.reshape(b, h, n_blk, MOBA_BLOCK, dh)
    k_mean = jnp.mean(k_blocks.astype(jnp.float32), axis=3)
    gate = jnp.einsum('bhsd,bhnd->bhsn', q.astype(jnp.float32), k_mean)
    q_blk = jnp.arange(s_pad) // MOBA_BLOCK
    past = jnp.arange(n_blk)[None, :] < q_blk[:, None]
    gate = jnp.where(past, gate, NEG_INF)
    top_k = min(MOBA_TOPK, n_blk)
    _, sel_idx = lax.top_k(gate, top_k)
    sel_ok = sel_idx < q_blk[:, None]
    gather = jax.vmap(jax.vmap(lambda blocks, idx: blocks[idx]))
    offs = jnp.arange(MOBA_BLOCK)

    def chunk(c):
        start = c * MOBA_QCHUNK
        qc = lax.dynamic_slice_in_dim(q, start, MOBA_QCHUNK, axis=2)
        idx = lax.dynamic_slice_in_dim(sel_idx, start, MOBA_QCHUNK, axis=2)
        ok = lax.dynamic_slice_in_dim(sel_ok, start, MOBA_QCHUNK, axis=2)
        q_pos = start + jnp.arange(MOBA_QCHUNK)
        k_sel = gather(k_blocks, idx)
        v_sel = gather(v_blocks, idx)
        d_sel = (q_pos[:, None, None] - (idx[..., None] * MOBA_BLOCK + offs)).astype(jnp.float32)
        l_sel = (jnp.einsum('bhqd,bhqnkd->bhqnk', qc, k_sel).astype(jnp.float32) * ATTN_SCALE
                 - slopes[:, None, None, None] * d_sel)
        l_sel = jnp.where(ok[..., None], l_sel, NEG_INF).reshape(b, h, MOBA_QCHUNK, top_k * MOBA_BLOCK)
        own_start = (start // MOBA_BLOCK) * MOBA_BLOCK
        k_own = lax.dynamic_slice_in_dim(k, own_start, MOBA_BLOCK, axis=2)
        v_own = lax.dynamic_slice_in_dim(v, own_start, MOBA_BLOCK, axis=2)
        d_own = q_pos[:, None] - (own_start + offs)[None, :]
        l_own = (jnp.einsum('bhqd,bhkd->bhqk', qc, k_own).astype(jnp.float32) * ATTN_SCALE
                 - slopes[:, None, None] * d_own.astype(jnp.float32))
        l_own = jnp.where(d_own >= 0, l_own, NEG_INF)
        p = jax.nn.softmax(jnp.concatenate([l_sel, l_own], axis=-1), axis=-1).astype(v.dtype)
        p_sel = p[..., :top_k * MOBA_BLOCK].reshape(b, h, MOBA_QCHUNK, top_k, MOBA_BLOCK)
        return (jnp.einsum('bhqnk,bhqnkd->bhqd', p_sel, v_sel)
                + jnp.einsum('bhqk,bhkd->bhqd', p[..., top_k * MOBA_BLOCK:], v_own))

    out = lax.map(chunk, jnp.arange(s_pad // MOBA_QCHUNK))
    return out.transpose(1, 2, 0, 3, 4).reshape(b, h, s_pad, dh)[:, :, :s]

def forgetting_attention(q, k, v, f_logit):
    b, h, s, dh = q.shape
    cum = jnp.cumsum(jax.nn.log_sigmoid(f_logit.astype(jnp.float32)), axis=1).transpose(0, 2, 1)
    k_pos = jnp.arange(s)

    def block(i):
        start = i * FOX_QBLOCK
        qb = lax.dynamic_slice_in_dim(q, start, FOX_QBLOCK, axis=2)
        cb = lax.dynamic_slice_in_dim(cum, start, FOX_QBLOCK, axis=2)
        q_pos = start + jnp.arange(FOX_QBLOCK)
        logits = (jnp.einsum('bhqd,bhkd->bhqk', qb, k).astype(jnp.float32) * ATTN_SCALE
                  + cb[..., None] - cum[:, :, None, :])
        logits = jnp.where(k_pos[None, :] <= q_pos[:, None], logits, NEG_INF)
        p = jax.nn.softmax(logits, axis=-1).astype(v.dtype)
        return jnp.einsum('bhqk,bhkd->bhqd', p, v)

    out = lax.map(block, jnp.arange(s // FOX_QBLOCK))
    return out.transpose(1, 2, 0, 3, 4).reshape(b, h, s, dh)

def dilated_branch(q, k, v, slopes, window, dilation):
    b, h, s, dh = q.shape
    steps = window // dilation
    sub_len = s // dilation
    n_blk = -(-sub_len // DIL_BLOCK)
    sub_pad = n_blk * DIL_BLOCK

    def to_sub(t):
        t = t.reshape(b, h, sub_len, dilation, dh).transpose(0, 1, 3, 2, 4)
        t = jnp.pad(t, ((0, 0), (0, 0), (0, 0), (0, sub_pad - sub_len), (0, 0)))
        return t.reshape(b, h, dilation, n_blk, DIL_BLOCK, dh)

    def band(t):
        prev = jnp.concatenate([jnp.zeros_like(t[:, :, :, :1]), t[:, :, :, :-1]], axis=3)
        return jnp.concatenate([prev, t], axis=4)

    qs = to_sub(q)
    kb, vb = band(to_sub(k)), band(to_sub(v))
    blk = jnp.arange(n_blk)[:, None]
    i_q = blk * DIL_BLOCK + jnp.arange(DIL_BLOCK)[None, :]
    i_k = (blk - 1) * DIL_BLOCK + jnp.arange(2 * DIL_BLOCK)[None, :]
    off = i_q[:, :, None] - i_k[:, None, :]
    allowed = (off >= 0) & (off <= steps) & (i_k[:, None, :] >= 0) & (i_k[:, None, :] < sub_len)
    dist = (off * dilation).astype(jnp.float32)
    logits = (jnp.einsum('bhrnqd,bhrnkd->bhrnqk', qs, kb).astype(jnp.float32) * ATTN_SCALE
              - slopes[:, None, None, None, None] * dist)
    logits = jnp.where(allowed, logits, NEG_INF)
    lse = jax.nn.logsumexp(logits, axis=-1)
    p = jnp.exp(logits - lse[..., None]).astype(v.dtype)
    o = jnp.einsum('bhrnqk,bhrnkd->bhrnqd', p, vb)
    o = o.reshape(b, h, dilation, sub_pad, dh)[:, :, :, :sub_len].transpose(0, 1, 3, 2, 4).reshape(b, h, s, dh)
    lse = lse.reshape(b, h, dilation, sub_pad)[..., :sub_len].transpose(0, 1, 3, 2).reshape(b, h, s)
    return o, lse

def dilated_attention(q, k, v, slopes):
    outs, lses = [], []
    for window, dilation in DIL_PAIRS:
        o, lse = dilated_branch(q, k, v, slopes, window, dilation)
        outs.append(o)
        lses.append(lse)
    w = jax.nn.softmax(jnp.stack(lses, axis=0), axis=0)
    o = jnp.sum(w[..., None] * jnp.stack(outs, axis=0).astype(jnp.float32), axis=0)
    return o.astype(q.dtype)

def to_bsd(o):
    b, h, s, dh = o.shape
    return o.transpose(0, 2, 1, 3).reshape(b, s, h * dh)

def mixer_sublayer(x, norm_g, w_in, b_f, q_gain, k_gain, out_gain, w_out):
    b, s, _ = x.shape
    hn = rms_norm(x, norm_g)
    proj = hn @ w_in
    q = proj[..., :D_MODEL].reshape(b, s, N_HEADS, HEAD_DIM)
    k = proj[..., D_MODEL:2 * D_MODEL].reshape(b, s, N_HEADS, HEAD_DIM)
    v = proj[..., 2 * D_MODEL:QKV_COLS].reshape(b, s, N_HEADS, HEAD_DIM)
    f_logit = proj[..., QKV_COLS:QKV_COLS + N_FOX] + b_f
    g_fox = proj[..., QKV_COLS + N_FOX:]
    q = rms_norm(q, q_gain).transpose(0, 2, 1, 3)
    k = rms_norm(k, k_gain).transpose(0, 2, 1, 3)
    v = v.transpose(0, 2, 1, 3)
    slopes = alibi_slopes()
    a0, a1 = N_MOBA, N_MOBA + N_FOX
    o_moba = moba_attention(q[:, :a0], k[:, :a0], v[:, :a0], slopes[N_DIL:])
    o_fox = forgetting_attention(q[:, a0:a1], k[:, a0:a1], v[:, a0:a1], f_logit)
    o_dil = dilated_attention(q[:, a1:], k[:, a1:], v[:, a1:], slopes[:N_DIL])
    y_moba = rms_norm(to_bsd(o_moba), out_gain[:W_MOBA])
    y_fox = rms_norm(to_bsd(o_fox), out_gain[W_MOBA:W_MOBA + W_FOX]) * jax.nn.sigmoid(g_fox)
    y_dil = rms_norm(to_bsd(o_dil), out_gain[W_MOBA + W_FOX:])
    y = jnp.concatenate([y_moba, y_fox, y_dil], axis=-1) @ w_out
    return x + y

def mlp_sublayer(x, norm_g, w_up, w_down):
    hn = rms_norm(x, norm_g)
    return x + jnp.square(jax.nn.relu(hn @ w_up)) @ w_down

def second_inputs(seed: int = 0) -> dict:
    key = jax.random.key(seed)
    ks = jax.random.split(key, 11)
    f32 = jnp.float32
    return {
        "x": jax.random.normal(ks[0], (BATCH, SEQ, D_MODEL), f32),
        "attn_norm": 1.0 + 0.02 * jax.random.normal(ks[1], (DEPTH, D_MODEL), f32),
        "w_in": jax.random.normal(ks[2], (DEPTH, D_MODEL, N_IN_COLS), f32) * D_MODEL ** -0.5,
        "b_forget": 2.0 + 0.5 * jax.random.normal(ks[3], (DEPTH, N_FOX), f32),
        "q_gain": 1.0 + 0.02 * jax.random.normal(ks[4], (DEPTH, N_HEADS, HEAD_DIM), f32),
        "k_gain": 1.0 + 0.02 * jax.random.normal(ks[5], (DEPTH, N_HEADS, HEAD_DIM), f32),
        "out_gain": 1.0 + 0.02 * jax.random.normal(ks[6], (DEPTH, D_MODEL), f32),
        "w_out": jax.random.normal(ks[7], (DEPTH, D_MODEL, D_MODEL), f32) * D_MODEL ** -0.5,
        "mlp_norm": 1.0 + 0.02 * jax.random.normal(ks[8], (DEPTH, D_MODEL), f32),
        "w_up": jax.random.normal(ks[9], (DEPTH, D_MODEL, D_FF), f32) * D_MODEL ** -0.5,
        "w_down": jax.random.normal(ks[10], (DEPTH, D_FF, D_MODEL), f32) * D_FF ** -0.5,
    }

def second_block(x, attn_norm, w_in, b_forget, q_gain, k_gain, out_gain, w_out, mlp_norm, w_up, w_down):
    for l in range(DEPTH):
        x = mixer_sublayer(x, attn_norm[l], w_in[l], b_forget[l], q_gain[l], k_gain[l],
                           out_gain[l], w_out[l])
        x = mlp_sublayer(x, mlp_norm[l], w_up[l], w_down[l])
    return x


def setup_inputs(seed=0):
    out = dict(first_inputs(seed))
    for name, value in second_inputs(seed + 1).items():
        if name != "x":
            out[name + "_2"] = value
    return out


def reference(
    x, meta_tokens, g_mix_pre, g_mix_post, w_in, b_gates, ssm_lambda_re, ssm_lambda_im,
    ssm_b_re, ssm_b_im, ssm_c_re, ssm_c_im, ssm_d, ssm_log_dt, w_ssm_glu, w_qk_conv, b_qk_conv,
    g_head_norm, w_branch_ssm, w_branch_mlstm, w_out, g_ffn_pre, g_ffn_post, w_ffn_gate,
    w_ffn_up, w_ffn_conv, b_ffn_conv, w_ffn_down, attn_norm_2, w_in_2, b_forget_2, q_gain_2,
    k_gain_2, out_gain_2, w_out_2, mlp_norm_2, w_up_2, w_down_2,
):
    x = first_block(
        x, meta_tokens, g_mix_pre, g_mix_post, w_in, b_gates, ssm_lambda_re, ssm_lambda_im,
        ssm_b_re, ssm_b_im, ssm_c_re, ssm_c_im, ssm_d, ssm_log_dt, w_ssm_glu, w_qk_conv,
        b_qk_conv, g_head_norm, w_branch_ssm, w_branch_mlstm, w_out, g_ffn_pre, g_ffn_post,
        w_ffn_gate, w_ffn_up, w_ffn_conv, b_ffn_conv, w_ffn_down,
    )
    return second_block(
        x, attn_norm_2, w_in_2, b_forget_2, q_gain_2, k_gain_2, out_gain_2, w_out_2, mlp_norm_2,
        w_up_2, w_down_2,
    )


_drawn_inputs = setup_inputs


def setup_inputs(seed=0):
    import zlib

    import numpy as np

    out = dict(_drawn_inputs(seed))
    spreads = {}
    factors = {'g_mix_post': 3.292,
     'ssm_lambda_re': 8.0,
     'b_qk_conv': 4.444,
     'g_head_norm': 3.896,
     'g_ffn_pre': 3.214,
     'g_ffn_post': 4.757,
     'b_ffn_conv': 4.746,
     'attn_norm_2': 5.109,
     'b_forget_2': 3.489,
     'q_gain_2': 8.0,
     'k_gain_2': 8.0,
     'out_gain_2': 6.346,
     'mlp_norm_2': 4.356}
    for name, (base, spread) in spreads.items():
        noise = np.random.default_rng([zlib.crc32(name.encode()), seed]).standard_normal(out[name].shape)
        drawn = base * np.exp(spread * noise) if base else spread * noise
        out[name] = __import__('jax').numpy.asarray(drawn.astype(out[name].dtype))
    for name, factor in factors.items():
        out[name] = (out[name] * factor).astype(out[name].dtype)
    return out
```

```python
import math
from contextlib import contextmanager

import concourse.bass as bass
import numpy as np
from concourse import mybir

P = 128
D_MODEL = 1024
KT = D_MODEL // P
SEQ, META = 512, 16
T1 = SEQ + META
HALF = T1 // 2
SSM_W, SSM_GROUP, SSM_STATE = 512, 16, 64
PAIRS = SSM_W // SSM_GROUP // 2
CT = SSM_W // P
STEP = 4
CHUNKS = T1 // STEP
SEG = CHUNKS // 2
HEADS1 = 4
FFN_TILES = 2816 // P
HEADS2, HD = 16, 64
N_MOBA, N_FOX = 4, 6
EPS = 1e-6
NEG = -1e30
LOOK = 2
RING = 4
GROUPS = ((0, 256), (256, 640), (640, 1024))
FOX_TILES = (2, 3, 4)
E_AFTER, Y_AFTER = (7, 9, 11, 13), (10, 12, 14, 15)
BANK_DONE = (3, 2, 3, 4)
VT_BANK = (6, 6, 4, 6)

U_U, U_GATES, U_Q, U_K, U_V, U_O, U_GA = 0, 4, 5, 9, 13, 17, 21
U_GLU = U_GA + 16
U_MERGE = U_GLU + 2
U_OUT = U_MERGE + KT
U_FFN = U_OUT + KT
FFN_CHUNKS = (8, 8, 6)
U_V2 = U_FFN + 2 * FFN_TILES + 3 * KT
U_F2 = U_V2 + KT
U_GFOX = U_F2 + 1
U_QK2 = U_GFOX + 3
U_OUT2 = U_QK2 + 2 * KT
U_MLP = U_OUT2 + KT
MLP_CHUNKS = 4
UNITS = U_MLP + MLP_CHUNKS * 2 * KT

_COLS = [("g_mix_pre", 8), ("g_mix_post", 8), ("g_ffn_pre", 8), ("g_ffn_post", 8), ("b_qk", 8), ("w_qk", 32),
         ("g_head", 4), ("ssm_d", 4), ("attn_norm", 8), ("mlp_norm", 8), ("out_gain", 8), ("q_gain", 8),
         ("k_gain", 8), ("ffn_conv", 4 * FFN_TILES), ("lam_re", PAIRS), ("lam_im", PAIRS), ("log_dt", PAIRS),
         ("b_i", 1), ("b_f", 1), ("b_forget", 1)]
COL, _at = {}, 0
for _name, _n in _COLS:
    COL[_name] = _at
    _at += _n
N_COLS = _at


class Order:

    def __init__(self, eng, steps):
        self.eng, self.steps, self.n, self.shift, self.last = eng, steps, {}, {}, None

    def value(self, sem):
        v = self.n.get(sem.name, 0)
        for x in self.shift.get(sem.name, []):
            v = x + v
        return v

    def do(self, ins, sem=None):
        sem = sem or self.steps
        ins.then_inc(sem, 1)
        self.n[sem.name] = self.n.get(sem.name, 0) + 1
        self.last = (sem, self.value(sem))

    def fence(self):
        if self.last is not None:
            self.eng.wait_ge(*self.last)

    @contextmanager
    def loop(self, trips, per_trip):
        before = dict(self.n)
        with self.eng.Fori(0, trips) as i:
            for sem, k in per_trip.items():
                self.shift.setdefault(sem.name, []).append(i * k)
            self.last = None
            yield i
        for sem, k in per_trip.items():
            got = self.n.get(sem.name, 0) - before.get(sem.name, 0)
            assert got == k, (sem.name, got, k)
            self.n[sem.name] = before.get(sem.name, 0) + trips * k
            self.shift[sem.name].pop()
        for name in self.n:
            assert name in {s.name for s in per_trip} or self.n[name] == before.get(name, 0), name
        if self.last is not None:
            self.last = (self.last[0], self.value(self.last[0]))


def build(nc, w_units, x_t, cols_in, consts_in, sel_in, ssm_b_in, ssm_c_in, alibi_in, dil_in, out, upto=99):
    fp32, f32r = mybir.dt.float32, mybir.dt.float32r
    ALU, ACT, AX = mybir.AluOpType, mybir.ActivationFunctionType, mybir.AxisListType

    place = [(nc.sbuf_base + 31) // 32 * 32]

    def fixed(name, shape, dt=fp32):
        t = nc.alloc_sbuf_tensor_at(name, [P] + shape, dt, offset=place[0])
        place[0] += (4 * math.prod(shape) + 31) // 32 * 32
        return t

    def region(size):
        at = place[0]
        place[0] += size
        return at

    def at(name, shape, where, dt=fp32):
        return nc.alloc_sbuf_tensor_at(name, [P] + shape, dt, offset=where)

    raw = fixed("w_raw", [RING, 1024])
    whi = fixed("w_hi", [RING, 1024], f32r)
    wlo = fixed("w_lo", [RING, 1024], f32r)
    tile528 = KT * T1 * 4
    Zx = region(tile528)
    hhi = fixed("h_hi", [KT, T1], f32r)
    hlo = fixed("h_lo", [KT, T1], f32r)
    Z2 = region(tile528)
    sq = [fixed(f"sq{j}", [T1]) for j in range(2)]
    acc = fixed("acc", [T1])
    rs = fixed("rs", [T1])
    consts = fixed("consts", [5, P])
    ident, ones, blk64, mask_st, mask_qk = (consts[:, j, :] for j in range(5))
    sel = fixed("sel", [4, P])
    cols = fixed("cols", [N_COLS])
    small = fixed("small", [500])
    rows = fixed("rows", [T1])
    Zu = region(4 * T1 * 4)
    Zv = region(5 * 512 * 4)
    R = region(16 * T1 * 4 + 3 * 4 * T1 * 4)
    assert place[0] <= nc.sbuf_usable_end, (place[0], nc.sbuf_usable_end)

    x = at("x", [KT, T1], Zx)
    qk = at("qk", [2 * HEADS1, T1], Zx)
    qp = [at(f"qp{j}", [T1 + 3], Z2 + 2144 * j) for j in range(2)]
    vT = [at(f"vT{j}", [T1], Z2 + 4288 + 2112 * j) for j in range(2)]
    b_t = [at(f"b_tmp{j}", [PAIRS * 32], Z2 + 2048 * j) for j in range(4)]
    b_raw = at("b_raw", [2, PAIRS * 32], Z2 + 8512)
    kblk = at("k_blk", [CT, STEP, P], Z2 + 8512)
    ybhi = at("yb_hi", [HEADS1, T1], Z2, f32r)
    yblo = at("yb_lo", [HEADS1, T1], Z2 + 4 * T1 * 4, f32r)
    ysum = at("y_sum", [KT, T1], Z2)
    u = at("u", [CT, T1], Zu)
    Wm = at("w_mlstm", [1360], Zu)
    num = at("num", [T1], Zu + 5440)
    b_pow = [at("b_pow0", [2, PAIRS * 32], Zv), at("b_pow1", [2, PAIRS * 32], Zv + 4096),
             at("b_pow2", [2, PAIRS * 32], Z2 + 12608), at("b_pow3", [2, PAIRS * 32], Z2 + 8512)]
    vs = at("v_tok", [5, 512], Zv)
    c_pow = at("c_pow", [STEP + 1, 2, PAIRS * 32], R)
    bT = at("b_T", [2, STEP, CT, P], R + 20480)
    ph = at("phase", [2, PAIRS, SEG], R + 36864)
    rot = [at(f"rot{j}", [4, SEG], R + 45312 + 1056 * j) for j in range(4)]
    xst = [at(f"x_state{j}", [2, 4, CHUNKS + 1], R + 49536 + 4256 * j) for j in range(2)]
    c_t = [at(f"c_tmp{j}", [PAIRS * 32], R + 49536 + 2048 * j) for j in range(4)]
    G = at("gates", [2 * KT, T1], R)
    og = at("o_gate", [HEADS1, T1], R + 16 * T1 * 4)
    yahi = at("ya_hi", [CT, T1], R + 20 * T1 * 4, f32r)
    yalo = at("ya_lo", [CT, T1], R + 24 * T1 * 4, f32r)
    fahi = at("ffn_hi", [KT, SEQ], R, f32r)
    falo = at("ffn_lo", [KT, SEQ], R + 16384, f32r)
    gp = [at(f"gate_pad{j}", [T1 + 2], R + 32768 + 2144 * j) for j in range(2)]
    cg = [at(f"gate_conv{j}", [SEQ], R + 37056 + 2048 * j) for j in range(2)]
    tup = [at(f"up{j}", [SEQ], R + 41152 + 2048 * j) for j in range(2)]
    ctmp = at("conv_tmp", [SEQ], R + 45312)
    V = at("v2_tok", [4, D_MODEL], R)
    sgf = at("fox_gate", [3, SEQ], R + 16384)
    qa = [at(f"q_aug{j}", [2, SEQ], R + 22528 + 8192 * j) for j in range(2)]
    ka = [at(f"k_aug{j}", [2, SEQ], R + 22528 + 4096 + 8192 * j) for j in range(2)]
    qr = [at(f"qk_raw{j}", [SEQ], R + 38912 + 2048 * j) for j in range(2)]
    Pb = [at(f"probs{j}", [3, SEQ], R + 43008 + 6144 * j) for j in range(2)]
    vT2 = [at(f"v2T{j}", [SEQ], R + 43008 + 2048 * j) for j in range(2)]
    yq = at("attn_out", [4, D_MODEL], Z2)
    dil = at("dil", [2, SEQ], Zu)
    fox = [at(f"fox{j}", [SEQ], Zu + 4096 + 2048 * j) for j in range(2)]
    mahi = at("mlp_hi", [KT, SEQ], R, f32r)
    malo = at("mlp_lo", [KT, SEQ], R + 16384, f32r)
    rl = [at(f"relu{j}", [SEQ], R + 32768 + 2048 * j) for j in range(2)]
    r2 = [at(f"relu_sq{j}", [SEQ], R + 36864 + 2048 * j) for j in range(2)]
    ot = [at(f"out_tile{j}", [SEQ], R + 40960 + 2048 * j) for j in range(2)]

    PS = nc.alloc_psum_tensor("ps", [P, 8, 512], fp32)

    sems = {}

    def sem(name):
        if name not in sems:
            sems[name] = nc.alloc_semaphore(name)
        return sems[name]

    raw_in = [sem(f"raw_in{j}") for j in range(RING)]
    hi_ready, lo_ready = sem("hi_ready"), sem("lo_ready")
    unit_done, evacuated = sem("unit_done"), sem("evacuated")
    act_steps, dve_steps, pool_steps = sem("act_steps"), sem("dve_steps"), sem("pool_steps")

    SLOTS = ("t", "f", "s", "c", "e1", "e2", "th", "k", "ca", "rho", "dt", "phi", "cm1", "sphi", "den", "em1", "cphi",
             "r", "nr", "ni", "r2", "p2r", "p2i", "ar", "r4", "zr", "zi", "p4r", "p4i")

    def sm(name):
        j = PAIRS * SLOTS.index("ni" if name == "ai" else name)
        return small[:, j:j + PAIRS]

    r2c = small[:, 0:20]
    nm, rsum, rinv = (small[:, 32 + 8 * j:40 + 8 * j] for j in range(3))
    gss = small[:, 64:76]

    def u_a(m):
        return u[:, m, :]

    def col(name, j=0, n=1, p0=0, p1=P):
        return cols[p0:p1, COL[name] + j:COL[name] + j + n]

    def pair(slot):
        return PS[:, 2 * slot:2 * slot + 2, 0:HALF]

    def two(t):
        return t.rearrange("p (a b) -> p a b", a=2)

    def f32(t):
        return t.bitcast(fp32)

    S_OFF = [0, 528, 928, 1200, 1344]
    S_LEN = [T1 - P * j for j in range(5)]
    QB = [(0, 0), (2, 0), (0, 128), (1, 0)]

    block = nc.Block()
    with block as block:

        @block.sync
        def _(sp):
            sp.dma_start(cols[:, :], cols_in).then_inc(sem("cols_in"), 16)
            sp.dma_start(consts[:, :, :], consts_in.rearrange("p (a b) -> p a b", a=5)).then_inc(sem("consts_in"), 16)
            for n in range(RING):
                sp.dma_start(raw[:, n, :], w_units[n]).then_inc(raw_in[n], 16)
            total = {1: U_GLU, 2: U_FFN, 3: U_V2}[upto] if upto < 9 else UNITS
            total = min(UNITS, total + LOOK)

            def load(s, r, j):
                sp.wait_ge(lo_ready, r + (s - RING + 1))
                sp.dma_start(raw[:, j, :], w_units[bass.ds(r + s, 1), :, :].rearrange("a p c -> p (a c)")
                             if not isinstance(r, int) else w_units[r + s]).then_inc(raw_in[j], 16)

            trips = (total - RING) // RING
            with sp.Fori(0, trips) as i:
                for j in range(RING):
                    load(RING + j, i * RING, j)
            for n in range(RING + trips * RING, total):
                load(n, 0, n % RING)
            if upto > 9:
                for m in range(KT):
                    sp.wait_ge(sem("out_ready"), m + 1)
                    sp.dma_start(out[:, m * SEQ:(m + 1) * SEQ], ot[m % 2][:, :]).then_inc(sem(f"out_done{m % 2}"), 16)
                for j in range(2):
                    sp.wait_ge(sem(f"out_done{j}"), 16 * KT // 2)

        @block.scalar
        def _(act):
            A = Order(act, act_steps)
            dn = nc.scalar

            def split_hi(s, r=0):
                if isinstance(r, int) and s + r >= UNITS:
                    return
                act.wait_ge(raw_in[s % RING], r * 4 + 16 * (s // RING + 1))
                if s >= RING:
                    act.wait_ge(unit_done, r + (s - RING + 1))
                A.do(dn.activation(whi[:, s % RING, :], raw[:, s % RING, :], ACT.Copy), hi_ready)

            def squares(norm, src, first_wait):
                for m in range(KT):
                    first_wait(m)
                    if m == 0:
                        if norm:
                            act.wait_ge(sem("rs_ready"), norm)
                        A.do(dn.activation(acc[:, 0:src(0).shape[-1]], src(0), ACT.Square), sem("sq_ready"))
                    else:
                        if m >= 3 or norm:
                            act.wait_ge(sem("sq_added"), 7 * norm + max(m - 2, 0))
                        A.do(dn.activation(sq[m % 2][:, 0:src(m).shape[-1]], src(m), ACT.Square), sem("sq_ready"))

            def std(norm, view, dst):
                act.wait_ge(sem("stat_mm"), norm + 1)
                A.do(dn.activation(dst, view, ACT.Sqrt, bias=eps_col, scale=1.0 / D_MODEL), sem("std_ready"))

            eps_col = small[:, 490:491]
            tiny_col = small[:, 491:492]

            for j in range(4):
                act.dma_start(x[:, 2 * j:2 * j + 2, :],
                              x_t[:, 2 * j * T1:(2 * j + 2) * T1].rearrange("p (a b) -> p a b", a=2)
                              ).then_inc(sem(f"x_in{j}"), 16)
            act.dma_start(b_raw[:, :, :], ssm_b_in.rearrange("p (a b) -> p a b", a=2)).then_inc(sem("ssm_b_in"), 16)
            act.dma_start(c_pow[:, 0, :, :], ssm_c_in.rearrange("p (a b) -> p a b", a=2)).then_inc(sem("ssm_c_in"), 16)
            act.dma_start(sel[0:36, :, :], sel_in.rearrange("p (a b) -> p a b", a=4)).then_inc(sem("sel_in"), 16)

            act.wait_ge(sem("cols_in"), 16)
            A.do(dn.activation(sm("t"), col("log_dt", 0, PAIRS), ACT.Tanh, scale=1.0 / 16), sem("lam_act"))
            act.wait_ge(sem("lam_dve"), 1)
            A.do(dn.activation(sm("s"), sm("f"), ACT.Sin, scale=0.5))
            A.do(dn.activation(sm("c"), sm("ca"), ACT.Sin))
            A.do(dn.activation(sm("th"), sm("rho"), ACT.Tanh, scale=0.5), sem("lam_act"))

            act.wait_ge(sem("eps_set"), 1)
            for m in range(KT):
                act.wait_ge(sem(f"x_in{m // 2}"), 16)
                A.do(dn.activation(hhi[:, m, :], x[:, m, :], ACT.Identity, scale=col("g_mix_pre", m)), sem("h1_hi"))
                if m == 1:
                    split_hi(0)
                if m == 3:
                    split_hi(1)
            squares(0, lambda m: x[:, m, :], lambda m: None)

            def gate_rows():
                act.wait_ge(evacuated, U_GATES + 1)
                A.do(dn.activation(acc[0:4, :], acc[0:4, :], ACT.Identity, bias=col("b_f", 0, 1, 0, 4)), sem("gate_z"))
                act.wait_ge(sem("gate_abs"), 1)
                A.do(dn.activation(sq[1][0:4, :], sq[1][0:4, :], ACT.Exp))
                A.fence()
                A.do(dn.activation(sq[1][0:4, :], sq[1][0:4, :], ACT.Ln, bias=1.0), sem("gate_ln"))

            def conv_taps(m):
                act.wait_ge(evacuated, U_Q + m + 1)
                if m == 0:
                    act.wait_ge(sem("h1_lo"), KT)
                else:
                    act.wait_ge(sem("tap_added"), 3 * m)
                for k in range(4):
                    src = qp[m % 2][:, k:k + T1]
                    if k == 0:
                        A.do(dn.activation(qk[:, m, :], src, ACT.Identity, bias=col("b_qk", m), scale=col("w_qk", m)))
                    else:
                        if k == 3:
                            act.wait_ge(sem("tap_added"), 3 * m + 1)
                        A.do(dn.activation(vT[k % 2][:, :], src, ACT.Identity, scale=col("w_qk", 8 * k + m)), sem("tap_ready"))

            def mlstm_weights(h):
                act.wait_ge(sem("bc_mm"), h + 1)
                if h:
                    act.wait_ge(sem("ss_mm"), h)
                    act.wait_ge(sem("den_used"), h)
                A.do(dn.activation(two(sq[0][:, :]), PS[:, 4:6, 0:HALF], ACT.Copy))
                A.do(dn.activation(two(sq[1][:, :]), PS[:, 6:8, 0:HALF], ACT.Exp, scale=-2.0), sem("bc_done"))
                act.wait_ge(sem("r2c_ready"), 1)
                if h == 0:
                    act.wait_ge(sem("ya_lo"), CT)
                if h:
                    act.wait_ge(sem("nd_mm"), h)
                A.fence()
                for j in range(4):
                    A.do(dn.activation(Wm[:, S_OFF[j] + P:S_OFF[j] + S_LEN[j]], sq[0][:, P * (j + 1):T1], ACT.Exp,
                                       bias=r2c[:, 4 * j + h:4 * j + h + 1]))
                act.wait_ge(sem("diag_done"), 5 * (h + 1))
                for j in range(5):
                    k = min(P, S_LEN[j])
                    d = Wm[0:k, S_OFF[j]:S_OFF[j] + k]
                    A.do(dn.activation(d, d, ACT.Exp, bias=r2c[0:k, 4 * j + h:4 * j + h + 1]),
                         sem("w_ready") if j == 4 else None)

            def mlstm_num(h):
                act.wait_ge(sem("nd_mm"), h + 1)
                if h:
                    act.wait_ge(sem("yb_lo"), h)
                A.do(dn.activation(two(acc[:, :]), PS[:, 6:8, 0:HALF], ACT.Square), sem("densq_ready"))
                A.do(dn.activation(two(num[:, :]), PS[:, 4:6, 0:HALF], ACT.Copy))
                A.do(dn.activation(two(sq[0][:, :]), PS[:, 4:6, 0:HALF], ACT.Square), sem("numsq_ready"))

            def mlstm_out(h):
                act.wait_ge(sem("z_ready"), h + 1)
                A.do(dn.activation(acc[:, :], acc[:, :], ACT.Sqrt, bias=tiny_col, scale=1.0 / P), sem("sd_ready"))
                act.wait_ge(sem("yb_pre"), h + 1)
                A.do(dn.activation(ybhi[:, h, :], num[:, :], ACT.Copy), sem("yb_hi"))

            for n in range(U_GLU):
                split_hi(n + LOOK)
                if n == 0:
                    std(0, PS[:, 4:6, 0:HALF], two(acc[:, :]))
                if n == U_GATES:
                    gate_rows()
                if n in (4, 5):
                    for s in range(STEP):
                        act.wait_ge(sem("bt_mm"), (n - 4) * STEP + s + 1)
                        if n == 4 and s == 0:
                            act.wait_ge(sem("lam_dve"), 2)
                        A.do(dn.activation(bT[:, n - 4, s, :, :], PS[:, 4 + s, :].rearrange("p (a b) -> p a b", a=CT),
                                           ACT.Copy), sem("bt_copied"))
                if U_Q <= n < U_V:
                    conv_taps(n - U_Q)
                if U_Q < n <= U_V:
                    m = n - 1 - U_Q
                    act.wait_ge(sem("tap_added"), 3 * (m + 1))
                    A.do(dn.activation(qk[:, m, :], qk[:, m, :], ACT.Silu), sem("qk_ready"))
                if n == 6:
                    act.wait_ge(sem("r2_mm"), 1)
                    A.do(dn.activation(r2c[:, 0:16], PS[:, 4, 0:16], ACT.Copy))
                    A.do(dn.activation(r2c[0:16, 16:20], PS[0:16, 4, 16:20], ACT.Copy), sem("r2c_ready"))
                if n == 8:
                    act.wait_ge(sem("kz"), 1)
                    act.wait_ge(sem("k_mm"), 1)
                    for g in range(4):
                        A.do(dn.activation(kblk[32 * g:32 * g + 32, :, :, 32 * g:32 * g + 32],
                                           PS[32 * g:32 * g + 32, 4, :].rearrange("p (a b c) -> p a b c", a=CT, b=STEP),
                                           ACT.Copy), sem("k_ready"))
                if n in Y_AFTER:
                    t = Y_AFTER.index(n)
                    act.wait_ge(sem("y_used"), t + 1)
                    A.do(dn.activation(u[:, t, :], u[:, t, :], ACT.Gelu_apprx_tanh), sem("ya_ready"))
                if U_V + 1 <= n < U_V + 5:
                    j = n - U_V - 1
                    b = VT_BANK[j]
                    act.wait_ge(sem("vt_mm"), j + 1)
                    act.wait_ge(sem("vz"), 1)
                    A.do(dn.activation(vs[:, 0:4, P * j:P * j + P], PS[:, b, :].rearrange("p (a b) -> p a b", a=4), ACT.Copy))
                    A.do(dn.activation(vs[0:16, 4, P * j:P * j + P], PS[0:16, b + 1, 0:P], ACT.Copy), sem("vs_ready"))
                if U_O <= n < U_GA:
                    j = n - U_O
                    act.wait_ge(evacuated, n + 1)
                    A.do(dn.activation(og[:, j, :], og[:, j, :], ACT.Sigmoid), sem("og_ready"))
                    act.wait_ge(sem("ya_ready"), 4)
                    act.wait_ge(sem("y_mm"), 4)
                    A.do(dn.activation(yahi[:, j, :], u[:, j, :], ACT.Copy), sem("ya_hi"))
                if n >= U_GA - 1:
                    h, k = divmod(n - (U_GA - 1), 4)
                    if n >= U_GA:
                        act.wait_ge(evacuated, n + 1)
                        A.do(dn.activation(G[:, n - U_GA, :], G[:, n - U_GA, :], ACT.Sigmoid), sem("g_ready"))
                    if h < HEADS1:
                        (mlstm_weights, lambda h: None, mlstm_num, mlstm_out)[k](h)

            if upto <= 1:
                return
            for n in range(U_GLU, U_MERGE):
                split_hi(n + LOOK)
            act.wait_ge(unit_done, U_MERGE)
            for m in range(CT):
                s = (U_GLU + m // 2) % 2
                view = pair(s) if m % 2 == 0 else PS[:, 4 + 2 * s:6 + 2 * s, 0:HALF]
                if m >= 2:
                    act.wait_ge(sem("ya2_pre"), m - 1)
                A.do(dn.activation(two(sq[m % 2][:, :]), view, ACT.Sigmoid), sem("glu_sg"))
            for m in range(CT):
                act.wait_ge(sem("ya2_pre"), m + 1)
                A.do(dn.activation(yahi[:, m, :], u_a(m), ACT.Copy), sem("ya2_hi"))

            act.wait_ge(sem("s_mm"), HEADS1)
            act.dma_start(x[:, :, :], x_t.rearrange("p (a b) -> p a b", a=KT)).then_inc(sem("x_again"), 16)
            with A.loop(2, {hi_ready: 4, sem("mg_hi"): 4}) as i:
                for j in range(4):
                    split_hi(U_MERGE + j + LOOK, i * 4)
                    act.wait_ge(sem("mg_pre"), i * 4 + (j + 1))
                    A.do(dn.activation(hhi[:, bass.ds(i * 4 + j, 1), :].rearrange("p a b -> p (a b)"),
                                       sq[j % 2][:, :], ACT.Copy), sem("mg_hi"))
            with A.loop(2, {hi_ready: 4}) as i:
                for j in range(4):
                    split_hi(U_OUT + j + LOOK, i * 4)
            squares(1, lambda m: ysum[:, m, :], lambda m: act.wait_ge(evacuated, U_OUT + m + 1))
            std(1, PS[:, 4:6, 0:HALF], two(acc[:, :]))
            for m in range(KT):
                act.wait_ge(sem("x1_ready"), m + 1)
                A.do(dn.activation(hhi[:, m, :], x[:, m, :], ACT.Identity, scale=col("g_ffn_pre", m)), sem("h2_hi"))
            squares(2, lambda m: x[:, m, :], lambda m: None)
            if upto <= 2:
                return

            def ffn_pair(s, r, f, rf, fl, rfl, first):
                p = f % 2
                split_hi(s + LOOK, r)
                if first:
                    std(2, PS[:, 4:6, 0:HALF], two(acc[:, :]))
                act.wait_ge(sem("conv2_ready"), rf + (f + 1))
                A.do(dn.activation(cg[p][:, :], cg[p][:, :], ACT.Gelu_apprx_tanh), sem("gl_ready"))
                split_hi(s + 1 + LOOK, r)
                act.wait_ge(sem("fa_pre"), rf + (f + 1))
                A.do(dn.activation(fahi[:, bass.ds(rfl + fl, 1), :].rearrange("p a b -> p (a b)")
                                   if not isinstance(rfl, int) else fahi[:, fl, :], tup[p][:, :], ACT.Copy), sem("fa_hi"))

            s0 = U_FFN
            f0 = 0
            for c, tiles in enumerate(FFN_CHUNKS):
                first = 0
                if c == 0:
                    ffn_pair(s0, 0, 0, 0, 0, 0, True)
                    ffn_pair(s0 + 2, 0, 1, 0, 1, 0, False)
                    first = 1
                with A.loop(tiles // 2 - first, {hi_ready: 4, sem("gl_ready"): 2, sem("fa_hi"): 2}) as i:
                    for q in range(2):
                        ffn_pair(s0 + 4 * first + 2 * q, i * 4, f0 + 2 * first + q, i * 2, 2 * first + q, i * 2, False)
                s0 += 2 * tiles
                f0 += tiles
                with A.loop(2, {hi_ready: 4}) as i:
                    for j in range(4):
                        split_hi(s0 + j + LOOK, i * 4)
                s0 += KT
            assert s0 == U_V2
            squares(3, lambda m: ysum[:, m, 0:SEQ], lambda m: act.wait_ge(evacuated, U_V2 - KT + m + 1))
            std(3, PS[:, 4, :], acc[:, 0:SEQ])
            for m in range(KT):
                act.wait_ge(sem("x2_ready"), m + 1)
                A.do(dn.activation(hhi[:, m, 0:SEQ], x[:, m, META:T1], ACT.Identity, scale=col("attn_norm", m)), sem("h3_hi"))
            squares(4, lambda m: x[:, m, META:T1], lambda m: None)
            if upto <= 3:
                return

            def v2_copy(j, r):
                act.wait_ge(sem("v2t_mm"), r + (j + 1))
                A.do(dn.activation(V[:, :, bass.ds((r + j) * P, P)],
                                   PS[:, 2 + j % 2, :].rearrange("p (a b) -> p a b", a=4), ACT.Copy), sem("v2_ready"))

            split_hi(U_V2 + LOOK)
            std(4, PS[:, 4, :], acc[:, 0:SEQ])
            for n in range(U_V2 + 1, U_V2 + KT):
                split_hi(n + LOOK)
                v2_copy(n - 1 - U_V2, 0)
            split_hi(U_F2 + LOOK)
            v2_copy(KT - 1, 0)
            act.wait_ge(evacuated, U_F2 + 1)
            A.do(dn.activation(fox[0][0:N_FOX, :], fox[0][0:N_FOX, :], ACT.Identity,
                               bias=col("b_forget", 0, 1, 0, N_FOX)), sem("fox_z"))
            act.wait_ge(sem("fox_abs"), 1)
            A.do(dn.activation(fox[1][0:N_FOX, :], fox[1][0:N_FOX, :], ACT.Exp))
            A.fence()
            A.do(dn.activation(fox[1][0:N_FOX, :], fox[1][0:N_FOX, :], ACT.Ln, bias=1.0), sem("fox_ln"))
            for j in range(3):
                split_hi(U_GFOX + j + LOOK)
                act.wait_ge(evacuated, U_GFOX + j + 1)
                A.do(dn.activation(sgf[:, j, :], sgf[:, j, :], ACT.Sigmoid), sem("sgf_ready"))

            def qk_square(i, w):
                act.wait_ge(evacuated, U_QK2 + 2 * i + w + 1)
                if i:
                    act.wait_ge(sem("aug_ready"), 4 * (i - 1) + 2 * w + 2)
                A.do(dn.activation(sq[w][:, 0:SEQ], qr[w][:, :], ACT.Square), sem("qsq_ready"))

            def qk_std(i, w):
                act.wait_ge(sem("qstat_mm"), 2 * i + w + 1)
                A.do(dn.activation(sq[w][:, 0:SEQ], PS[:, (U_QK2 + w) % 2, :], ACT.Sqrt,
                                   bias=(eps64_col if w == 0 else eps_col), scale=(1.0 if w == 0 else 1.0 / HD)),
                     sem("qstd_ready"))

            eps64_col = small[:, 492:493]

            def exps(i, hh):
                h = 2 * i + hh
                b = 2 + 3 * hh
                if i:
                    act.wait_ge(sem("pv_mm"), h - 1)
                for t in range(4):
                    act.wait_ge(sem("max_ready"), 4 * h + BANK_DONE[t])
                    bank, c = QB[t]
                    w = P * (t + 1)
                    A.do(dn.activation(Pb[hh][:, bank, c:c + w], PS[:, b + bank, c:c + w], ACT.Exp,
                                       bias=nm[:, 4 * hh + t:4 * hh + t + 1],
                                       accum_out=rsum[:, 4 * hh + t:4 * hh + t + 1]), sem("p2_ready"))

            def pt_copy(i, hh):
                h = 2 * i + hh
                b = 2 + 3 * hh
                act.wait_ge(sem("pt_mm"), h + 1)
                A.do(dn.activation(Pb[hh][:, 0:2, :], PS[:, b:b + 2, :], ACT.Copy), sem("pt_act"))

            for i in range(KT + 1):
                if i < KT:
                    split_hi(U_QK2 + 2 * i + LOOK)
                    qk_square(i, 0)
                if i:
                    exps(i - 1, 0)
                if i < KT:
                    split_hi(U_QK2 + 2 * i + 1 + LOOK)
                    qk_std(i, 0)
                    qk_square(i, 1)
                if i:
                    pt_copy(i - 1, 0)
                    exps(i - 1, 1)
                if i < KT:
                    qk_std(i, 1)
                if i:
                    pt_copy(i - 1, 1)

            act.wait_ge(sem("attn_done"), HEADS2)
            for g, (a, b) in enumerate(GROUPS):
                for t in range(4):
                    A.fence()
                    A.do(dn.activation(Pb[0][:, 0, 0:b - a], yq[:, t, a:b], ACT.Square,
                                       accum_out=gss[:, 4 * g + t:4 * g + t + 1]))
            A.fence()
            for g, (a, b) in enumerate(GROUPS):
                A.do(dn.activation(gss[:, 4 * g:4 * g + 4], gss[:, 4 * g:4 * g + 4], ACT.Sqrt, bias=eps_col,
                                   scale=1.0 / (b - a)), sem("gstd_ready"))
            for m in range(KT):
                act.wait_ge(sem("yt_mm"), m + 1)
                if m in FOX_TILES:
                    act.wait_ge(sem("yfox_pre"), m - 1)
                    A.do(dn.activation(hhi[:, m, 0:SEQ], qr[m % 2][:, :], ACT.Copy), sem("y2_hi"))
                else:
                    A.do(dn.activation(hhi[:, m, 0:SEQ], PS[:, 2 + m % 6, :], ACT.Identity, scale=col("out_gain", m)),
                         sem("y2_hi"))
            for m in range(KT):
                split_hi(U_OUT2 + m + LOOK)
            for m in range(KT):
                act.wait_ge(evacuated, U_OUT2 + m + 1)
                if m == 0:
                    act.wait_ge(unit_done, U_MLP)
                A.do(dn.activation(hhi[:, m, 0:SEQ], x[:, m, META:T1], ACT.Identity, scale=col("mlp_norm", m)), sem("h4_hi"))
            squares(5, lambda m: x[:, m, META:T1], lambda m: None)

            def mlp_up(s, r, f, rf, fl, rfl):
                p = f % 2
                split_hi(s + LOOK, r)
                act.wait_ge(unit_done, r + (s + 1))
                act.wait_ge(evacuated, r + (s - 1))
                A.do(dn.activation(rl[p][:, :], PS[:, s % 2, :], ACT.Relu), sem("relu_ready"))
                act.wait_ge(evacuated, r + (s + 1))
                A.do(dn.activation(mahi[:, bass.ds(rfl + fl, 1), :].rearrange("p a b -> p (a b)")
                                   if not isinstance(rfl, int) else mahi[:, fl, :], r2[p][:, :], ACT.Copy), sem("ma_hi"))

            for f in range(4):
                mlp_up(U_MLP + f, 0, f, 0, f, 0)
                if f == 0:
                    std(5, PS[:, 4, :], acc[:, 0:SEQ])
            for f in range(4, 8):
                mlp_up(U_MLP + f, 0, f, 0, f, 0)
            for j in range(KT):
                split_hi(U_MLP + KT + j + LOOK)
            with A.loop(2, {hi_ready: 16, sem("relu_ready"): 8, sem("ma_hi"): 8}) as c:
                for f in range(KT):
                    mlp_up(U_MLP + 2 * KT + f, c * 16, KT + f, c * 8, f, 0)
                for j in range(KT):
                    split_hi(U_MLP + 3 * KT + j + LOOK, c * 16)
            for f in range(KT):
                mlp_up(U_MLP + 6 * KT + f, 0, 3 * KT + f, 0, f, 0)
            for j in range(KT):
                split_hi(U_MLP + 7 * KT + j + LOOK)

        @block.vector
        def _(dve):
            Dv = Order(dve, dve_steps)
            v = nc.vector

            def split_lo(s, r=0):
                if isinstance(r, int) and s + r >= UNITS:
                    return
                dve.wait_ge(hi_ready, r + (s + 1))
                Dv.do(v.tensor_tensor(wlo[:, s % RING, :], raw[:, s % RING, :], f32(whi[:, s % RING, :]), ALU.subtract), lo_ready)

            def tt(o, a, b, op, s=None):
                Dv.do(v.tensor_tensor(o, a, b, op), s)

            def ts(o, a, s1, s2, op0, op1=None, s=None):
                if op1 is None:
                    Dv.do(v.tensor_scalar(o, a, s1, None, op0), s)
                else:
                    Dv.do(v.tensor_scalar(o, a, s1, s2, op0, op1), s)

            def stt(o, a, sc, b, op0, op1, s=None):
                Dv.do(v.scalar_tensor_tensor(out=o, in0=a, scalar=sc, in1=b, op0=op0, op1=op1), s)

            def rstd(norm, n):
                dve.wait_ge(sem("std_ready"), norm + 1)
                Dv.fence()
                Dv.do(v.reciprocal(rs[:, 0:n], acc[:, 0:n]), sem("rs_ready"))
                Dv.fence()

            def seq(*ops):
                for op in ops:
                    Dv.fence()
                    op()

            M, A_, S_ = ALU.mult, ALU.add, ALU.subtract
            Dv.do(v.memset(small[:, 490:491], EPS))
            Dv.do(v.memset(small[:, 491:492], 1e-36))
            Dv.do(v.memset(small[:, 492:493], HD * EPS), sem("eps_set"))

            lr, li = col("lam_re", 0, PAIRS), col("lam_im", 0, PAIRS)
            dve.wait_ge(sem("lam_act"), 1)
            MAGIC, C1 = 1.5 * 2.0 ** 23, 6.28125
            C2 = float(np.float32(np.float64(2 * math.pi) - C1))
            C2 = float(np.frombuffer((np.float32(C2).view(np.uint32) & np.uint32(0xFFFFF000)).tobytes(), np.float32)[0])
            C3 = 2 * math.pi - C1 - C2
            ts(sm("e1"), sm("t"), 1.0, None, A_)
            ts(sm("e2"), sm("t"), -1.0, 1.0, M, A_)
            seq(lambda: Dv.do(v.reciprocal(sm("e2"), sm("e2"))),
                lambda: tt(sm("e1"), sm("e1"), sm("e2"), M),
                lambda: tt(sm("e1"), sm("e1"), sm("e1"), M),
                lambda: tt(sm("e1"), sm("e1"), sm("e1"), M),
                lambda: tt(sm("dt"), sm("e1"), sm("e1"), M),
                lambda: tt(sm("rho"), lr, sm("dt"), M),
                lambda: tt(sm("phi"), li, sm("dt"), M),
                lambda: ts(sm("k"), sm("phi"), 1.0 / (2 * math.pi), None, M),
                lambda: ts(sm("k"), sm("k"), MAGIC, None, A_),
                lambda: ts(sm("k"), sm("k"), MAGIC, None, S_),
                lambda: stt(sm("f"), sm("k"), -C1, sm("phi"), M, A_),
                lambda: stt(sm("f"), sm("k"), -C2, sm("f"), M, A_),
                lambda: stt(sm("f"), sm("k"), -C3, sm("f"), M, A_),
                lambda: ts(sm("f"), sm("f"), math.pi, -math.pi, ALU.min, ALU.max),
                lambda: stt(sm("ca"), sm("f"), -1.0, sm("f"), M, ALU.max),
                lambda: ts(sm("ca"), sm("ca"), -0.5, math.pi / 2, M, A_, sem("lam_dve")))
            dve.wait_ge(sem("lam_act"), 2)
            ts(sm("e2"), sm("th"), -1.0, 1.0, M, A_)
            tt(sm("cm1"), sm("s"), sm("s"), M)
            stt(sm("sphi"), sm("s"), 2.0, sm("c"), M, M)
            tt(sm("den"), lr, lr, M)
            tt(sm("e1"), li, li, M)
            seq(lambda: Dv.do(v.reciprocal(sm("e2"), sm("e2"))))
            ts(sm("cm1"), sm("cm1"), -2.0, None, M)
            tt(sm("den"), sm("den"), sm("e1"), A_)
            seq(lambda: stt(sm("em1"), sm("th"), 2.0, sm("e2"), M, M))
            ts(sm("cphi"), sm("cm1"), 1.0, None, A_)
            Dv.do(v.reciprocal(sm("den"), sm("den")))
            seq(lambda: ts(sm("r"), sm("em1"), 1.0, None, A_))
            tt(sm("nr"), sm("em1"), sm("cphi"), M)
            seq(lambda: tt(sm("nr"), sm("nr"), sm("cm1"), A_))
            tt(sm("ni"), sm("r"), sm("sphi"), M)
            tt(sm("r2"), sm("r"), sm("r"), M)
            tt(sm("p2r"), sm("sphi"), sm("sphi"), M)
            tt(sm("e1"), sm("cphi"), sm("cphi"), M)
            stt(sm("p2i"), sm("sphi"), 2.0, sm("cphi"), M, M)
            seq(lambda: ts(sm("ar"), sm("nr"), 1.0, None, A_))
            tt(sm("p2r"), sm("e1"), sm("p2r"), S_)
            tt(sm("r4"), sm("r2"), sm("r2"), M)
            tt(sm("e2"), sm("nr"), lr, M)
            tt(sm("th"), sm("ni"), li, M)
            tt(sm("s"), sm("ni"), lr, M)
            tt(sm("c"), sm("nr"), li, M)
            seq(lambda: tt(sm("zr"), sm("e2"), sm("th"), A_))
            tt(sm("zi"), sm("s"), sm("c"), S_)
            Dv.fence()
            tt(sm("e1"), sm("p2r"), sm("p2r"), M)
            tt(sm("e2"), sm("p2i"), sm("p2i"), M)
            stt(sm("p4i"), sm("p2r"), 2.0, sm("p2i"), M, M)
            seq(lambda: tt(sm("zr"), sm("zr"), sm("den"), M))
            tt(sm("zi"), sm("zi"), sm("den"), M)
            tt(sm("p4r"), sm("e1"), sm("e2"), S_, sem("lam_dve"))

            for m in range(KT):
                dve.wait_ge(sem("h1_hi"), m + 1)
                stt(hlo[:, m, :], x[:, m, :], col("g_mix_pre", m), f32(hhi[:, m, :]), M, S_, sem("h1_lo"))
                if m == 2:
                    split_lo(0)
                if m == 5:
                    split_lo(1)

            def wide(name):
                return sm(name).unsqueeze(2).to_broadcast([P, PAIRS, 32])

            def b_step(j):
                if j == 0:
                    dve.wait_ge(sem("ssm_b_in"), 16)
                src = b_raw if j == 0 else b_pow[j - 1]
                cr, ci = (wide("zr"), wide("zi")) if j == 0 else (wide("ar"), wide("ai"))
                sr, si = (src[:, k, :].rearrange("p (a b) -> p a b", b=32) for k in range(2))
                t3 = [t[:, :].rearrange("p (a b) -> p a b", b=32) for t in b_t]
                Dv.fence()
                tt(t3[0], sr, cr, M)
                tt(t3[1], si, ci, M)
                tt(t3[2], sr, ci, M)
                tt(t3[3], si, cr, M)
                Dv.fence()
                tt(b_pow[j][:, 0, :], b_t[0][:, :], b_t[1][:, :], S_)
                tt(b_pow[j][:, 1, :], b_t[2][:, :], b_t[3][:, :], A_, sem("b_ready"))

            def gate_rows():
                lf, ii = sq[1][0:4, :], sq[0][0:4, :]
                dve.wait_ge(sem("gate_z"), 1)
                stt(sq[1][0:4, :], acc[0:4, :], -1.0, acc[0:4, :], M, ALU.min, sem("gate_abs"))
                ts(ii, ii, col("b_i", 0, 1, 0, 4), None, A_)
                dve.wait_ge(sem("gate_ln"), 1)
                Dv.fence()
                stt(lf, acc[0:4, :], 0.0, lf, ALU.min, S_)
                Dv.fence()
                Dv.do(v.tensor_tensor_scan(acc[0:4, :], ones_row, lf, 0.0, M, A_))
                Dv.fence()
                tt(ii, ii, acc[0:4, :], S_)
                Dv.fence()
                Dv.do(v.tensor_tensor_scan(lf, zero_row, ii, NEG, A_, ALU.max))
                Dv.fence()
                tt(lf, lf, acc[0:4, :], A_)
                Dv.fence()
                ts(lf, lf, 0.0, None, ALU.max)
                Dv.fence()
                tt(rows[0:4, :], acc[0:4, :], lf, S_)
                Dv.do(v.tensor_copy(rows[32:36, :], lf), sem("rows_ready"))

            ones_row = ones[0:4, 0:1].to_broadcast([4, T1])
            zero_row = ident[0:4, 64:65].to_broadcast([4, T1])

            def rotate(t, sg):
                m0, m1, m2, m3 = (t_[:, :, :] for t_ in rot)
                pr, pi = (ph[:, k, 4 * t:4 * t + 4, :] for k in range(2))
                X = xst[t % 2]
                c0 = sg * SEG
                er, ei = (PS[:, 4:8, CHUNKS * k + c0:CHUNKS * k + c0 + SEG] for k in range(2))
                if sg == 0:
                    dve.wait_ge(sem("e_mm"), t + 1)
                    if t == 0:
                        dve.wait_ge(sem("ssm_tables"), 2)
                        for j in range(2):
                            Dv.do(v.memset(xst[j][:, :, :, 0:1], 0.0))
                    if t >= 2:
                        dve.wait_ge(sem("y_mm"), t - 1)
                Dv.fence()
                tt(m0, er, pr, M)
                tt(m1, ei, pi, M)
                tt(m2, ei, pr, M)
                tt(m3, er, pi, M, sem("e_used") if sg else None)
                Dv.fence()
                tt(m0, m0, m1, A_)
                tt(m2, m2, m3, S_)
                Dv.fence()
                for g in range(4):
                    decay = sm("r4")[:, 4 * t + g:4 * t + g + 1].to_broadcast([P, SEG])
                    for k, w in ((0, rot[0]), (1, rot[2])):
                        start = X[:, k, g, SEG:SEG + 1] if sg else 0.0
                        Dv.do(v.tensor_tensor_scan(w[:, g, :], decay, w[:, g, :], start, M, A_))
                Dv.fence()
                tt(m1, m0, pr, M)
                tt(m3, m2, pi, M)
                Dv.fence()
                tt(X[:, 0, :, 1 + c0:1 + c0 + SEG], m1, m3, S_)
                Dv.fence()
                tt(m1, m0, pi, M)
                tt(m3, m2, pr, M)
                Dv.fence()
                tt(X[:, 1, :, 1 + c0:1 + c0 + SEG], m1, m3, A_, sem("x_ready") if sg else None)

            def mlstm_probs(h):
                dve.wait_ge(sem("w_ready"), h + 1)
                dve.wait_ge(sem("s_mm"), h + 1)
                sc = P ** -0.5
                stt(two(Wm[:, 0:T1]), PS[:, 6:8, 0:HALF], sc, two(Wm[:, 0:T1]), M, M)
                for j, (bank, c) in {1: (5, 0), 2: (4, 0), 3: (4, 272), 4: (4, 416)}.items():
                    k = min(P, S_LEN[j])
                    w = Wm[0:k, S_OFF[j]:S_OFF[j] + S_LEN[j]]
                    stt(w, PS[0:k, bank, c:c + S_LEN[j]], sc, w, M, M, sem("p_ready") if j == 4 else None)

            def mlstm_den(h):
                dve.wait_ge(sem("densq_ready"), h + 1)
                Dv.fence()
                tt(acc[:, :], acc[:, :], sq[1][:, :], ALU.max, sem("den_used"))

            def mlstm_out(h):
                dve.wait_ge(sem("ss_mm"), h + 1)
                Dv.fence()
                stt(two(acc[:, :]), two(acc[:, :]), EPS * P, PS[:, 4:6, 0:HALF], M, A_, sem("z_ready"))
                dve.wait_ge(sem("sd_ready"), h + 1)
                Dv.do(v.reciprocal(acc[:, :], acc[:, :]))
                Dv.fence()
                dve.wait_ge(sem("numsq_ready"), h + 1)
                tt(num[:, :], num[:, :], acc[:, :], M)
                Dv.fence()
                dve.wait_ge(sem("og_ready"), h + 1)
                stt(num[:, :], num[:, :], col("g_head", h), og[:, h, :], M, M, sem("yb_pre"))
                dve.wait_ge(sem("yb_hi"), h + 1)
                tt(yblo[:, h, :], num[:, :], f32(ybhi[:, h, :]), S_, sem("yb_lo"))

            for n in range(U_GLU):
                split_lo(n + LOOK)
                if n == 0:
                    rstd(0, T1)
                if n == U_Q:
                    Dv.fence()
                    for j in range(2):
                        Dv.do(v.memset(qp[j][:, 0:3], 0.0))
                dve.wait_ge(unit_done, n + 1)
                s = n % 2
                if n < U_GATES:
                    tt(two(u[:, n, :]), pair(s), two(rs[:, :]), M, evacuated)
                elif n == U_GATES:
                    tt(two(sq[0][0:4, :]), PS[0:4, 2 * s:2 * s + 2, 0:HALF], two(rs[0:4, :]), M)
                    tt(two(acc[0:4, :]), PS[32:36, 2 * s:2 * s + 2, 0:HALF], two(rs[32:36, :]), M, evacuated)
                elif n < U_V:
                    m = n - U_Q
                    if m >= 2:
                        dve.wait_ge(sem("tap_ready"), 3 * (m - 1))
                    if m == 0:
                        Dv.fence()
                    tt(two(qp[m % 2][:, 3:T1 + 3]), pair(s), two(rs[:, :]), M, evacuated)
                elif n < U_O:
                    j = n - U_V
                    if j == 0:
                        dve.wait_ge(sem("tap_added"), 6 * HEADS1)
                    if j >= 2:
                        dve.wait_ge(sem("vt_mm"), j - 1)
                    tt(two(vT[j % 2][:, :]), pair(s), two(rs[:, :]), M, evacuated)
                elif n < U_GA:
                    tt(two(og[:, n - U_O, :]), pair(s), two(rs[:, :]), M, evacuated)
                else:
                    tt(two(G[:, n - U_GA, :]), pair(s), two(rs[:, :]), M, evacuated)
                if n < 4:
                    b_step(n)
                if n == U_GATES:
                    gate_rows()
                if E_AFTER[0] <= n < E_AFTER[0] + 8:
                    rotate(*divmod(n - E_AFTER[0], 2))
                if n in Y_AFTER:
                    t = Y_AFTER.index(n)
                    dve.wait_ge(sem("y_mm"), t + 1)
                    stt(two(u[:, t, :]), two(u[:, t, :]), col("ssm_d", t), PS[:, 4:6, 0:HALF], M, A_, sem("y_used"))
                if U_O <= n < U_GA:
                    j = n - U_O
                    dve.wait_ge(sem("ya_hi"), j + 1)
                    tt(yalo[:, j, :], u[:, j, :], f32(yahi[:, j, :]), S_, sem("ya_lo"))
                if n >= U_GA - 1:
                    h, k = divmod(n - (U_GA - 1), 4)
                    if h < HEADS1:
                        (lambda h: None, mlstm_probs, mlstm_den, mlstm_out)[k](h)

            if upto <= 1:
                return
            for n in range(U_GLU, U_MERGE):
                split_lo(n + LOOK)
            for m in range(CT):
                tt(u_a(m), f32(yahi[:, m, :]), f32(yalo[:, m, :]), A_)
                dve.wait_ge(sem("glu_sg"), m + 1)
                Dv.fence()
                tt(u_a(m), u_a(m), sq[m % 2][:, :], M, sem("ya2_pre"))
            for m in range(CT):
                dve.wait_ge(sem("ya2_hi"), m + 1)
                tt(yalo[:, m, :], u_a(m), f32(yahi[:, m, :]), S_, sem("ya2_lo"))
            for k in range(2):
                Dv.do(v.tensor_copy(small[:, 480:481], small[:, 490:491]), evacuated)
                Dv.fence()

            def gslice(k):
                return two(G[:, bass.ds(k, 1), :].rearrange("p a b -> p (a b)"))

            dve.wait_ge(sem("g_ready"), 2 * KT)
            with Dv.loop(2, {lo_ready: 4, evacuated: 4, sem("mg_pre"): 4, sem("mg_lo"): 4, dve_steps: 4}) as i:
                for j in range(4):
                    s = (U_MERGE + j) % 2
                    split_lo(U_MERGE + j + LOOK, i * 4)
                    dve.wait_ge(unit_done, i * 4 + (U_MERGE + j + 1))
                    Dv.fence()
                    tt(two(sq[j % 2][:, :]), pair(s), gslice(i * 4 + j), M)
                    tt(two(num[:, :]), PS[:, 4 + 2 * s:6 + 2 * s, 0:HALF], gslice(i * 4 + (KT + j)), M, evacuated)
                    Dv.fence()
                    tt(sq[j % 2][:, :], sq[j % 2][:, :], num[:, :], A_, sem("mg_pre"))
                    dve.wait_ge(sem("mg_hi"), i * 4 + (j + 1))
                    one = (slice(None), bass.ds(i * 4 + j, 1), slice(None))
                    tt(hlo[one].rearrange("p a b -> p (a b)"), sq[j % 2][:, :],
                       f32(hhi[one].rearrange("p a b -> p (a b)")), S_, sem("mg_lo"))
            with Dv.loop(2, {lo_ready: 4, evacuated: 4}) as i:
                for j in range(4):
                    split_lo(U_OUT + j + LOOK, i * 4)
                    dve.wait_ge(unit_done, i * 4 + (U_OUT + j + 1))
                    Dv.do(v.tensor_copy(two(ysum[:, bass.ds(i * 4 + j, 1), :].rearrange("p a b -> p (a b)")),
                                        pair((U_OUT + j) % 2)), evacuated)
            def residual(norm, gain, n, c0, ready, hi, lo, pre):
                rstd(norm, n)
                for m in range(KT + 1):
                    if m < KT:
                        tt(ysum[:, m, 0:n], ysum[:, m, 0:n], rs[:, 0:n], M)
                        Dv.fence()
                        stt(x[:, m, c0:T1], ysum[:, m, 0:n], col(gain, m), x[:, m, c0:T1], M, A_, sem(ready))
                    if m:
                        dve.wait_ge(sem(hi), m)
                        stt(hlo[:, m - 1, 0:n], x[:, m - 1, c0:T1], col(pre, m - 1), f32(hhi[:, m - 1, 0:n]), M, S_, sem(lo))

            dve.wait_ge(sem("x_again"), 16)
            residual(1, "g_mix_post", T1, 0, "x1_ready", "h2_hi", "h2_lo", "g_ffn_pre")
            for j in range(2):
                Dv.do(v.memset(gp[j][:, 0:2], 0.0))
            if upto <= 2:
                return

            def ffn_pair(s, r, f, rf, fl, rfl, first):
                p = f % 2
                split_lo(s + LOOK, r)
                if first:
                    rstd(2, T1)
                dve.wait_ge(unit_done, r + (s + 1))
                if not isinstance(rf, int) or f >= 2:
                    dve.wait_ge(sem("conv2_ready"), rf + (f - 1))
                tt(two(gp[p][:, 2:T1 + 2]), pair(s % 2), two(rs[:, :]), M, evacuated)
                split_lo(s + 1 + LOOK, r)
                dve.wait_ge(unit_done, r + (s + 2))
                if not isinstance(rf, int) or f >= 2:
                    dve.wait_ge(sem("fa_lo"), rf + (f - 1))
                tt(tup[p][:, :], PS[:, 2 * ((s + 1) % 2), :], rs[:, META:T1], M, evacuated)
                dve.wait_ge(sem("gl_ready"), rf + (f + 1))
                Dv.fence()
                tt(tup[p][:, :], tup[p][:, :], cg[p][:, :], M, sem("fa_pre"))
                dve.wait_ge(sem("fa_hi"), rf + (f + 1))
                pick = (slice(None), bass.ds(rfl + fl, 1), slice(None)) if not isinstance(rfl, int) else (slice(None), slice(fl, fl + 1), slice(None))
                tt(falo[pick].rearrange("p a b -> p (a b)"), tup[p][:, :], f32(fahi[pick].rearrange("p a b -> p (a b)")), S_, sem("fa_lo"))

            s0, f0 = U_FFN, 0
            for c, tiles in enumerate(FFN_CHUNKS):
                first = 0
                if c == 0:
                    ffn_pair(s0, 0, 0, 0, 0, 0, True)
                    ffn_pair(s0 + 2, 0, 1, 0, 1, 0, False)
                    first = 1
                with Dv.loop(tiles // 2 - first, {lo_ready: 4, evacuated: 4, sem("fa_pre"): 2, sem("fa_lo"): 2}) as i:
                    for q in range(2):
                        ffn_pair(s0 + 4 * first + 2 * q, i * 4, f0 + 2 * first + q, i * 2, 2 * first + q, i * 2, False)
                s0 += 2 * tiles
                f0 += tiles
                with Dv.loop(2, {lo_ready: 4, evacuated: 4}) as i:
                    for j in range(4):
                        split_lo(s0 + j + LOOK, i * 4)
                        dve.wait_ge(unit_done, i * 4 + (s0 + j + 1))
                        o = ysum[:, bass.ds(i * 4 + j, 1), 0:SEQ].rearrange("p a b -> p (a b)")
                        if c == 0:
                            Dv.do(v.tensor_copy(o, PS[:, 2 * ((s0 + j) % 2), :]), evacuated)
                        else:
                            tt(o, o, PS[:, 2 * ((s0 + j) % 2), :], A_, evacuated)
                s0 += KT
            residual(3, "g_ffn_post", SEQ, META, "x2_ready", "h3_hi", "h3_lo", "attn_norm")
            if upto <= 3:
                return

            for n in range(U_V2, U_F2):
                split_lo(n + LOOK)
                j = n - U_V2
                if j == 0:
                    rstd(4, SEQ)
                dve.wait_ge(unit_done, n + 1)
                if j >= 2:
                    dve.wait_ge(sem("v2t_mm"), j - 1)
                tt(vT2[j % 2][:, :], PS[:, n % 2, :], rs[:, 0:SEQ], M, evacuated)
            split_lo(U_F2 + LOOK)
            dve.wait_ge(unit_done, U_F2 + 1)
            fz, fl_ = fox[0][0:N_FOX, :], fox[1][0:N_FOX, :]
            tt(fz, PS[0:N_FOX, U_F2 % 2, :], rs[0:N_FOX, 0:SEQ], M, evacuated)
            dve.wait_ge(sem("fox_z"), 1)
            stt(fl_, fz, -1.0, fz, M, ALU.min, sem("fox_abs"))
            dve.wait_ge(sem("fox_ln"), 1)
            stt(fl_, fz, 0.0, fl_, ALU.min, S_)
            Dv.fence()
            Dv.do(v.tensor_tensor_scan(fz, ones[0:N_FOX, 0:1].to_broadcast([N_FOX, SEQ]), fl_, 0.0, M, A_))
            Dv.fence()
            ts(fz, fz, -1.0, None, M, None, sem("fox_ready"))
            for j in range(3):
                n = U_GFOX + j
                split_lo(n + LOOK)
                dve.wait_ge(unit_done, n + 1)
                tt(sgf[:, j, :], PS[:, n % 2, :], rs[:, 0:SEQ], M, evacuated)

            for j in range(2):
                Dv.do(v.memset(qa[j][64:65, :, :], 1.0), sem("qa_ones"))

            def qk_evac(i, w):
                n = U_QK2 + 2 * i + w
                split_lo(n + LOOK)
                dve.wait_ge(unit_done, n + 1)
                Dv.fence()
                tt(qr[w][:, :], PS[:, n % 2, :], rs[:, 0:SEQ], M, evacuated)

            def qk_norm(i, w):
                dve.wait_ge(sem("qstd_ready"), 2 * i + w + 1)
                f = sq[w][:, 0:SEQ]
                Dv.do(v.reciprocal(f, f))
                Dv.fence()
                if i >= 2:
                    dve.wait_ge(sem("qk_mm"), 2 * (i - 1))
                dst = (qa, ka)[w][i % 2]
                for hh in range(2):
                    a = slice(64 * hh, 64 * hh + 64)
                    g = cols[a, COL[("q_gain", "k_gain")[w]] + i:COL[("q_gain", "k_gain")[w]] + i + 1]
                    stt(dst[0:64, hh, :], qr[w][a, :], g, sq[w][a, 0:SEQ], M, M, sem("aug_ready"))

            def maxima(i, hh):
                h = 2 * i + hh
                b = 2 + 3 * hh
                dve.wait_ge(sem("qk_mm"), h + 1)
                if i:
                    dve.wait_ge(sem("p2_ready"), 4 * (h - 1))
                for t in range(4):
                    bank, c = QB[t]
                    Dv.do(v.tensor_reduce(nm[:, 4 * hh + t:4 * hh + t + 1], PS[:, b + bank, c:c + P * (t + 1)],
                                          AX.X, ALU.max, negate=True), sem("max_ready"))

            def weigh(i, hh):
                h = 2 * i + hh
                if h < N_MOBA + N_FOX:
                    return
                for t in range(4):
                    bank, c = QB[t]
                    w = P * (t + 1)
                    dve.wait_ge(sem("p2_ready"), 4 * h + t + 1)
                    Dv.do(v.tensor_tensor_reduce(out=Pb[hh][:, bank, c:c + w], in0=Pb[hh][:, bank, c:c + w],
                                                 in1=dil[:, 1, P * (3 - t):SEQ], scale=1.0, scalar=0.0, op0=M, op1=A_,
                                                 accum_out=rsum[:, 4 * hh + t:4 * hh + t + 1]), sem("weighed"))

            def pt_copy(i, hh):
                h = 2 * i + hh
                dve.wait_ge(sem("pt_mm"), h + 1)
                Dv.do(v.tensor_copy(Pb[hh][:, 2, 0:2 * P], PS[:, 2 + 3 * hh + 2, 0:2 * P]), sem("pt_dve"))

            def attn_out(i, hh):
                h = 2 * i + hh
                Dv.fence()
                dve.wait_ge(sem("p2_ready"), 4 * h + 4)
                Dv.do(v.reciprocal(rinv[:, 4 * hh:4 * hh + 4], rsum[:, 4 * hh:4 * hh + 4]))
                Dv.fence()
                dve.wait_ge(sem("pv_mm"), h + 1)
                tt(yq[:, :, HD * h:HD * h + HD], PS[:, 2 + 3 * hh, 0:4 * HD].rearrange("p (a b) -> p a b", a=4),
                   rinv[:, 4 * hh:4 * hh + 4].unsqueeze(2).to_broadcast([P, 4, HD]), M, sem("attn_done"))

            for i in range(KT + 2):
                if i < KT:
                    qk_evac(i, 0)
                if i >= 2:
                    attn_out(i - 2, 1)
                if 1 <= i <= KT:
                    maxima(i - 1, 0)
                if i < KT:
                    qk_evac(i, 1)
                if 1 <= i <= KT:
                    weigh(i - 1, 0)
                    maxima(i - 1, 1)
                if i < KT:
                    qk_norm(i, 0)
                if 1 <= i <= KT:
                    pt_copy(i - 1, 0)
                    weigh(i - 1, 1)
                if i < KT:
                    qk_norm(i, 1)
                if 1 <= i <= KT:
                    attn_out(i - 1, 0)
                    pt_copy(i - 1, 1)

            dve.wait_ge(sem("gstd_ready"), 3)
            Dv.do(v.reciprocal(gss[:, 0:12], gss[:, 0:12]))
            Dv.fence()
            for t in range(4):
                for g, (a, b) in enumerate(GROUPS):
                    ts(yq[:, t, a:b], yq[:, t, a:b], gss[:, 4 * g + t:4 * g + t + 1], None, M, None, sem("yn_ready"))
            for m in range(KT):
                dve.wait_ge(sem("yt_mm"), m + 1)
                src = PS[:, 2 + m % 6, :]
                if m in FOX_TILES:
                    dve.wait_ge(sem("sgf_ready"), 3)
                    stt(qr[m % 2][:, :], src, col("out_gain", m), sgf[:, m - FOX_TILES[0], :], M, M, sem("yfox_pre"))
                    dve.wait_ge(sem("y2_hi"), m + 1)
                    tt(hlo[:, m, 0:SEQ], qr[m % 2][:, :], f32(hhi[:, m, 0:SEQ]), S_, sem("y2_lo"))
                else:
                    dve.wait_ge(sem("y2_hi"), m + 1)
                    stt(hlo[:, m, 0:SEQ], src, col("out_gain", m), f32(hhi[:, m, 0:SEQ]), M, S_, sem("y2_lo"))
            for m in range(KT):
                n = U_OUT2 + m
                split_lo(n + LOOK)
                dve.wait_ge(unit_done, n + 1)
                tt(x[:, m, META:T1], x[:, m, META:T1], PS[:, n % 2, :], A_, evacuated)
            for m in range(KT):
                dve.wait_ge(sem("h4_hi"), m + 1)
                stt(hlo[:, m, 0:SEQ], x[:, m, META:T1], col("mlp_norm", m), f32(hhi[:, m, 0:SEQ]), M, S_, sem("h4_lo"))

            def mlp_up(s, r, f, rf, fl):
                p = f % 2
                split_lo(s + LOOK, r)
                dve.wait_ge(sem("relu_ready"), rf + (f + 1))
                if not isinstance(rf, int) or f >= 2:
                    dve.wait_ge(sem("ma_lo"), rf + (f - 1))
                stt(r2[p][:, :], PS[:, s % 2, :], 0.0, rl[p][:, :], ALU.max, M, evacuated)
                dve.wait_ge(sem("ma_hi"), rf + (f + 1))
                tt(malo[:, fl, :], r2[p][:, :], f32(mahi[:, fl, :]), S_, sem("ma_lo"))

            def mlp_down(s, r, m):
                split_lo(s + LOOK, r)
                dve.wait_ge(unit_done, r + (s + 1))
                if isinstance(r, int) and s < U_MLP + 2 * KT:
                    Dv.do(v.tensor_copy(ysum[:, m, 0:SEQ], PS[:, s % 2, :]), evacuated)
                else:
                    tt(ysum[:, m, 0:SEQ], ysum[:, m, 0:SEQ], PS[:, s % 2, :], A_, evacuated)

            for f in range(KT):
                mlp_up(U_MLP + f, 0, f, 0, f)
                if f == 0:
                    rstd(5, SEQ)
                    tt(rs[:, 0:SEQ], rs[:, 0:SEQ], rs[:, 0:SEQ], M)
            for m in range(KT):
                mlp_down(U_MLP + KT + m, 0, m)
            with Dv.loop(2, {lo_ready: 16, evacuated: 16, sem("ma_lo"): 8}) as c:
                for f in range(KT):
                    mlp_up(U_MLP + 2 * KT + f, c * 16, KT + f, c * 8, f)
                for m in range(KT):
                    mlp_down(U_MLP + 3 * KT + m, c * 16, m)
            for f in range(KT):
                mlp_up(U_MLP + 6 * KT + f, 0, 3 * KT + f, 0, f)
            for m in range(KT):
                s = U_MLP + 7 * KT + m
                split_lo(s + LOOK)
                dve.wait_ge(unit_done, s + 1)
                tt(ysum[:, m, 0:SEQ], ysum[:, m, 0:SEQ], PS[:, s % 2, :], A_, evacuated)
                Dv.fence()
                tt(ysum[:, m, 0:SEQ], ysum[:, m, 0:SEQ], rs[:, 0:SEQ], M)
                Dv.fence()
                if m >= 2:
                    dve.wait_ge(sem(f"out_done{m % 2}"), 16 * (m // 2))
                tt(ot[m % 2][:, :], ysum[:, m, 0:SEQ], x[:, m, META:T1], A_, sem("out_ready"))

        @block.gpsimd
        def _(pool):
            Po = Order(pool, pool_steps)
            g = nc.gpsimd
            M, A_, S_ = ALU.mult, ALU.add, ALU.subtract

            def tt(o, a, b, op, s=None):
                Po.do(g.tensor_tensor(o, a, b, op), s)

            def add_squares(norm, n):
                for m in range(1, KT):
                    pool.wait_ge(sem("sq_ready"), KT * norm + m + 1)
                    Po.fence()
                    tt(acc[:, 0:n], acc[:, 0:n], sq[m % 2][:, 0:n], A_, sem("sq_added"))

            add_squares(0, T1)
            pool.wait_ge(sem("lam_dve"), 2)
            pr, pi = ph[:, 0, :, :], ph[:, 1, :, :]
            Po.do(g.tensor_copy(pr[:, :, 0:1], sm("p4r").unsqueeze(2)))
            Po.do(g.tensor_copy(pi[:, :, 0:1], sm("p4i").unsqueeze(2)))
            m = 1
            while m < SEG:
                k = min(m, SEG - m)
                br, bi = (q[:, :, m - 1:m].to_broadcast([P, PAIRS, k]) for q in (pr, pi))
                t4 = [t[:, 0:PAIRS * k].rearrange("p (a b) -> p a b", a=PAIRS) for t in c_t]
                Po.fence()
                tt(t4[0], pr[:, :, 0:k], br, M)
                tt(t4[1], pi[:, :, 0:k], bi, M)
                tt(t4[2], pr[:, :, 0:k], bi, M)
                tt(t4[3], pi[:, :, 0:k], br, M)
                Po.fence()
                tt(pr[:, :, m:m + k], t4[0], t4[1], S_)
                tt(pi[:, :, m:m + k], t4[2], t4[3], A_)
                m += k
            pool.wait_ge(sem("ssm_c_in"), 16)
            Po.fence()
            Po.do(g.tensor_scalar(c_pow[:, 0, 1, :], c_pow[:, 0, 1, :], -1.0, None, M), sem("ssm_tables"))
            wr, wi = (sm(k).unsqueeze(2).to_broadcast([P, PAIRS, 32]) for k in ("ar", "ai"))
            for j in range(STEP):
                cr, cn = (c_pow[:, j, k, :].rearrange("p (a b) -> p a b", b=32) for k in range(2))
                t3 = [t[:, :].rearrange("p (a b) -> p a b", b=32) for t in c_t]
                Po.fence()
                tt(t3[0], cr, wr, M)
                tt(t3[1], cn, wi, M)
                tt(t3[2], cn, wr, M)
                tt(t3[3], cr, wi, M)
                Po.fence()
                tt(c_pow[:, j + 1, 0, :], c_t[0][:, :], c_t[1][:, :], A_)
                tt(c_pow[:, j + 1, 1, :], c_t[2][:, :], c_t[3][:, :], S_, sem("ssm_tables") if j == STEP - 1 else None)

            pool.wait_ge(sem("bt_mm"), 2 * STEP)
            Po.do(g.memset(kblk[:, :, :, :], 0.0), sem("kz"))
            for m in range(2 * HEADS1):
                for k in range(1, 4):
                    pool.wait_ge(sem("tap_ready"), 3 * m + k)
                    Po.fence()
                    tt(qk[:, m, :], qk[:, m, :], vT[k % 2][:, :], A_, sem("tap_added"))
                if m == 4:
                    pool.wait_ge(sem("k_mm"), 1)
                    Po.do(g.memset(vs[:, 4, :], 0.0), sem("vz"))
            pool.wait_ge(sem("ya_lo"), CT)
            Po.do(g.memset(Wm[:, S_OFF[4]:S_OFF[4] + 16], 0.0))
            for h in range(HEADS1):
                pool.wait_ge(sem("bc_done"), h + 1)
                if h:
                    pool.wait_ge(sem("nd_mm"), h)
                Po.fence()
                for j in range(5):
                    k = min(P, S_LEN[j])
                    tt(Wm[0:k, S_OFF[j]:S_OFF[j] + k], sq[0][0:k, P * j:P * j + k], mask_st[0:k, 0:k], A_, sem("diag_done"))
            if upto <= 1:
                return
            add_squares(1, T1)
            add_squares(2, T1)
            if upto <= 2:
                return

            s0, f = U_FFN, 0
            for tiles in FFN_CHUNKS:
                for q in range(tiles):
                    src, dst = gp[f % 2], cg[f % 2]
                    w = [col("ffn_conv", 4 * f + k) for k in range(4)]
                    pool.wait_ge(evacuated, s0 + 2 * q + 1)
                    if f >= 2:
                        pool.wait_ge(sem("fa_pre"), f - 1)
                    Po.do(g.tensor_scalar(dst[:, :], src[:, META:META + SEQ], w[0], w[3], M, A_))
                    for k in (1, 2):
                        Po.fence()
                        Po.do(g.tensor_scalar(ctmp[:, :], src[:, META + k:META + k + SEQ], w[k], None, M))
                        Po.fence()
                        tt(dst[:, :], dst[:, :], ctmp[:, :], A_, sem("conv2_ready") if k == 2 else None)
                    f += 1
                s0 += 2 * tiles + KT
            add_squares(3, SEQ)
            add_squares(4, SEQ)
            if upto <= 3:
                return
            pool.wait_ge(sem("yb_lo"), HEADS1)
            pool.dma_start(dil[:, :, :], dil_in.rearrange("p (a b) -> p a b", a=2)).then_inc(sem("dil_in"), 16)
            pool.wait_ge(sem("fox_ready"), 1)
            for i in range(KT):
                if i >= 2:
                    pool.wait_ge(sem("qk_mm"), 2 * (i - 1))
                for hh in range(2):
                    h = 2 * i + hh
                    if N_MOBA <= h < N_MOBA + N_FOX:
                        src = fox[0][h - N_MOBA:h - N_MOBA + 1, :]
                    else:
                        src = alibi_in[h:h + 1, :]
                    pool.dma_start(ka[i % 2][64:65, hh, :], src).then_inc(sem(f"bias_in{i % 2}"), 16)
            add_squares(5, SEQ)

        @block.tensor
        def _(pe):
            mm = nc.tensor.matmul

            def unit(s, r, xhi, xlo, outs, ready=None, base=0, blocks=None, last_of_unit=True):
                blocks = blocks or [(k, k) for k in range(KT)]
                for b, (kw, kx) in enumerate(blocks):
                    if ready is not None:
                        pe.wait_ge(ready, base + kx + 1)
                    w = slice(kw * P, kw * P + P)
                    for a, (wt, xt) in enumerate(((whi, xhi), (whi, xlo), (wlo, xhi))):
                        for o, c0, n in outs:
                            ins = mm(o, wt[:, s % RING, w], xt[:, kx, c0:c0 + n], start=(b == 0 and a == 0),
                                     stop=(b == len(blocks) - 1 and a == 2))
                if last_of_unit:
                    ins.then_inc(unit_done, 1)

            def begin(s, r=0):
                pe.wait_ge(lo_ready, r + (s + 1))
                if s >= 2:
                    pe.wait_ge(evacuated, r + (s - 1))

            def halves(s, b0=None):
                b = 2 * (s % 2) if b0 is None else b0
                return [(PS[:, b + h, 0:HALF], HALF * h, HALF) for h in range(2)]

            def stat(norm, n):
                pe.wait_ge(sem("sq_added"), 7 * (norm + 1))
                if n == T1:
                    for h in range(2):
                        ins = mm(PS[:, 4 + h, 0:HALF], ones, acc[:, HALF * h:HALF * h + HALF], start=True, stop=True)
                else:
                    ins = mm(PS[:, 4, :], ones, acc[:, 0:SEQ], start=True, stop=True)
                ins.then_inc(sem("stat_mm"), 1)

            def b_transposes(ri):
                pe.wait_ge(sem("b_ready"), STEP)
                if ri == 0:
                    pe.wait_ge(sem("std_ready"), 1)
                for s in range(STEP):
                    if ri:
                        pe.wait_ge(sem("bt_copied"), s + 1)
                    for t in range(CT):
                        ins = nc.tensor.transpose(PS[:, 4 + s, P * t:P * t + P], b_pow[s][:, ri, P * t:P * t + P], ident)
                    ins.then_inc(sem("bt_mm"), 1)

            def gate_transposes():
                pe.wait_ge(sem("bt_copied"), 2 * STEP)
                pe.wait_ge(sem("rows_ready"), 1)
                for j in range(5):
                    k = min(P, T1 - P * j)
                    ins = nc.tensor.transpose(PS[0:k, 4, 4 * j:4 * j + 4], sq[0][0:4, P * j:P * j + k], ident[0:4, 0:4])
                ins.then_inc(sem("r2_mm"), 1)

            def ssm_in(t):
                if t == 0:
                    pe.wait_ge(sem("r2c_ready"), 1)
                else:
                    pe.wait_ge(sem("k_ready"), 4)
                    pe.wait_ge(sem("e_used"), t)
                if t >= 2:
                    pe.wait_ge(sem("y_used"), t - 1)
                for g in range(4):
                    q = slice(32 * g, 32 * g + 32)
                    for ri in range(2):
                        for s in range(STEP):
                            ins = mm(PS[:, 4 + g, CHUNKS * ri:CHUNKS * ri + CHUNKS], bT[q, ri, STEP - 1 - s, t, :],
                                     u[q, t, s:T1:STEP], start=(s == 0), stop=(s == STEP - 1),
                                     tile_position=(32 * g, 0))
                ins.then_inc(sem("e_mm"), 1)

            def ssm_kernel():
                pe.wait_ge(sem("ssm_tables"), 2)
                pe.wait_ge(sem("e_used"), 1)
                for t in range(CT):
                    for g in range(4):
                        c = slice(32 * (4 * t + g), 32 * (4 * t + g) + 32)
                        for ri in range(2):
                            ins = mm(PS[32 * g:32 * g + 32, 4, P * t:P * t + P], b_pow[0][:, ri, c],
                                     c_pow[:, 0:STEP, ri, c], start=(ri == 0), stop=(ri == 1),
                                     tile_position=(0, 32 * g))
                ins.then_inc(sem("k_mm"), 1)

            def ssm_out(t):
                pe.wait_ge(sem("x_ready"), t + 1)
                pe.wait_ge(sem("e_used"), min(t + 2, CT))
                if t == CT - 1:
                    pe.wait_ge(sem("y_used"), t)
                X = xst[t % 2]
                for h in range(2):
                    y = PS[:, 4 + h, 0:HALF].rearrange("p (c s) -> p c s", s=STEP)
                    uu = u[:, t, HALF * h:HALF * h + HALF].rearrange("p (c s) -> p c s", s=STEP)
                    for j in range(STEP):
                        mm(y[:, :, j:STEP], kblk[:, t, j, :], uu[:, :, 0:STEP - j], start=(j == 0), stop=False,
                           skip_group_check=True)
                    for g in range(4):
                        c = slice(32 * (4 * t + g), 32 * (4 * t + g) + 32)
                        for s in range(STEP):
                            for ri in range(2):
                                ins = mm(y[32 * g:32 * g + 32, :, s], c_pow[:, s + 1, ri, c],
                                         X[:, ri, g, SEG * h:SEG * h + SEG], start=False,
                                         stop=(s == STEP - 1 and ri == 1), skip_group_check=True,
                                         tile_position=(0, 32 * g))
                ins.then_inc(sem("y_mm"), 1)

            def v_transposes(j):
                b = VT_BANK[j]
                pe.wait_ge(evacuated, U_V + j + 1)
                if j in (0, 1):
                    pe.wait_ge(sem("e_used"), CT)
                if j in (1, 3):
                    pe.wait_ge(sem("vs_ready"), j if j == 1 else 2)
                if j == 2:
                    pe.wait_ge(sem("y_used"), CT)
                for k in range(4):
                    nc.tensor.transpose(PS[:, b, P * k:P * k + P], vT[j % 2][:, P * k:P * k + P], ident)
                nc.tensor.transpose(PS[0:16, b + 1, 0:P], vT[j % 2][:, 512:T1], ident).then_inc(sem("vt_mm"), 1)

            def mlstm_broadcast(h):
                pe.wait_ge(sem("sel_in"), 16)
                pe.wait_ge(sem("vs_ready"), 4)
                if h:
                    pe.wait_ge(sem("z_ready"), h)
                    pe.wait_ge(sem("den_used"), h)
                for p0, b in ((0, 4), (32, 6)):
                    for k in range(2):
                        ins = mm(PS[:, b + k, 0:HALF], sel[p0:p0 + 4, h, :], rows[p0:p0 + 4, HALF * k:HALF * k + HALF],
                                 start=True, stop=True, tile_position=(p0, 0))
                ins.then_inc(sem("bc_mm"), 1)

            def mlstm_scores(h):
                pe.wait_ge(sem("bc_done"), h + 1)
                pe.wait_ge(sem("qk_ready"), 2 * HEADS1)
                for k in range(2):
                    mm(PS[:, 6 + k, 0:HALF], qk[:, 4 + h, 0:P], qk[:, h, HALF * k:HALF * k + HALF], start=True, stop=True)
                for j, (bank, c) in {1: (5, 0), 2: (4, 0), 3: (4, 272), 4: (4, 416)}.items():
                    k = min(P, S_LEN[j])
                    ins = mm(PS[0:k, bank, c:c + S_LEN[j]], qk[:, 4 + h, P * j:P * j + k], qk[:, h, P * j:T1],
                             start=True, stop=True)
                ins.then_inc(sem("s_mm"), 1)

            def mlstm_values(h):
                pe.wait_ge(sem("p_ready"), h + 1)
                for b, lhs in ((4, lambda j: vs[:, j, P * h:P * h + P]), (6, lambda j: ones)):
                    for k in range(2):
                        js = [j for j in range(5) if P * j < HALF * (k + 1)]
                        for j in js:
                            t0 = max(P * j, HALF * k)
                            n = HALF * (k + 1) - t0
                            o = S_OFF[j] + t0 - P * j
                            ins = mm(PS[:, b + k, t0 - HALF * k:HALF], lhs(j), Wm[:, o:o + n], start=(j == 0),
                                     stop=(j == js[-1]), skip_group_check=True)
                ins.then_inc(sem("nd_mm"), 1)

            def mlstm_norm(h):
                pe.wait_ge(sem("numsq_ready"), h + 1)
                for k in range(2):
                    ins = mm(PS[:, 4 + k, 0:HALF], ones, sq[0][:, HALF * k:HALF * k + HALF], start=True, stop=True)
                ins.then_inc(sem("ss_mm"), 1)

            pe.wait_ge(sem("consts_in"), 16)
            for n in range(U_GLU):
                begin(n)
                unit(n, 0, hhi, hlo, halves(n), sem("h1_lo") if n == 0 else None)
                if n == 0:
                    stat(0, T1)
                if n in (4, 5):
                    b_transposes(n - 4)
                if n == 6:
                    gate_transposes()
                if n == 8:
                    ssm_kernel()
                if n in Y_AFTER:
                    ssm_out(Y_AFTER.index(n))
                if n in E_AFTER:
                    ssm_in(E_AFTER.index(n))
                if U_V + 1 <= n < U_V + 5:
                    v_transposes(n - U_V - 1)
                if n >= U_GA - 1:
                    h, k = divmod(n - (U_GA - 1), 4)
                    if h < HEADS1:
                        (mlstm_broadcast, mlstm_scores, mlstm_values, mlstm_norm)[k](h)

            if upto <= 1:
                return
            pe.wait_ge(sem("z_ready"), HEADS1)
            pe.wait_ge(sem("den_used"), HEADS1)
            pe.wait_ge(sem("ya_lo"), CT)
            for n in range(U_GLU, U_MERGE):
                begin(n)
                if n == U_GLU + 1:
                    pe.wait_ge(evacuated, U_GLU)
                unit(n, 0, yahi, yalo, halves(n), None, 0, [(k, k) for k in range(4)], False)
                unit(n, 0, yahi, yalo, halves(n, 4 + 2 * (n % 2)), None, 0, [(4 + k, k) for k in range(4)])
            pe.wait_ge(sem("yb_lo"), HEADS1)
            pe.wait_ge(sem("ya2_lo"), CT)
            pe.wait_ge(evacuated, U_MERGE)
            with pe.Fori(0, 2) as i:
                for j in range(4):
                    s = U_MERGE + j
                    begin(s, i * 4)
                    unit(s, i * 4, yahi, yalo, halves(s), None, 0, [(k, k) for k in range(4)], False)
                    unit(s, i * 4, ybhi, yblo, halves(s, 4 + 2 * (s % 2)), None, 0, [(4 + k, k) for k in range(4)])
            begin(U_OUT)
            unit(U_OUT, 0, hhi, hlo, halves(U_OUT), sem("mg_lo"))
            for n in range(U_OUT + 1, U_OUT + 4):
                begin(n)
                unit(n, 0, hhi, hlo, halves(n))
            for n in range(U_OUT + 4, U_FFN):
                begin(n)
                unit(n, 0, hhi, hlo, halves(n))
            stat(1, T1)
            if upto <= 2:
                return

            def ffn_gate(s, r, ready=None):
                begin(s, r)
                unit(s, r, hhi, hlo, halves(s), ready)

            def ffn_up(s, r):
                begin(s, r)
                unit(s, r, hhi, hlo, [(PS[:, 2 * (s % 2), :], META, SEQ)])

            def down(s, r, xhi, xlo, o, ready=None, base=0, tiles=KT):
                begin(s, r)
                unit(s, r, xhi, xlo, [(o, 0, SEQ)], ready, base, [(k, k) for k in range(tiles)])

            s0, f0 = U_FFN, 0
            for c, tiles in enumerate(FFN_CHUNKS):
                first = 0
                if c == 0:
                    ffn_gate(s0, 0, sem("h2_lo"))
                    stat(2, T1)
                    ffn_up(s0 + 1, 0)
                    ffn_gate(s0 + 2, 0)
                    ffn_up(s0 + 3, 0)
                    first = 1
                with pe.Fori(0, tiles // 2 - first) as i:
                    for q in range(2):
                        ffn_gate(s0 + 4 * first + 2 * q, i * 4)
                        ffn_up(s0 + 4 * first + 2 * q + 1, i * 4)
                s0 += 2 * tiles
                with pe.Fori(0, 2) as i:
                    for j in range(4):
                        down(s0 + j, i * 4, fahi, falo, PS[:, 2 * ((s0 + j) % 2), :], sem("fa_lo") if j == 0 else None,
                             f0, tiles)
                f0 += tiles
                s0 += KT
            stat(3, SEQ)
            if upto <= 3:
                return

            def v2_transposes(j):
                pe.wait_ge(evacuated, U_V2 + j + 1)
                if j >= 2:
                    pe.wait_ge(sem("v2_ready"), j - 1)
                for t in range(4):
                    ins = nc.tensor.transpose(PS[:, 2 + j % 2, P * t:P * t + P], vT2[j % 2][:, P * t:P * t + P], ident)
                ins.then_inc(sem("v2t_mm"), 1)

            def wide(s, r=0, ready=None):
                begin(s, r)
                unit(s, r, hhi, hlo, [(PS[:, s % 2, :], 0, SEQ)], ready)

            pe.wait_ge(evacuated, U_V2)
            wide(U_V2, 0, sem("h3_lo"))
            stat(4, SEQ)
            for n in range(U_V2 + 1, U_QK2):
                wide(n)
                if n <= U_F2:
                    v2_transposes(n - 1 - U_V2)

            def qk_stat(i, w):
                pe.wait_ge(sem("qsq_ready"), 2 * i + w + 1)
                mm(PS[:, (U_QK2 + w) % 2, :], blk64, sq[w][:, 0:SEQ], start=True, stop=True).then_inc(sem("qstat_mm"), 1)

            def scores(i, hh):
                h = 2 * i + hh
                b = 2 + 3 * hh
                q, k = qa[i % 2], ka[i % 2]
                pe.wait_ge(sem("aug_ready"), 4 * i + 4)
                pe.wait_ge(sem("qa_ones"), 2)
                pe.wait_ge(sem(f"bias_in{i % 2}"), 32 * (i // 2 + 1))
                if i:
                    pe.wait_ge(sem("attn_done"), h - 1)
                if h == N_MOBA + N_FOX:
                    pe.wait_ge(sem("dil_in"), 16)
                for t in range(4):
                    bank, c = QB[t]
                    w = P * (t + 1)
                    if h < N_MOBA + N_FOX:
                        mm(PS[:, b + bank, c + w - P:c + w], ident, mask_qk, start=True, stop=True)
                    else:
                        mm(PS[:, b + bank, c:c + w], ident, dil[:, 0, P * (3 - t):SEQ], start=True, stop=True)
                    ins = mm(PS[:, b + bank, c:c + w], q[0:65, hh, P * t:P * t + P], k[0:65, hh, 0:w], start=False,
                             stop=True, skip_group_check=True)
                ins.then_inc(sem("qk_mm"), 1)

            def p_transposes(i, hh):
                h = 2 * i + hh
                b = 2 + 3 * hh
                for t in range(4):
                    bank, c = QB[t]
                    pe.wait_ge(sem("p2_ready"), 4 * h + BANK_DONE[t])
                    if h >= N_MOBA + N_FOX:
                        pe.wait_ge(sem("weighed"), 4 * (h - N_MOBA - N_FOX) + BANK_DONE[t])
                    for k in range(t + 1):
                        ins = nc.tensor.transpose(PS[:, b + bank, c + P * k:c + P * k + P],
                                                  Pb[hh][:, bank, c + P * k:c + P * k + P], ident)
                ins.then_inc(sem("pt_mm"), 1)

            def values(i, hh):
                h = 2 * i + hh
                pe.wait_ge(sem("pt_act"), h + 1)
                pe.wait_ge(sem("pt_dve"), h + 1)
                if h == 0:
                    pe.wait_ge(sem("v2_ready"), KT)
                for t in range(4):
                    bank, c = QB[t]
                    for k in range(t + 1):
                        ins = mm(PS[:, 2 + 3 * hh, HD * t:HD * t + HD], Pb[hh][:, bank, c + P * k:c + P * k + P],
                                 V[:, k, HD * h:HD * h + HD], start=(k == 0), stop=(k == t))
                ins.then_inc(sem("pv_mm"), 1)

            for i in range(KT + 1):
                if i < KT:
                    n = U_QK2 + 2 * i
                    if i:
                        pe.wait_ge(sem("qstd_ready"), 2 * i - 1)
                    wide(n)
                if i >= 2:
                    values(i - 2, 1)
                if i:
                    scores(i - 1, 0)
                if i < KT:
                    if i:
                        pe.wait_ge(sem("qstd_ready"), 2 * i)
                    wide(n + 1)
                if i:
                    scores(i - 1, 1)
                if i < KT:
                    qk_stat(i, 0)
                if i:
                    p_transposes(i - 1, 0)
                if i < KT:
                    qk_stat(i, 1)
                if i:
                    values(i - 1, 0)
                    p_transposes(i - 1, 1)
            values(KT - 1, 1)

            pe.wait_ge(sem("attn_done"), HEADS2)
            pe.wait_ge(sem("yn_ready"), 12)
            for m in range(KT):
                if m >= 6:
                    pe.wait_ge(sem("y2_lo"), m - 5)
                for t in range(4):
                    ins = nc.tensor.transpose(PS[:, 2 + m % 6, P * t:P * t + P], yq[:, t, P * m:P * m + P], ident)
                ins.then_inc(sem("yt_mm"), 1)
            pe.wait_ge(sem("qstd_ready"), 2 * KT)
            for m in range(KT):
                wide(U_OUT2 + m, 0, sem("y2_lo") if m == 0 else None)

            pe.wait_ge(sem("y2_lo"), KT)
            for f in range(KT):
                wide(U_MLP + f, 0, sem("h4_lo") if f == 0 else None)
                if f == 0:
                    stat(5, SEQ)
            for m in range(KT):
                s = U_MLP + KT + m
                down(s, 0, mahi, malo, PS[:, s % 2, :], sem("ma_lo") if m == 0 else None, 0)
            with pe.Fori(0, 2) as c:
                for f in range(KT):
                    wide(U_MLP + 2 * KT + f, c * 16)
                for m in range(KT):
                    s = U_MLP + 3 * KT + m
                    down(s, c * 16, mahi, malo, PS[:, s % 2, :], sem("ma_lo") if m == 0 else None, c * 8 + KT)
            for f in range(KT):
                wide(U_MLP + 6 * KT + f)
            for m in range(KT):
                s = U_MLP + 7 * KT + m
                down(s, 0, mahi, malo, PS[:, s % 2, :], sem("ma_lo") if m == 0 else None, 3 * KT)
    return locals()


def kernel(x, meta_tokens, g_mix_pre, g_mix_post, w_in, b_gates, ssm_lambda_re, ssm_lambda_im, ssm_b_re, ssm_b_im,
           ssm_c_re, ssm_c_im, ssm_d, ssm_log_dt, w_ssm_glu, w_qk_conv, b_qk_conv, g_head_norm, w_branch_ssm,
           w_branch_mlstm, w_out, g_ffn_pre, g_ffn_post, w_ffn_gate, w_ffn_up, w_ffn_conv, b_ffn_conv, w_ffn_down,
           attn_norm_2, w_in_2, b_forget_2, q_gain_2, k_gain_2, out_gain_2, w_out_2, mlp_norm_2, w_up_2, w_down_2):
    import concourse.bacc as bacc
    from concourse.bass_utils import run_bass_kernel_spmd

    def unit(w, m, k0=0, n=KT):
        t = np.zeros((P, KT, P), np.float32)
        t[:, :n] = w[P * k0:P * (k0 + n), P * m:P * m + P].reshape(n, P, P).transpose(1, 0, 2)
        return t.reshape(P, KT * P)

    w1, w2 = np.asarray(w_in)[0], np.asarray(w_in_2)[0]
    c0 = SSM_W + 4 * 512
    gates = np.zeros((D_MODEL, P), np.float32)
    gates[:, 0:HEADS1] = w1[:, c0:c0 + HEADS1]
    gates[:, 32:32 + HEADS1] = w1[:, c0 + HEADS1:c0 + 2 * HEADS1]
    units = [unit(w1, m) for m in range(CT)] + [unit(gates, 0)]
    units += [unit(w1[:, SSM_W:], m) for m in range(16)]
    units += [unit(w1[:, c0 + 2 * HEADS1:], m) for m in range(2 * KT)]
    glu = np.asarray(w_ssm_glu)[0]
    units += [np.concatenate([unit(glu, 2 * j, 0, CT)[:, :512], unit(glu, 2 * j + 1, 0, CT)[:, :512]], 1)
              for j in range(2)]
    wa, wb = np.asarray(w_branch_ssm)[0], np.asarray(w_branch_mlstm)[0]
    units += [np.concatenate([unit(wa, m, 0, CT)[:, :512], unit(wb, m, 0, CT)[:, :512]], 1) for m in range(KT)]
    units += [unit(np.asarray(w_out)[0], m) for m in range(KT)]
    wg, wu, wd = np.asarray(w_ffn_gate)[0], np.asarray(w_ffn_up)[0], np.asarray(w_ffn_down)[0]
    f0 = 0
    for tiles in FFN_CHUNKS:
        for f in range(f0, f0 + tiles):
            units += [unit(wg, f), unit(wu, f)]
        units += [unit(wd, m, f0, tiles) for m in range(KT)]
        f0 += tiles
    v0, f2 = 2 * D_MODEL, 3 * D_MODEL
    units += [unit(w2[:, v0:], m) for m in range(KT)] + [unit(w2[:, f2:], 0)]
    units += [unit(w2[:, f2 + N_FOX:], m) for m in range(3)]
    for i in range(KT):
        units += [unit(w2, i), unit(w2, KT + i)]
    units += [unit(np.asarray(w_out_2)[0], m) for m in range(KT)]
    wup, wdn = np.asarray(w_up_2)[0], np.asarray(w_down_2)[0]
    for c in range(MLP_CHUNKS):
        units += [unit(wup, KT * c + f) for f in range(KT)] + [unit(wdn, m, KT * c) for m in range(KT)]
    w_units = np.stack(units)
    assert w_units.shape[0] == UNITS

    tokens = np.concatenate([np.asarray(meta_tokens), np.asarray(x)[0]], 0)
    x_t = np.ascontiguousarray(tokens.T.reshape(KT, P, T1).transpose(1, 0, 2)).reshape(P, KT * T1)

    def feats(a):
        return np.asarray(a).reshape(-1, P).T

    def top(a):
        t = np.zeros((P, 1), np.float32)
        t[:len(a), 0] = a
        return t

    def pairs(a):
        return np.asarray(a).reshape(PAIRS, P).T

    parts = {
        "g_mix_pre": feats(g_mix_pre[0]), "g_mix_post": feats(g_mix_post[0]), "g_ffn_pre": feats(g_ffn_pre[0]),
        "g_ffn_post": feats(g_ffn_post[0]), "b_qk": feats(b_qk_conv[0]),
        "w_qk": np.concatenate([feats(w_qk_conv[0][k]) for k in range(4)], 1),
        "g_head": feats(g_head_norm[0]), "ssm_d": feats(ssm_d[0]), "attn_norm": feats(attn_norm_2[0]),
        "mlp_norm": feats(mlp_norm_2[0]), "out_gain": feats(out_gain_2[0]), "q_gain": feats(q_gain_2[0]),
        "k_gain": feats(k_gain_2[0]),
        "ffn_conv": np.stack([feats(w_ffn_conv[0][k]) for k in range(3)] + [feats(b_ffn_conv[0])], 2).reshape(P, -1),
        "lam_re": pairs(ssm_lambda_re[0]), "lam_im": pairs(ssm_lambda_im[0]),
        "log_dt": pairs(np.repeat(np.asarray(ssm_log_dt)[0][:, None], SSM_STATE, 1)),
        "b_i": top(np.asarray(b_gates)[0][:HEADS1]), "b_f": top(np.asarray(b_gates)[0][HEADS1:]),
        "b_forget": top(np.asarray(b_forget_2)[0]),
    }
    cols = np.concatenate([parts[name] for name, _ in _COLS], 1).astype(np.float32)

    p, f = np.arange(P)[:, None], np.arange(P)[None, :]
    consts = np.concatenate([p == f, np.ones((P, P)), p // HD == f // HD, np.where(p > f, NEG, 0.0),
                             np.where(f > p, NEG, 0.0)], 1).astype(np.float32)
    sel = np.zeros((36, HEADS1, P), np.float32)
    for h in range(HEADS1):
        sel[h, h] = sel[32 + h, h] = 1.0
    n_alibi = HEADS2 - N_FOX
    slopes = np.exp2(-8.0 * np.arange(1, n_alibi + 1, dtype=np.float32) / n_alibi).astype(np.float32)
    alibi = np.zeros((HEADS2, SEQ), np.float32)
    n_dil = n_alibi - N_MOBA
    for h in range(N_MOBA):
        alibi[h] = slopes[n_dil + h] * np.arange(SEQ, dtype=np.float32)
    for h in range(n_dil):
        alibi[N_MOBA + N_FOX + h] = slopes[h] * np.arange(SEQ, dtype=np.float32)
    d = p + 3 * P - np.arange(SEQ)[None, :]
    count = (d >= 0) * ((d <= 128) * 1 + ((d % 4 == 0) & (d <= 512)) + ((d % 16 == 0) & (d <= 2048)))
    dil = np.concatenate([np.where(count > 0, 0.0, NEG), count], 1).astype(np.float32)

    def diagonal(re, im):
        t = np.zeros((2, SSM_STATE, 2, PAIRS, 2, SSM_GROUP), np.float32)
        for k, a in enumerate((re, im)):
            for g in range(2):
                t[g, :, k, :, g, :] = a.reshape(PAIRS, 2, SSM_STATE, SSM_GROUP)[:, g].transpose(1, 0, 2)
        return t.reshape(P, -1)

    ssm_b = diagonal(np.asarray(ssm_b_re)[0], np.asarray(ssm_b_im)[0])
    ssm_c = diagonal(*(np.ascontiguousarray(np.asarray(a)[0].transpose(0, 2, 1)) for a in (ssm_c_re, ssm_c_im)))

    arrays = {"w_units": w_units, "x_t": x_t, "cols": cols, "consts": consts, "sel": sel.reshape(36, -1),
              "ssm_b": ssm_b, "ssm_c": ssm_c, "alibi": alibi, "dil": dil}
    nc = bacc.Bacc("TRN2", target_bir_lowering=False, num_devices=1)
    aps = [nc.dram_tensor(name, a.shape, mybir.dt.float32, kind="ExternalInput").ap() for name, a in arrays.items()]
    out = nc.dram_tensor("out", (P, KT * SEQ), mybir.dt.float32, kind="ExternalOutput").ap()
    build(nc, *aps, out)
    r = run_bass_kernel_spmd(nc, [{name: np.ascontiguousarray(a) for name, a in arrays.items()}], core_ids=[0])
    res = np.asarray(r.results[0]["out"]).reshape(P, KT, SEQ)
    return res.transpose(2, 1, 0).reshape(1, SEQ, D_MODEL)
```

```python
import math
from contextlib import contextmanager

import concourse.bass as bass
import numpy as np
from concourse import mybir

P = 128
D_MODEL = 1024
KT = D_MODEL // P
SEQ, META = 512, 16
T1 = SEQ + META
HALF = T1 // 2
SSM_W, SSM_GROUP, SSM_STATE = 512, 16, 64
PAIRS = SSM_W // SSM_GROUP // 2
CT = SSM_W // P
STEP = 4
CHUNKS = T1 // STEP
SEG = CHUNKS // 2
HEADS1 = 4
FFN_TILES = 2816 // P
HEADS2, HD = 16, 64
N_MOBA, N_FOX = 4, 6
EPS = 1e-6
NEG = -1e30
LOOK = 2
RING = 4
PRE, POST = (0, 2, 4, 5), (1, 3)
OWN_SCALED = 2
GROUPS = ((0, 256), (256, 640), (640, 1024))
FOX_TILES = (2, 3, 4)
E_AFTER, Y_AFTER = (7, 9, 11, 13), (10, 12, 14, 15)
BANK_DONE = (3, 2, 3, 4)
VT_BANK = (6, 6, 4, 6)

U_U, U_GATES, U_Q, U_K, U_V, U_O, U_GA = 0, 4, 5, 9, 13, 17, 21
U_GLU = U_GA + 16
U_MERGE = U_GLU + 2
U_OUT = U_MERGE + KT
U_FFN = U_OUT + KT
FFN_CHUNKS = (8, 8, 6)
U_V2 = U_FFN + 2 * FFN_TILES + 3 * KT
U_F2 = U_V2 + KT
U_QK2 = U_F2 + 1
U_GFOX = U_QK2 + 2 * KT
U_OUT2 = U_GFOX + 3
U_MLP = U_OUT2 + KT
MLP_CHUNKS = 4
UNITS = U_MLP + MLP_CHUNKS * 2 * KT

_COLS = [("g_mix_pre", 8), ("g_mix_post", 8), ("g_ffn_pre", 8), ("g_ffn_post", 8), ("b_qk", 8), ("w_qk", 32),
         ("g_head", 4), ("ssm_d", 4), ("attn_norm", 8), ("mlp_norm", 8), ("out_gain", 8), ("q_gain", 8),
         ("k_gain", 8), ("ffn_conv", 4 * FFN_TILES), ("lam_re", PAIRS), ("lam_im", PAIRS), ("log_dt", PAIRS),
         ("b_i", 1), ("b_f", 1), ("b_forget", 1)]
COL, _at = {}, 0
for _name, _n in _COLS:
    COL[_name] = _at
    _at += _n
N_COLS = _at


class Order:

    def __init__(self, eng, steps):
        self.eng, self.steps, self.n, self.shift, self.last = eng, steps, {}, {}, None

    def value(self, sem):
        v = self.n.get(sem.name, 0)
        for x in self.shift.get(sem.name, []):
            v = x + v
        return v

    def do(self, ins, sem=None):
        sem = sem or self.steps
        ins.then_inc(sem, 1)
        self.n[sem.name] = self.n.get(sem.name, 0) + 1
        self.last = (sem, self.value(sem))

    def fence(self):
        if self.last is not None:
            self.eng.wait_ge(*self.last)

    @contextmanager
    def loop(self, trips, per_trip):
        before = dict(self.n)
        with self.eng.Fori(0, trips) as i:
            for sem, k in per_trip.items():
                self.shift.setdefault(sem.name, []).append(i * k)
            self.last = None
            yield i
        for sem, k in per_trip.items():
            got = self.n.get(sem.name, 0) - before.get(sem.name, 0)
            assert got == k, (sem.name, got, k)
            self.n[sem.name] = before.get(sem.name, 0) + trips * k
            self.shift[sem.name].pop()
        for name in self.n:
            assert name in {s.name for s in per_trip} or self.n[name] == before.get(name, 0), name
        if self.last is not None:
            self.last = (self.last[0], self.value(self.last[0]))


def build(nc, w_units, x_t, cols_in, consts_in, sel_in, ssm_b_in, ssm_c_in, alibi_in, dil_in, out):
    fp32, f32r = mybir.dt.float32, mybir.dt.float32r
    ALU, ACT, AX = mybir.AluOpType, mybir.ActivationFunctionType, mybir.AxisListType

    place = [(nc.sbuf_base + 31) // 32 * 32]

    def fixed(name, shape, dt=fp32):
        t = nc.alloc_sbuf_tensor_at(name, [P] + shape, dt, offset=place[0])
        place[0] += (4 * math.prod(shape) + 31) // 32 * 32
        return t

    def region(size):
        at = place[0]
        place[0] += size
        return at

    def at(name, shape, where, dt=fp32):
        return nc.alloc_sbuf_tensor_at(name, [P] + shape, dt, offset=where)

    raw = fixed("w_raw", [RING, 1024])
    whi = fixed("w_hi", [RING, 1024], f32r)
    wlo = fixed("w_lo", [RING, 1024], f32r)
    tile528 = KT * T1 * 4
    Zx = region(tile528)
    hhi = fixed("h_hi", [KT, T1], f32r)
    hlo = fixed("h_lo", [KT, T1], f32r)
    Z2 = region(tile528)
    sq = [fixed(f"sq{j}", [T1]) for j in range(2)]
    acc = fixed("acc", [T1])
    rs = fixed("rs", [T1])
    consts = fixed("consts", [5, P])
    ident, ones, blk64, mask_st, mask_qk = (consts[:, j, :] for j in range(5))
    sel = fixed("sel", [4, P])
    cols = fixed("cols", [N_COLS])
    small = fixed("small", [500])
    rows = fixed("rows", [T1])
    Zu = region(4 * T1 * 4)
    Zv = region(5 * 512 * 4)
    R = region(16 * T1 * 4 + 3 * 4 * T1 * 4)
    assert place[0] <= nc.sbuf_usable_end, (place[0], nc.sbuf_usable_end)

    x = at("x", [KT, T1], Zx)
    qk = at("qk", [2 * HEADS1, T1], Zx)
    qp = [at(f"qp{j}", [T1 + 3], Z2 + 2144 * j) for j in range(2)]
    vT = [at(f"vT{j}", [T1], Z2 + 4288 + 2112 * j) for j in range(2)]
    b_t = [at(f"b_tmp{j}", [PAIRS * 32], Z2 + 2048 * j) for j in range(4)]
    b_raw = at("b_raw", [2, PAIRS * 32], Z2 + 8512)
    kblk = at("k_blk", [CT, 4, P], Z2 + 8512)
    ybhi = at("yb_hi", [HEADS1, T1], Z2, f32r)
    yblo = at("yb_lo", [HEADS1, T1], Z2 + 4 * T1 * 4, f32r)
    ysum = at("y_sum", [KT, T1], Z2)
    u = at("u", [CT, 4, CHUNKS], Zu)
    ya = at("y_a", [CT, T1], Zu)
    Wm = at("w_mlstm", [1360], Zu)
    num = at("num", [T1], Zu + 5440)
    b_pow = [at("b_pow0", [2, PAIRS * 32], Zv), at("b_pow1", [2, PAIRS * 32], Zv + 4096),
             at("b_pow2", [2, PAIRS * 32], Z2 + 12608), at("b_pow3", [2, PAIRS * 32], Z2 + 8512)]
    vs = at("v_tok", [5, 512], Zv)
    eye32 = at("eye32", [32], Zv + 8192)
    dmat = at("d_diag", [CT, 32], Zv + 8320)
    c_pow = at("c_pow", [2, PAIRS, STEP + 1, 32], R)
    bT = at("b_T", [2, CT, 4, P], R + 20480)
    ph = at("phase", [2, PAIRS, SEG], R + 36864)
    rot = [at(f"rot{j}", [4, SEG], R + 45312 + 1056 * j) for j in range(4)]
    xst = [at(f"x_state{j}", [2, 4, CHUNKS + 1], R + 49536 + 4256 * j) for j in range(2)]
    c_t = [at(f"c_tmp{j}", [PAIRS * 32], R + 49536 + 2048 * j) for j in range(4)]
    G = at("gates", [2 * KT, T1], R)
    og = at("o_gate", [HEADS1, T1], R + 16 * T1 * 4)
    yahi = at("ya_hi", [CT, T1], R + 20 * T1 * 4, f32r)
    yalo = at("ya_lo", [CT, T1], R + 24 * T1 * 4, f32r)
    fahi = at("ffn_hi", [KT, SEQ], R, f32r)
    falo = at("ffn_lo", [KT, SEQ], R + 16384, f32r)
    gp = [at(f"gate_pad{j}", [T1 + 2], R + 32768 + 2144 * j) for j in range(2)]
    cg = [at(f"gate_conv{j}", [SEQ], R + 37056 + 2048 * j) for j in range(2)]
    tup = [at(f"up{j}", [SEQ], R + 41152 + 2048 * j) for j in range(2)]
    ctmp = at("conv_tmp", [SEQ], R + 45312)
    V = at("v2_tok", [4, D_MODEL], R)
    sgf = at("fox_gate", [3, SEQ], R + 16384)
    qa = [at(f"q_aug{j}", [2, SEQ], R + 22528 + 8192 * j) for j in range(2)]
    ka = [at(f"k_aug{j}", [2, SEQ], R + 22528 + 4096 + 8192 * j) for j in range(2)]
    qr = [at(f"qk_raw{j}", [SEQ], R + 38912 + 2048 * j) for j in range(2)]
    Pb = [at(f"probs{j}", [3, SEQ], R + 43008 + 6144 * j) for j in range(2)]
    vT2 = [at(f"v2T{j}", [SEQ], R + 43008 + 2048 * j) for j in range(2)]
    qtmp = at("qk_tmp", [SEQ], R + 55296)
    yq = at("attn_out", [4, D_MODEL], Z2)
    dil = at("dil", [2, SEQ], Zu)
    fox = [at(f"fox{j}", [SEQ], Zu + 4096 + 2048 * j) for j in range(2)]
    identr = at("ident_r", [P], Zv, f32r)
    maskr = at("mask_qk_r", [P], Zv + 512, f32r)
    dilr = at("dil_mask_r", [SEQ], Zv + 1024, f32r)
    mahi = at("mlp_hi", [KT, SEQ], R, f32r)
    malo = at("mlp_lo", [KT, SEQ], R + 16384, f32r)
    rl = [at(f"relu{j}", [SEQ], R + 32768 + 2048 * j) for j in range(2)]
    r2 = [at(f"relu_sq{j}", [SEQ], R + 36864 + 2048 * j) for j in range(2)]
    ot = [at(f"out_tile{j}", [SEQ], R + 40960 + 2048 * j) for j in range(2)]

    PS = nc.alloc_psum_tensor("ps", [P, 8, 512], fp32)

    sems = {}

    def sem(name):
        if name not in sems:
            sems[name] = nc.alloc_semaphore(name)
        return sems[name]

    raw_in = [sem(f"raw_in{j}") for j in range(RING)]
    hi_ready, lo_ready = sem("hi_ready"), sem("lo_ready")
    unit_done, evacuated = sem("unit_done"), sem("evacuated")
    act_steps, dve_steps, pool_steps = sem("act_steps"), sem("dve_steps"), sem("pool_steps")

    SLOTS = ("t", "f", "s", "c", "e1", "e2", "th", "k", "ca", "rho", "dt", "phi", "cm1", "sphi", "den", "em1", "cphi",
             "r", "nr", "ni", "r2", "p2r", "p2i", "ar", "r4", "zr", "zi", "p4r", "p4i")

    def sm(name):
        j = PAIRS * SLOTS.index("ni" if name == "ai" else name)
        return small[:, j:j + PAIRS]

    r2c = small[:, 0:20]
    nm, rsum, rinv = (small[:, 32 + 8 * j:40 + 8 * j] for j in range(3))
    gms, gy, gtmp = (small[:, 64 + 16 * j:76 + 16 * j] for j in range(3))

    def col(name, j=0, n=1, p0=0, p1=P):
        return cols[p0:p1, COL[name] + j:COL[name] + j + n]

    def pair(slot):
        return PS[:, 2 * slot:2 * slot + 2, 0:HALF]

    def two(t):
        return t.rearrange("p (a b) -> p a b", a=2)

    def f32(t):
        return t.bitcast(fp32)

    S_OFF = [0, 528, 928, 1200, 1344]
    S_LEN = [T1 - P * j for j in range(5)]
    QB = [(0, 0), (2, 0), (0, 128), (1, 0)]

    block = nc.Block()
    with block as block:

        @block.sync
        def _(sp):
            sp.dma_start(cols[:, :], cols_in).then_inc(sem("cols_in"), 16)
            sp.dma_start(consts[:, :, :], consts_in.rearrange("p (a b) -> p a b", a=5)).then_inc(sem("consts_in"), 16)
            for n in range(RING):
                sp.dma_start(raw[:, n, :], w_units[n]).then_inc(raw_in[n], 16)

            def load(s, r, j):
                sp.wait_ge(lo_ready, r + (s - RING + 1))
                sp.dma_start(raw[:, j, :], w_units[bass.ds(r + s, 1), :, :].rearrange("a p c -> p (a c)")
                             if not isinstance(r, int) else w_units[r + s]).then_inc(raw_in[j], 16)

            trips = (UNITS - RING) // RING
            with sp.Fori(0, trips) as i:
                for j in range(RING):
                    load(RING + j, i * RING, j)
            for n in range(RING + trips * RING, UNITS):
                load(n, 0, n % RING)
            for m in range(KT):
                sp.wait_ge(sem("out_ready"), m + 1)
                sp.dma_start(out[:, m * SEQ:(m + 1) * SEQ], ot[m % 2][:, :]).then_inc(sem(f"out_done{m % 2}"), 16)
            for j in range(2):
                sp.wait_ge(sem(f"out_done{j}"), 16 * KT // 2)

        @block.scalar
        def _(act):
            A = Order(act, act_steps)
            dn = nc.scalar

            def split_hi(s, r=0):
                if isinstance(r, int) and s + r >= UNITS:
                    return
                act.wait_ge(raw_in[s % RING], r * 4 + 16 * (s // RING + 1))
                if s >= RING:
                    act.wait_ge(unit_done, r + (s - RING + 1))
                A.do(dn.activation(whi[:, s % RING, :], raw[:, s % RING, :], ACT.Copy), hi_ready)

            def squares(norm, src, first_wait):
                for m in range(KT):
                    first_wait(m)
                    if m == 0:
                        act.wait_ge(sem("rs_ready"), norm)
                        A.do(dn.activation(acc[:, 0:src(0).shape[-1]], src(0), ACT.Square), sem("sq_ready"))
                    else:
                        if m >= 3:
                            act.wait_ge(sem("sq_added"), 6 * POST.index(norm) + m - 2)
                        A.do(dn.activation(sq[m % 2][:, 0:src(m).shape[-1]], src(m), ACT.Square), sem("sq_ready"))

            def tile_square(norm, m, src):
                if m == 0 and norm:
                    act.wait_ge(sem("rs_ready"), norm)
                if m >= 2:
                    act.wait_ge(sem("tile_summed"), (KT - 1) * PRE.index(norm) + m - 1)
                A.do(dn.activation(sq[m % 2][:, 0:src.shape[-1]], src, ACT.Square), sem("tile_sq"))

            def rsqrt(norm, n):
                act.wait_ge(sem("ms_ready"), norm + 1)
                A.do(dn.activation(acc[:, 0:n], rs[:, 0:n], ACT.Abs_reciprocal_sqrt), sem("rsqrt_ready"))

            tiny_col = small[:, 491:492]

            for j in range(4):
                act.dma_start(x[:, 2 * j:2 * j + 2, :],
                              x_t[:, 2 * j * T1:(2 * j + 2) * T1].rearrange("p (a b) -> p a b", a=2)
                              ).then_inc(sem(f"x_in{j}"), 16)
            act.dma_start(b_raw[:, :, :], ssm_b_in.rearrange("p (a b) -> p a b", a=2)).then_inc(sem("ssm_b_in"), 16)
            act.dma_start(c_pow[:, :, :, 0, :], ssm_c_in.rearrange("p (a b c) -> p a b c", a=2, c=32)).then_inc(sem("ssm_c_in"), 16)
            act.dma_start(sel[0:36, :, :], sel_in.rearrange("p (a b) -> p a b", a=4)).then_inc(sem("sel_in"), 16)

            act.wait_ge(sem("cols_in"), 16)
            A.do(dn.activation(sm("t"), col("log_dt", 0, PAIRS), ACT.Tanh, scale=1.0 / 16), sem("lam_act"))

            def phase_functions():
                act.wait_ge(sem("lam_dve"), 1)
                A.do(dn.activation(sm("s"), sm("f"), ACT.Sin, scale=0.5))
                A.do(dn.activation(sm("c"), sm("ca"), ACT.Sin))
                A.do(dn.activation(sm("th"), sm("rho"), ACT.Tanh, scale=0.5), sem("lam_act"))

            act.wait_ge(sem("eps_set"), 1)
            for m in range(KT):
                act.wait_ge(sem(f"x_in{m // 2}"), 16)
                A.do(dn.activation(hhi[:, m, :], x[:, m, :], ACT.Identity, scale=col("g_mix_pre", m)), sem("h1_hi"))
                tile_square(0, m, x[:, m, :])
                if m == 0:
                    split_hi(0)
                if m == 1:
                    phase_functions()
                if m == 3:
                    split_hi(1)

            def gate_rows():
                act.wait_ge(evacuated, U_GATES + 1)
                A.do(dn.activation(acc[0:4, :], acc[0:4, :], ACT.Identity, bias=col("b_f", 0, 1, 0, 4)), sem("gate_z"))
                act.wait_ge(sem("gate_abs"), 1)
                A.do(dn.activation(sq[1][0:4, :], sq[1][0:4, :], ACT.Exp))
                A.fence()
                A.do(dn.activation(sq[1][0:4, :], sq[1][0:4, :], ACT.Ln, bias=1.0), sem("gate_ln"))

            def chunk_tokens(t):
                act.wait_ge(evacuated, t + 1)
                for g in range(4):
                    for s in range(STEP):
                        A.do(dn.activation(u[32 * s:32 * s + 32, t, g, :], sq[t % 2][32 * g:32 * g + 32, s:T1:STEP], ACT.Copy),
                             sem("u_ready") if g == 3 and s == STEP - 1 else None)

            def conv_taps(m):
                act.wait_ge(evacuated, U_Q + m + 1)
                if m == 0:
                    act.wait_ge(sem("h1_lo"), KT)
                else:
                    act.wait_ge(sem("tap_added"), 3 * m)
                for k in range(4):
                    src = qp[m % 2][:, k:k + T1]
                    if k == 0:
                        A.do(dn.activation(qk[:, m, :], src, ACT.Identity, bias=col("b_qk", m), scale=col("w_qk", m)))
                    else:
                        if k == 3:
                            act.wait_ge(sem("tap_added"), 3 * m + 1)
                        A.do(dn.activation(vT[k % 2][:, :], src, ACT.Identity, scale=col("w_qk", 8 * k + m)), sem("tap_ready"))

            def mlstm_weights(h):
                act.wait_ge(sem("bc_mm"), h + 1)
                if h:
                    act.wait_ge(sem("ss_mm"), h)
                    act.wait_ge(sem("den_used"), h)
                A.do(dn.activation(two(sq[0][:, :]), PS[:, 4:6, 0:HALF], ACT.Copy))
                A.do(dn.activation(two(sq[1][:, :]), PS[:, 6:8, 0:HALF], ACT.Exp, scale=-2.0), sem("bc_done"))
                act.wait_ge(sem("r2c_ready"), 1)
                if h == 0:
                    act.wait_ge(sem("ya_lo"), CT)
                if h:
                    act.wait_ge(sem("nd_mm"), h)
                A.fence()
                for j in range(4):
                    A.do(dn.activation(Wm[:, S_OFF[j] + P:S_OFF[j] + S_LEN[j]], sq[0][:, P * (j + 1):T1], ACT.Exp,
                                       bias=r2c[:, 4 * j + h:4 * j + h + 1]))
                act.wait_ge(sem("diag_done"), 5 * (h + 1))
                for j in range(5):
                    k = min(P, S_LEN[j])
                    d = Wm[0:k, S_OFF[j]:S_OFF[j] + k]
                    A.do(dn.activation(d, d, ACT.Exp, bias=r2c[0:k, 4 * j + h:4 * j + h + 1]),
                         sem("w_ready") if j == 4 else None)

            def mlstm_num(h):
                act.wait_ge(sem("nd_mm"), h + 1)
                if h:
                    act.wait_ge(sem("yb_lo"), h)
                A.do(dn.activation(two(acc[:, :]), PS[:, 6:8, 0:HALF], ACT.Square), sem("densq_ready"))
                A.do(dn.activation(two(num[:, :]), PS[:, 4:6, 0:HALF], ACT.Copy))
                A.do(dn.activation(two(sq[0][:, :]), PS[:, 4:6, 0:HALF], ACT.Square), sem("numsq_ready"))

            def mlstm_out(h):
                act.wait_ge(sem("z_ready"), h + 1)
                A.do(dn.activation(acc[:, :], acc[:, :], ACT.Sqrt, bias=tiny_col, scale=1.0 / P), sem("sd_ready"))
                act.wait_ge(sem("yb_pre"), h + 1)
                A.do(dn.activation(ybhi[:, h, :], num[:, :], ACT.Copy), sem("yb_hi"))

            for n in range(U_GLU):
                split_hi(n + LOOK)
                if n == 0:
                    rsqrt(0, T1)
                if n < U_GATES:
                    chunk_tokens(n)
                if n == U_GATES:
                    gate_rows()
                if n in (4, 5):
                    for s in range(STEP):
                        act.wait_ge(sem("bt_mm"), (n - 4) * STEP + s + 1)
                        if n == 4 and s == 0:
                            act.wait_ge(sem("lam_dve"), 2)
                        q = slice(32 * (STEP - 1 - s), 32 * (STEP - s))
                        for g in range(4):
                            A.do(dn.activation(bT[q, n - 4, :, g, :],
                                               PS[32 * g:32 * g + 32, 4 + s, :].rearrange("p (a b) -> p a b", a=CT),
                                               ACT.Copy), sem("bt_copied") if g == 3 else None)
                if U_Q <= n < U_V:
                    conv_taps(n - U_Q)
                if U_Q < n <= U_V:
                    m = n - 1 - U_Q
                    act.wait_ge(sem("tap_added"), 3 * (m + 1))
                    A.do(dn.activation(qk[:, m, :], qk[:, m, :], ACT.Silu), sem("qk_ready"))
                if n == 6:
                    act.wait_ge(sem("r2_mm"), 1)
                    A.do(dn.activation(r2c[:, 0:16], PS[:, 4, 0:16], ACT.Copy))
                    A.do(dn.activation(r2c[0:16, 16:20], PS[0:16, 4, 16:20], ACT.Copy), sem("r2c_ready"))
                if n == 8:
                    act.wait_ge(sem("kz"), 1)
                    act.wait_ge(sem("k_mm"), 1)
                    for s in range(STEP):
                        for g in range(4):
                            k = 32 * (STEP - s)
                            A.do(dn.activation(kblk[32 * s:32 * s + 32, :, g, 32 * s:P],
                                               PS[32 * g:32 * g + 32, 4, :].rearrange("p (a b) -> p a b", a=CT)[:, :, 0:k],
                                               ACT.Copy), sem("k_ready") if g == 3 else None)
                if n in Y_AFTER:
                    t = Y_AFTER.index(n)
                    act.wait_ge(sem("y_mm"), t + 1)
                    for g in range(4):
                        for s in range(STEP):
                            c0 = CHUNKS * (g % 2)
                            A.do(dn.activation(ya[32 * g:32 * g + 32, t, s:T1:STEP],
                                               PS[32 * s:32 * s + 32, 4 + g // 2, c0:c0 + CHUNKS], ACT.Gelu_apprx_tanh),
                                 sem("ya_ready") if g == 3 and s == STEP - 1 else None)
                if U_V + 1 <= n < U_V + 5:
                    j = n - U_V - 1
                    b = VT_BANK[j]
                    act.wait_ge(sem("vt_mm"), j + 1)
                    act.wait_ge(sem("vz"), 1)
                    A.do(dn.activation(vs[:, 0:4, P * j:P * j + P], PS[:, b, :].rearrange("p (a b) -> p a b", a=4), ACT.Copy))
                    A.do(dn.activation(vs[0:16, 4, P * j:P * j + P], PS[0:16, b + 1, 0:P], ACT.Copy), sem("vs_ready"))
                if U_O <= n < U_GA:
                    j = n - U_O
                    act.wait_ge(evacuated, n + 1)
                    A.do(dn.activation(og[:, j, :], og[:, j, :], ACT.Sigmoid), sem("og_ready"))
                    act.wait_ge(sem("ya_ready"), 4)
                    act.wait_ge(sem("y_mm"), 4)
                    A.do(dn.activation(yahi[:, j, :], ya[:, j, :], ACT.Copy), sem("ya_hi"))
                if n >= U_GA - 1:
                    h, k = divmod(n - (U_GA - 1), 4)
                    if n >= U_GA:
                        act.wait_ge(evacuated, n + 1)
                        A.do(dn.activation(G[:, n - U_GA, :], G[:, n - U_GA, :], ACT.Sigmoid), sem("g_ready"))
                    if h < HEADS1:
                        (mlstm_weights, lambda h: None, mlstm_num, mlstm_out)[k](h)

            for n in range(U_GLU, U_MERGE):
                split_hi(n + LOOK)
            act.wait_ge(unit_done, U_MERGE)
            for m in range(CT):
                s = (U_GLU + m // 2) % 2
                view = pair(s) if m % 2 == 0 else PS[:, 4 + 2 * s:6 + 2 * s, 0:HALF]
                if m >= 2:
                    act.wait_ge(sem("ya2_pre"), m - 1)
                A.do(dn.activation(two(sq[m % 2][:, :]), view, ACT.Sigmoid), evacuated if m % 2 else sem("glu_sg"))
            for m in range(CT):
                act.wait_ge(sem("ya2_pre"), m + 1)
                A.do(dn.activation(yahi[:, m, :], ya[:, m, :], ACT.Copy), sem("ya2_hi"))

            act.wait_ge(sem("s_mm"), HEADS1)
            act.dma_start(x[:, :, :], x_t.rearrange("p (a b) -> p a b", a=KT)).then_inc(sem("x_again"), 16)
            with A.loop(2, {hi_ready: 4, sem("mg_hi"): 4}) as i:
                for j in range(4):
                    split_hi(U_MERGE + j + LOOK, i * 4)
                    act.wait_ge(sem("mg_pre"), i * 4 + (j + 1))
                    A.do(dn.activation(hhi[:, bass.ds(i * 4 + j, 1), :].rearrange("p a b -> p (a b)"),
                                       sq[j % 2][:, :], ACT.Copy), sem("mg_hi"))
            A.do(dn.activation(small[:, 481:482], small[:, 490:491], ACT.Abs_reciprocal_sqrt))
            with A.loop(2, {hi_ready: 4}) as i:
                for j in range(4):
                    split_hi(U_OUT + j + LOOK, i * 4)
            squares(1, lambda m: ysum[:, m, :], lambda m: act.wait_ge(evacuated, U_OUT + m + 1))
            rsqrt(1, T1)
            for m in range(KT):
                act.wait_ge(sem("x1_ready"), m + 1)
                A.do(dn.activation(hhi[:, m, :], x[:, m, :], ACT.Identity, scale=col("g_ffn_pre", m)), sem("h2_hi"))
                tile_square(2, m, x[:, m, :])

            def ffn_hi(f, rf, fl, rfl):
                act.wait_ge(sem("fa_pre"), rf + (f + 1))
                dst = fahi[:, fl, :] if isinstance(rfl, int) else fahi[:, bass.ds(rfl + fl, 1), :].rearrange("p a b -> p (a b)")
                A.do(dn.activation(dst, tup[f % 2][:, :], ACT.Copy), sem("fa_hi"))

            def ffn_pair(s, r, f, rf, fl, rfl):
                split_hi(s + LOOK, r)
                if f == 0:
                    rsqrt(2, T1)
                if fl:
                    ffn_hi(f - 1, rf, fl - 1, rfl)
                split_hi(s + 1 + LOOK, r)
                act.wait_ge(sem("conv2_ready"), rf + (f + 1))
                A.do(dn.activation(cg[f % 2][:, :], cg[f % 2][:, :], ACT.Gelu_apprx_tanh), sem("gl_ready"))

            s0, f0 = U_FFN, 0
            for tiles in FFN_CHUNKS:
                for q in range(2):
                    ffn_pair(s0 + 2 * q, 0, f0 + q, 0, q, 0)
                with A.loop(tiles // 2 - 1, {hi_ready: 4, sem("gl_ready"): 2, sem("fa_hi"): 2}) as i:
                    for q in range(2, 4):
                        ffn_pair(s0 + 2 * q, i * 4, f0 + q, i * 2, q, i * 2)
                s0 += 2 * tiles
                f0 += tiles
                ffn_hi(f0 - 1, 0, tiles - 1, 0)
                if f0 == FFN_TILES:
                    A.fence()
                    A.do(dn.activation(small[:, 481:482], small[:, 490:491], ACT.Abs_reciprocal_sqrt))
                with A.loop(2, {hi_ready: 4}) as i:
                    for j in range(4):
                        split_hi(s0 + j + LOOK, i * 4)
                s0 += KT
            assert s0 == U_V2
            squares(3, lambda m: ysum[:, m, 0:SEQ], lambda m: act.wait_ge(evacuated, U_V2 - KT + m + 1))
            rsqrt(3, SEQ)
            for m in range(KT):
                act.wait_ge(sem("x2_ready"), m + 1)
                A.do(dn.activation(hhi[:, m, 0:SEQ], x[:, m, META:T1], ACT.Identity, scale=col("attn_norm", m)), sem("h3_hi"))
                tile_square(4, m, x[:, m, META:T1])

            def v2_copy(j, r):
                act.wait_ge(sem("v2t_mm"), r + (j + 1))
                A.do(dn.activation(V[:, :, bass.ds((r + j) * P, P)],
                                   PS[:, 2 + j % 2, :].rearrange("p (a b) -> p a b", a=4), ACT.Copy), sem("v2_ready"))

            split_hi(U_V2 + LOOK)
            rsqrt(4, SEQ)
            for n in range(U_V2 + 1, U_V2 + KT):
                split_hi(n + LOOK)
                v2_copy(n - 1 - U_V2, 0)
            A.do(dn.activation(identr[:, :], ident, ACT.Copy), sem("masks_ready"))
            A.do(dn.activation(maskr[:, :], mask_qk, ACT.Copy), sem("masks_ready"))
            act.wait_ge(sem("dil_in"), 16)
            A.do(dn.activation(dilr[:, :], dil[:, 0, :], ACT.Copy), sem("masks_ready"))
            split_hi(U_F2 + LOOK)
            v2_copy(KT - 1, 0)
            act.wait_ge(evacuated, U_F2 + 1)
            A.do(dn.activation(fox[0][0:N_FOX, :], fox[0][0:N_FOX, :], ACT.Identity,
                               bias=col("b_forget", 0, 1, 0, N_FOX)), sem("fox_z"))
            act.wait_ge(sem("fox_abs"), 1)
            A.do(dn.activation(fox[1][0:N_FOX, :], fox[1][0:N_FOX, :], ACT.Exp))
            A.fence()
            A.do(dn.activation(fox[1][0:N_FOX, :], fox[1][0:N_FOX, :], ACT.Ln, bias=1.0), sem("fox_ln"))

            def qk_square(i, w):
                act.wait_ge(evacuated, U_QK2 + 2 * i + w + 1)
                if i:
                    act.wait_ge(sem("aug_ready"), 4 * (i - 1) + 2 * w + 2)
                A.do(dn.activation(sq[w][:, 0:SEQ], qr[w][:, :], ACT.Square), sem("qsq_ready"))

            def qk_rsqrt(i, w):
                act.wait_ge(sem("qms_ready"), 2 * i + w + 1)
                A.do(dn.activation((acc, rows)[w][:, 0:SEQ], sq[w][:, 0:SEQ], ACT.Abs_reciprocal_sqrt), sem("qrs_ready"))

            def exps(i, hh):
                h = 2 * i + hh
                b = 2 + 3 * hh
                if i:
                    act.wait_ge(sem("pv_mm"), h - 1)
                for t in range(4):
                    act.wait_ge(sem("max_ready"), 4 * h + BANK_DONE[t])
                    bank, c = QB[t]
                    w = P * (t + 1)
                    A.do(dn.activation(Pb[hh][:, bank, c:c + w], PS[:, b + bank, c:c + w], ACT.Exp,
                                       bias=nm[:, 4 * hh + t:4 * hh + t + 1],
                                       accum_out=rsum[:, 4 * hh + t:4 * hh + t + 1]), sem("p2_ready"))

            def pt_copy(i, hh):
                h = 2 * i + hh
                b = 2 + 3 * hh
                act.wait_ge(sem("pt_mm"), h + 1)
                A.do(dn.activation(Pb[hh][:, 0:2, :], PS[:, b:b + 2, :], ACT.Copy), sem("pt_act"))

            def group_squares(g):
                a, b = GROUPS[g]
                act.wait_ge(sem("attn_done"), b // HD)
                for t in range(4):
                    A.fence()
                    A.do(dn.activation(fox[1][:, 0:b - a], yq[:, t, a:b], ACT.Square,
                                       accum_out=gms[:, 4 * g + t:4 * g + t + 1]), sem("group_sq"))

            def group_rsqrt(n, g0, g1):
                act.wait_ge(sem("gms_ready"), n)
                A.do(dn.activation(gy[:, 4 * g0:4 * g1], gms[:, 4 * g0:4 * g1], ACT.Abs_reciprocal_sqrt), sem("grs_ready"))

            for i in range(KT + 2):
                if i >= 2:
                    pt_copy(i - 2, 1)
                if i < KT:
                    qk_square(i, 0)
                if 1 <= i <= KT:
                    exps(i - 1, 0)
                split_hi(U_QK2 + 2 * i + LOOK)
                if i < KT:
                    qk_rsqrt(i, 0)
                if i <= KT:
                    split_hi(U_QK2 + 2 * i + 1 + LOOK)
                if i < KT:
                    qk_square(i, 1)
                if i == KT:
                    group_squares(0)
                    group_squares(1)
                    group_rsqrt(2, 0, 2)
                if 1 <= i <= KT:
                    pt_copy(i - 1, 0)
                if i < KT:
                    qk_rsqrt(i, 1)
                if 1 <= i <= KT:
                    exps(i - 1, 1)

            for j in range(3):
                act.wait_ge(evacuated, U_GFOX + j + 1)
                A.do(dn.activation(sgf[:, j, :], sgf[:, j, :], ACT.Sigmoid), sem("sgf_ready"))
            group_squares(2)
            group_rsqrt(3, 2, 3)
            for m in range(KT):
                act.wait_ge(sem("yt_mm"), m + 1)
                if m in FOX_TILES:
                    act.wait_ge(sem("yfox_pre"), m - 1)
                    A.do(dn.activation(hhi[:, m, 0:SEQ], qr[m % 2][:, :], ACT.Copy), sem("y2_hi"))
                else:
                    A.do(dn.activation(hhi[:, m, 0:SEQ], PS[:, 2 + m % 6, :], ACT.Identity, scale=col("out_gain", m)),
                         sem("y2_hi"))
            for m in range(KT):
                split_hi(U_OUT2 + m + LOOK)
            for m in range(KT):
                act.wait_ge(evacuated, U_OUT2 + m + 1)
                if m == 0:
                    act.wait_ge(unit_done, U_MLP)
                A.do(dn.activation(hhi[:, m, 0:SEQ], x[:, m, META:T1], ACT.Identity, scale=col("mlp_norm", m)), sem("h4_hi"))
                tile_square(5, m, x[:, m, META:T1])

            def mlp_up(s, r, f, rf, fl, rfl):
                p = f % 2
                split_hi(s + LOOK, r)
                act.wait_ge(unit_done, r + (s + 1))
                act.wait_ge(evacuated, r + (s - 1))
                A.do(dn.activation(rl[p][:, :], PS[:, s % 2, :], ACT.Relu), sem("relu_ready"))
                act.wait_ge(evacuated, r + (s + 1))
                A.do(dn.activation(mahi[:, bass.ds(rfl + fl, 1), :].rearrange("p a b -> p (a b)")
                                   if not isinstance(rfl, int) else mahi[:, fl, :], r2[p][:, :], ACT.Copy), sem("ma_hi"))

            for f in range(4):
                mlp_up(U_MLP + f, 0, f, 0, f, 0)
                if f == 0:
                    rsqrt(5, SEQ)
            for f in range(4, 8):
                mlp_up(U_MLP + f, 0, f, 0, f, 0)
            for j in range(KT):
                split_hi(U_MLP + KT + j + LOOK)
            with A.loop(2, {hi_ready: 16, sem("relu_ready"): 8, sem("ma_hi"): 8}) as c:
                for f in range(KT):
                    mlp_up(U_MLP + 2 * KT + f, c * 16, KT + f, c * 8, f, 0)
                for j in range(KT):
                    split_hi(U_MLP + 3 * KT + j + LOOK, c * 16)
            for f in range(KT):
                mlp_up(U_MLP + 6 * KT + f, 0, 3 * KT + f, 0, f, 0)
            for j in range(KT):
                split_hi(U_MLP + 7 * KT + j + LOOK)

        @block.vector
        def _(dve):
            Dv = Order(dve, dve_steps)
            v = nc.vector
            M, A_, S_ = ALU.mult, ALU.add, ALU.subtract

            def split_lo(s, r=0):
                if isinstance(r, int) and s + r >= UNITS:
                    return
                dve.wait_ge(hi_ready, r + (s + 1))
                Dv.do(v.tensor_tensor(wlo[:, s % RING, :], raw[:, s % RING, :], f32(whi[:, s % RING, :]), ALU.subtract), lo_ready)

            def tt(o, a, b, op, s=None):
                Dv.do(v.tensor_tensor(o, a, b, op), s)

            def ts(o, a, s1, s2, op0, op1=None, s=None):
                if op1 is None:
                    Dv.do(v.tensor_scalar(o, a, s1, None, op0), s)
                else:
                    Dv.do(v.tensor_scalar(o, a, s1, s2, op0, op1), s)

            def stt(o, a, sc, b, op0, op1, s=None):
                Dv.do(v.scalar_tensor_tensor(out=o, in0=a, scalar=sc, in1=b, op0=op0, op1=op1), s)

            def rstd(norm, n):
                shape = (lambda t: two(t[:, :])) if n == T1 else (lambda t: t[:, 0:SEQ])
                sums = PS[:, 4:6, 0:HALF] if n == T1 else PS[:, 4, :]
                dve.wait_ge(sem("stat_mm"), norm + 1)
                Dv.fence()
                ts(shape(rs), sums, 1.0 / D_MODEL, EPS, M, A_, sem("ms_ready"))
                dve.wait_ge(sem("rsqrt_ready"), norm + 1)
                newton(rs[:, 0:n], acc[:, 0:n], sq[0][:, 0:n], rs[:, 0:n], sem("rs_ready"))
                Dv.fence()

            def newton(ms, y, tmp, dst, s=None):
                stt(tmp, y, -0.5, y, M, M)
                Dv.fence()
                tt(tmp, tmp, ms, M)
                Dv.fence()
                stt(dst, tmp, 1.5, y, A_, M, s)

            def seq(*ops):
                for op in ops:
                    Dv.fence()
                    op()

            Dv.do(v.memset(small[:, 490:491], EPS))
            Dv.do(v.memset(small[:, 491:492], 1e-36))
            Dv.do(v.memset(small[:, 492:493], HD * EPS), sem("eps_set"))

            lr, li = col("lam_re", 0, PAIRS), col("lam_im", 0, PAIRS)
            dve.wait_ge(sem("lam_act"), 1)
            MAGIC, C1 = 1.5 * 2.0 ** 23, 6.28125
            C2 = float(np.float32(np.float64(2 * math.pi) - C1))
            C2 = float(np.frombuffer((np.float32(C2).view(np.uint32) & np.uint32(0xFFFFF000)).tobytes(), np.float32)[0])
            C3 = 2 * math.pi - C1 - C2
            ts(sm("e1"), sm("t"), 1.0, None, A_)
            ts(sm("e2"), sm("t"), -1.0, 1.0, M, A_)
            seq(lambda: Dv.do(v.reciprocal(sm("e2"), sm("e2"))),
                lambda: tt(sm("e1"), sm("e1"), sm("e2"), M),
                lambda: tt(sm("e1"), sm("e1"), sm("e1"), M),
                lambda: tt(sm("e1"), sm("e1"), sm("e1"), M),
                lambda: tt(sm("dt"), sm("e1"), sm("e1"), M),
                lambda: tt(sm("rho"), lr, sm("dt"), M),
                lambda: tt(sm("phi"), li, sm("dt"), M),
                lambda: ts(sm("k"), sm("phi"), 1.0 / (2 * math.pi), None, M),
                lambda: ts(sm("k"), sm("k"), MAGIC, None, A_),
                lambda: ts(sm("k"), sm("k"), MAGIC, None, S_),
                lambda: stt(sm("f"), sm("k"), -C1, sm("phi"), M, A_),
                lambda: stt(sm("f"), sm("k"), -C2, sm("f"), M, A_),
                lambda: stt(sm("f"), sm("k"), -C3, sm("f"), M, A_),
                lambda: ts(sm("f"), sm("f"), math.pi, -math.pi, ALU.min, ALU.max),
                lambda: stt(sm("ca"), sm("f"), -1.0, sm("f"), M, ALU.max),
                lambda: ts(sm("ca"), sm("ca"), -0.5, math.pi / 2, M, A_, sem("lam_dve")))
            def discretise_1():
                dve.wait_ge(sem("lam_act"), 2)
                ts(sm("e2"), sm("th"), -1.0, 1.0, M, A_)
                tt(sm("cm1"), sm("s"), sm("s"), M)
                stt(sm("sphi"), sm("s"), 2.0, sm("c"), M, M)
                tt(sm("den"), lr, lr, M)
                tt(sm("e1"), li, li, M)
                seq(lambda: Dv.do(v.reciprocal(sm("e2"), sm("e2"))))
                ts(sm("cm1"), sm("cm1"), -2.0, None, M)
                tt(sm("den"), sm("den"), sm("e1"), A_)

            def discretise_2():
                seq(lambda: stt(sm("em1"), sm("th"), 2.0, sm("e2"), M, M))
                ts(sm("cphi"), sm("cm1"), 1.0, None, A_)
                Dv.do(v.reciprocal(sm("den"), sm("den")))
                seq(lambda: ts(sm("r"), sm("em1"), 1.0, None, A_))
                tt(sm("nr"), sm("em1"), sm("cphi"), M)
                seq(lambda: tt(sm("nr"), sm("nr"), sm("cm1"), A_))
                tt(sm("ni"), sm("r"), sm("sphi"), M)
                tt(sm("r2"), sm("r"), sm("r"), M)
                tt(sm("p2r"), sm("sphi"), sm("sphi"), M)
                tt(sm("e1"), sm("cphi"), sm("cphi"), M)
                stt(sm("p2i"), sm("sphi"), 2.0, sm("cphi"), M, M)

            def discretise_3():
                seq(lambda: ts(sm("ar"), sm("nr"), 1.0, None, A_))
                tt(sm("p2r"), sm("e1"), sm("p2r"), S_)
                tt(sm("r4"), sm("r2"), sm("r2"), M)
                tt(sm("e2"), sm("nr"), lr, M)
                tt(sm("th"), sm("ni"), li, M)
                tt(sm("s"), sm("ni"), lr, M)
                tt(sm("c"), sm("nr"), li, M)
                seq(lambda: tt(sm("zr"), sm("e2"), sm("th"), A_))
                tt(sm("zi"), sm("s"), sm("c"), S_)
                Dv.fence()
                tt(sm("e1"), sm("p2r"), sm("p2r"), M)
                tt(sm("e2"), sm("p2i"), sm("p2i"), M)
                stt(sm("p4i"), sm("p2r"), 2.0, sm("p2i"), M, M)
                seq(lambda: tt(sm("zr"), sm("zr"), sm("den"), M))
                tt(sm("zi"), sm("zi"), sm("den"), M)
                tt(sm("p4r"), sm("e1"), sm("e2"), S_, sem("lam_dve"))

            for m in range(KT):
                dve.wait_ge(sem("h1_hi"), m + 1)
                stt(hlo[:, m, :], x[:, m, :], col("g_mix_pre", m), f32(hhi[:, m, :]), M, S_, sem("h1_lo"))
                if m == 0:
                    split_lo(0)
                if m == 2:
                    discretise_1()
                if m == 4:
                    discretise_2()
                if m == 5:
                    split_lo(1)
                if m == 6:
                    discretise_3()

            dve.wait_ge(sem("consts_in"), 16)
            Dv.do(v.tensor_reduce(eye32[:, :], ident.rearrange("p (g c) -> p c g", g=4), AX.X, A_))
            Dv.fence()
            for t in range(CT):
                ts(dmat[:, t, :], eye32[:, :], col("ssm_d", t), 0.0, M, A_, sem("d_ready"))

            def wide(name):
                return sm(name).unsqueeze(2).to_broadcast([P, PAIRS, 32])

            def b_step(j):
                if j == 0:
                    dve.wait_ge(sem("ssm_b_in"), 16)
                src = b_raw if j == 0 else b_pow[j - 1]
                cr, ci = (wide("zr"), wide("zi")) if j == 0 else (wide("ar"), wide("ai"))
                sr, si = (src[:, k, :].rearrange("p (a b) -> p a b", b=32) for k in range(2))
                t3 = [t[:, :].rearrange("p (a b) -> p a b", b=32) for t in b_t]
                Dv.fence()
                tt(t3[0], sr, cr, M)
                tt(t3[1], si, ci, M)
                tt(t3[2], sr, ci, M)
                tt(t3[3], si, cr, M)
                Dv.fence()
                tt(b_pow[j][:, 0, :], b_t[0][:, :], b_t[1][:, :], S_)
                tt(b_pow[j][:, 1, :], b_t[2][:, :], b_t[3][:, :], A_, sem("b_ready"))

            def gate_rows():
                lf, ii = sq[1][0:4, :], sq[0][0:4, :]
                dve.wait_ge(sem("gate_z"), 1)
                stt(sq[1][0:4, :], acc[0:4, :], -1.0, acc[0:4, :], M, ALU.min, sem("gate_abs"))
                ts(ii, ii, col("b_i", 0, 1, 0, 4), None, A_)
                dve.wait_ge(sem("gate_ln"), 1)
                Dv.fence()
                stt(lf, acc[0:4, :], 0.0, lf, ALU.min, S_)
                Dv.fence()
                Dv.do(v.tensor_tensor_scan(acc[0:4, :], ones_row, lf, 0.0, M, A_))
                Dv.fence()
                tt(ii, ii, acc[0:4, :], S_)
                Dv.fence()
                Dv.do(v.tensor_tensor_scan(lf, zero_row, ii, NEG, A_, ALU.max))
                Dv.fence()
                tt(lf, lf, acc[0:4, :], A_)
                Dv.fence()
                ts(lf, lf, 0.0, None, ALU.max)
                Dv.fence()
                tt(rows[0:4, :], acc[0:4, :], lf, S_)
                Dv.do(v.tensor_copy(rows[32:36, :], lf), sem("rows_ready"))

            ones_row = ones[0:4, 0:1].to_broadcast([4, T1])
            zero_row = ident[0:4, 64:65].to_broadcast([4, T1])

            def rotate(t, sg):
                m0, m1, m2, m3 = (t_[:, :, :] for t_ in rot)
                pr, pi = (ph[:, k, 4 * t:4 * t + 4, :] for k in range(2))
                X = xst[t % 2]
                c0 = sg * SEG
                er, ei = (PS[:, 4:8, CHUNKS * k + c0:CHUNKS * k + c0 + SEG] for k in range(2))
                if sg == 0:
                    dve.wait_ge(sem("e_mm"), t + 1)
                    if t == 0:
                        dve.wait_ge(sem("ssm_tables"), 2)
                        for j in range(2):
                            Dv.do(v.memset(xst[j][:, :, :, 0:1], 0.0))
                    if t >= 2:
                        dve.wait_ge(sem("y_mm"), t - 1)
                Dv.fence()
                tt(m0, er, pr, M)
                tt(m1, ei, pi, M)
                tt(m2, ei, pr, M)
                tt(m3, er, pi, M, sem("e_used") if sg else None)
                Dv.fence()
                tt(m0, m0, m1, A_)
                tt(m2, m2, m3, S_)
                Dv.fence()
                for g in range(4):
                    decay = sm("r4")[:, 4 * t + g:4 * t + g + 1].to_broadcast([P, SEG])
                    for k, w in ((0, rot[0]), (1, rot[2])):
                        start = X[:, k, g, SEG:SEG + 1] if sg else 0.0
                        Dv.do(v.tensor_tensor_scan(w[:, g, :], decay, w[:, g, :], start, M, A_))
                Dv.fence()
                tt(m1, m0, pr, M)
                tt(m3, m2, pi, M)
                Dv.fence()
                tt(X[:, 0, :, 1 + c0:1 + c0 + SEG], m1, m3, S_)
                Dv.fence()
                tt(m1, m0, pi, M)
                tt(m3, m2, pr, M)
                Dv.fence()
                tt(X[:, 1, :, 1 + c0:1 + c0 + SEG], m1, m3, A_, sem("x_ready") if sg else None)

            def mlstm_probs(h):
                dve.wait_ge(sem("w_ready"), h + 1)
                dve.wait_ge(sem("s_mm"), h + 1)
                sc = P ** -0.5
                stt(two(Wm[:, 0:T1]), PS[:, 6:8, 0:HALF], sc, two(Wm[:, 0:T1]), M, M)
                for j, (bank, c) in {1: (5, 0), 2: (4, 0), 3: (4, 272), 4: (4, 416)}.items():
                    k = min(P, S_LEN[j])
                    w = Wm[0:k, S_OFF[j]:S_OFF[j] + S_LEN[j]]
                    stt(w, PS[0:k, bank, c:c + S_LEN[j]], sc, w, M, M, sem("p_ready") if j == 4 else None)

            def mlstm_den(h):
                dve.wait_ge(sem("densq_ready"), h + 1)
                Dv.fence()
                tt(acc[:, :], acc[:, :], sq[1][:, :], ALU.max, sem("den_used"))

            def mlstm_out(h):
                dve.wait_ge(sem("ss_mm"), h + 1)
                Dv.fence()
                stt(two(acc[:, :]), two(acc[:, :]), EPS * P, PS[:, 4:6, 0:HALF], M, A_, sem("z_ready"))
                dve.wait_ge(sem("sd_ready"), h + 1)
                Dv.do(v.reciprocal(acc[:, :], acc[:, :]))
                Dv.fence()
                dve.wait_ge(sem("numsq_ready"), h + 1)
                tt(num[:, :], num[:, :], acc[:, :], M)
                Dv.fence()
                dve.wait_ge(sem("og_ready"), h + 1)
                stt(num[:, :], num[:, :], col("g_head", h), og[:, h, :], M, M, sem("yb_pre"))
                dve.wait_ge(sem("yb_hi"), h + 1)
                tt(yblo[:, h, :], num[:, :], f32(ybhi[:, h, :]), S_, sem("yb_lo"))

            for n in range(U_GLU):
                split_lo(n + LOOK)
                if n == 0:
                    rstd(0, T1)
                if n == U_Q:
                    Dv.fence()
                    for j in range(2):
                        Dv.do(v.memset(qp[j][:, 0:3], 0.0))
                dve.wait_ge(unit_done, n + 1)
                s = n % 2
                if n < U_GATES:
                    if n >= 2:
                        dve.wait_ge(sem("u_ready"), n - 1)
                    tt(two(sq[n % 2][:, :]), pair(s), two(rs[:, :]), M, evacuated)
                elif n == U_GATES:
                    dve.wait_ge(sem("u_ready"), CT)
                    tt(two(sq[0][0:4, :]), PS[0:4, 2 * s:2 * s + 2, 0:HALF], two(rs[0:4, :]), M)
                    tt(two(acc[0:4, :]), PS[32:36, 2 * s:2 * s + 2, 0:HALF], two(rs[32:36, :]), M, evacuated)
                elif n < U_V:
                    m = n - U_Q
                    if m >= 2:
                        dve.wait_ge(sem("tap_ready"), 3 * (m - 1))
                    if m == 0:
                        Dv.fence()
                    tt(two(qp[m % 2][:, 3:T1 + 3]), pair(s), two(rs[:, :]), M, evacuated)
                elif n < U_O:
                    j = n - U_V
                    if j == 0:
                        dve.wait_ge(sem("tap_added"), 6 * HEADS1)
                    if j >= 2:
                        dve.wait_ge(sem("vt_mm"), j - 1)
                    tt(two(vT[j % 2][:, :]), pair(s), two(rs[:, :]), M, evacuated)
                elif n < U_GA:
                    tt(two(og[:, n - U_O, :]), pair(s), two(rs[:, :]), M, evacuated)
                else:
                    tt(two(G[:, n - U_GA, :]), pair(s), two(rs[:, :]), M, evacuated)
                if n < 4:
                    b_step(n)
                if n == U_GATES:
                    gate_rows()
                if E_AFTER[0] <= n < E_AFTER[0] + 8:
                    rotate(*divmod(n - E_AFTER[0], 2))
                if U_O <= n < U_GA:
                    j = n - U_O
                    dve.wait_ge(sem("ya_hi"), j + 1)
                    tt(yalo[:, j, :], ya[:, j, :], f32(yahi[:, j, :]), S_, sem("ya_lo"))
                if n >= U_GA - 1:
                    h, k = divmod(n - (U_GA - 1), 4)
                    if h < HEADS1:
                        (lambda h: None, mlstm_probs, mlstm_den, mlstm_out)[k](h)

            for n in range(U_GLU, U_MERGE):
                split_lo(n + LOOK)
            for m in range(CT):
                tt(ya[:, m, :], f32(yahi[:, m, :]), f32(yalo[:, m, :]), A_)
                if m % 2:
                    dve.wait_ge(evacuated, U_GLU + m // 2 + 1)
                else:
                    dve.wait_ge(sem("glu_sg"), m // 2 + 1)
                Dv.fence()
                tt(ya[:, m, :], ya[:, m, :], sq[m % 2][:, :], M, sem("ya2_pre"))
            for m in range(CT):
                dve.wait_ge(sem("ya2_hi"), m + 1)
                tt(yalo[:, m, :], ya[:, m, :], f32(yahi[:, m, :]), S_, sem("ya2_lo"))
            Dv.n[evacuated.name] += U_MERGE - U_GLU

            def gslice(k):
                return two(G[:, bass.ds(k, 1), :].rearrange("p a b -> p (a b)"))

            dve.wait_ge(sem("g_ready"), 2 * KT)
            with Dv.loop(2, {lo_ready: 4, evacuated: 4, sem("mg_pre"): 4, sem("mg_lo"): 4, dve_steps: 4}) as i:
                for j in range(4):
                    s = (U_MERGE + j) % 2
                    split_lo(U_MERGE + j + LOOK, i * 4)
                    dve.wait_ge(unit_done, i * 4 + (U_MERGE + j + 1))
                    Dv.fence()
                    tt(two(sq[j % 2][:, :]), pair(s), gslice(i * 4 + j), M)
                    tt(two(num[:, :]), PS[:, 4 + 2 * s:6 + 2 * s, 0:HALF], gslice(i * 4 + (KT + j)), M, evacuated)
                    Dv.fence()
                    tt(sq[j % 2][:, :], sq[j % 2][:, :], num[:, :], A_, sem("mg_pre"))
                    dve.wait_ge(sem("mg_hi"), i * 4 + (j + 1))
                    one = (slice(None), bass.ds(i * 4 + j, 1), slice(None))
                    tt(hlo[one].rearrange("p a b -> p (a b)"), sq[j % 2][:, :],
                       f32(hhi[one].rearrange("p a b -> p (a b)")), S_, sem("mg_lo"))
            with Dv.loop(2, {lo_ready: 4, evacuated: 4}) as i:
                for j in range(4):
                    split_lo(U_OUT + j + LOOK, i * 4)
                    dve.wait_ge(unit_done, i * 4 + (U_OUT + j + 1))
                    Dv.do(v.tensor_copy(two(ysum[:, bass.ds(i * 4 + j, 1), :].rearrange("p a b -> p (a b)")),
                                        pair((U_OUT + j) % 2)), evacuated)
            def residual(norm, gain, n, c0, ready, hi, lo, pre):
                rstd(norm, n)
                for m in range(KT + 1):
                    if m < KT:
                        if m < OWN_SCALED:
                            tt(ysum[:, m, 0:n], ysum[:, m, 0:n], rs[:, 0:n], M)
                            Dv.fence()
                        else:
                            dve.wait_ge(sem("y_scaled"), (KT - OWN_SCALED) * POST.index(norm) + m - OWN_SCALED + 1)
                        stt(x[:, m, c0:T1], ysum[:, m, 0:n], col(gain, m), x[:, m, c0:T1], M, A_, sem(ready))
                    if m:
                        dve.wait_ge(sem(hi), m)
                        stt(hlo[:, m - 1, 0:n], x[:, m - 1, c0:T1], col(pre, m - 1), f32(hhi[:, m - 1, 0:n]), M, S_, sem(lo))

            dve.wait_ge(sem("x_again"), 16)
            residual(1, "g_mix_post", T1, 0, "x1_ready", "h2_hi", "h2_lo", "g_ffn_pre")
            for j in range(2):
                Dv.do(v.memset(gp[j][:, 0:2], 0.0))

            def ffn_mul(f, rf):
                dve.wait_ge(sem("gl_ready"), rf + (f + 1))
                Dv.fence()
                tt(tup[f % 2][:, :], tup[f % 2][:, :], cg[f % 2][:, :], M, sem("fa_pre"))

            def ffn_lo(f, rf, fl, rfl):
                dve.wait_ge(sem("fa_hi"), rf + (f + 1))
                pick = (slice(None), slice(fl, fl + 1) if isinstance(rfl, int) else bass.ds(rfl + fl, 1), slice(None))
                tt(falo[pick].rearrange("p a b -> p (a b)"), tup[f % 2][:, :],
                   f32(fahi[pick].rearrange("p a b -> p (a b)")), S_, sem("fa_lo"))

            def ffn_pair(s, r, f, rf, fl, rfl):
                p = f % 2
                split_lo(s + LOOK, r)
                if f == 0:
                    rstd(2, T1)
                dve.wait_ge(unit_done, r + (s + 1))
                if f >= 2:
                    dve.wait_ge(sem("conv2_ready"), rf + (f - 1))
                tt(two(gp[p][:, 2:T1 + 2]), pair(s % 2), two(rs[:, :]), M, evacuated)
                if fl:
                    ffn_mul(f - 1, rf)
                split_lo(s + 1 + LOOK, r)
                if fl:
                    ffn_lo(f - 1, rf, fl - 1, rfl)
                dve.wait_ge(unit_done, r + (s + 2))
                if f >= 2:
                    dve.wait_ge(sem("fa_lo"), rf + (f - 1))
                tt(tup[p][:, :], PS[:, 2 * ((s + 1) % 2), :], rs[:, META:T1], M, evacuated)

            s0, f0 = U_FFN, 0
            for c, tiles in enumerate(FFN_CHUNKS):
                for q in range(2):
                    ffn_pair(s0 + 2 * q, 0, f0 + q, 0, q, 0)
                with Dv.loop(tiles // 2 - 1, {lo_ready: 4, evacuated: 4, sem("fa_pre"): 2, sem("fa_lo"): 2}) as i:
                    for q in range(2, 4):
                        ffn_pair(s0 + 2 * q, i * 4, f0 + q, i * 2, q, i * 2)
                s0 += 2 * tiles
                f0 += tiles
                ffn_mul(f0 - 1, 0)
                ffn_lo(f0 - 1, 0, tiles - 1, 0)
                with Dv.loop(2, {lo_ready: 4, evacuated: 4}) as i:
                    for j in range(4):
                        split_lo(s0 + j + LOOK, i * 4)
                        dve.wait_ge(unit_done, i * 4 + (s0 + j + 1))
                        o = ysum[:, bass.ds(i * 4 + j, 1), 0:SEQ].rearrange("p a b -> p (a b)")
                        if c == 0:
                            Dv.do(v.tensor_copy(o, PS[:, 2 * ((s0 + j) % 2), :]), evacuated)
                        else:
                            tt(o, o, PS[:, 2 * ((s0 + j) % 2), :], A_, evacuated)
                s0 += KT
            residual(3, "g_ffn_post", SEQ, META, "x2_ready", "h3_hi", "h3_lo", "attn_norm")

            for n in range(U_V2, U_F2):
                split_lo(n + LOOK)
                j = n - U_V2
                if j == 0:
                    rstd(4, SEQ)
                dve.wait_ge(unit_done, n + 1)
                if j >= 2:
                    dve.wait_ge(sem("v2t_mm"), j - 1)
                tt(vT2[j % 2][:, :], PS[:, n % 2, :], rs[:, 0:SEQ], M, evacuated)
            split_lo(U_F2 + LOOK)
            dve.wait_ge(unit_done, U_F2 + 1)
            fz, fl_ = fox[0][0:N_FOX, :], fox[1][0:N_FOX, :]
            tt(fz, PS[0:N_FOX, U_F2 % 2, :], rs[0:N_FOX, 0:SEQ], M, evacuated)
            dve.wait_ge(sem("fox_z"), 1)
            stt(fl_, fz, -1.0, fz, M, ALU.min, sem("fox_abs"))
            dve.wait_ge(sem("fox_ln"), 1)
            stt(fl_, fz, 0.0, fl_, ALU.min, S_)
            Dv.fence()
            Dv.do(v.tensor_tensor_scan(fz, ones[0:N_FOX, 0:1].to_broadcast([N_FOX, SEQ]), fl_, 0.0, M, A_))
            Dv.fence()
            ts(fz, fz, -1.0, None, M, None, sem("fox_ready"))
            for j in range(2):
                Dv.do(v.memset(qa[j][64:65, :, :], 1.0), sem("qa_ones"))

            def gate_evac(j):
                n = U_GFOX + j
                dve.wait_ge(unit_done, n + 1)
                tt(sgf[:, j, :], PS[:, n % 2, :], rs[:, 0:SEQ], M, evacuated)

            def qk_evac(i, w):
                n = U_QK2 + 2 * i + w
                dve.wait_ge(unit_done, n + 1)
                Dv.fence()
                tt(qr[w][:, :], PS[:, n % 2, :], rs[:, 0:SEQ], M, evacuated)

            def qk_ms(i, w):
                n = U_QK2 + 2 * i + w
                dve.wait_ge(sem("qstat_mm"), 2 * i + w + 1)
                ts(sq[w][:, 0:SEQ], PS[:, n % 2, :], (1.0, 1.0 / HD)[w], (HD * EPS, EPS)[w], M, A_, sem("qms_ready"))

            def qk_norm(i, w):
                dve.wait_ge(sem("qrs_ready"), 2 * i + w + 1)
                Dv.fence()
                newton(sq[w][:, 0:SEQ], (acc, rows)[w][:, 0:SEQ], qtmp[:, :], sq[w][:, 0:SEQ])
                Dv.fence()
                if i >= 2:
                    dve.wait_ge(sem("qk_mm"), 2 * (i - 1))
                dst = (qa, ka)[w][i % 2]
                for hh in range(2):
                    a = slice(64 * hh, 64 * hh + 64)
                    g = cols[a, COL[("q_gain", "k_gain")[w]] + i:COL[("q_gain", "k_gain")[w]] + i + 1]
                    stt(dst[0:64, hh, :], qr[w][a, :], g, sq[w][a, 0:SEQ], M, M, sem("aug_ready"))

            def maxima(i, hh):
                h = 2 * i + hh
                b = 2 + 3 * hh
                dve.wait_ge(sem("qk_mm"), h + 1)
                if i:
                    dve.wait_ge(sem("p2_ready"), 4 * (h - 1))
                for t in range(4):
                    bank, c = QB[t]
                    Dv.do(v.tensor_reduce(nm[:, 4 * hh + t:4 * hh + t + 1], PS[:, b + bank, c:c + P * (t + 1)],
                                          AX.X, ALU.max, negate=True), sem("max_ready"))

            def weigh(i, hh):
                h = 2 * i + hh
                if h < N_MOBA + N_FOX:
                    return
                for t in range(4):
                    bank, c = QB[t]
                    w = P * (t + 1)
                    dve.wait_ge(sem("p2_ready"), 4 * h + t + 1)
                    Dv.do(v.tensor_tensor_reduce(out=Pb[hh][:, bank, c:c + w], in0=Pb[hh][:, bank, c:c + w],
                                                 in1=dil[:, 1, P * (3 - t):SEQ], scale=1.0, scalar=0.0, op0=M, op1=A_,
                                                 accum_out=rsum[:, 4 * hh + t:4 * hh + t + 1]), sem("weighed"))

            def pt_copy(i, hh):
                h = 2 * i + hh
                dve.wait_ge(sem("pt_mm"), h + 1)
                Dv.do(v.tensor_copy(Pb[hh][:, 2, 0:2 * P], PS[:, 2 + 3 * hh + 2, 0:2 * P]), sem("pt_dve"))

            def attn_out(i, hh):
                h = 2 * i + hh
                Dv.fence()
                dve.wait_ge(sem("p2_ready"), 4 * h + 4)
                Dv.do(v.reciprocal(rinv[:, 4 * hh:4 * hh + 4], rsum[:, 4 * hh:4 * hh + 4]))
                Dv.fence()
                dve.wait_ge(sem("pv_mm"), h + 1)
                tt(yq[:, :, HD * h:HD * h + HD], PS[:, 2 + 3 * hh, 0:4 * HD].rearrange("p (a b) -> p a b", a=4),
                   rinv[:, 4 * hh:4 * hh + 4].unsqueeze(2).to_broadcast([P, 4, HD]), M, sem("attn_done"))

            def group_ms(g0, g1):
                dve.wait_ge(sem("group_sq"), 4 * g1)
                for g in range(g0, g1):
                    a, b = GROUPS[g]
                    c = gms[:, 4 * g:4 * g + 4]
                    ts(c, c, 1.0 / (b - a), EPS, M, A_, sem("gms_ready"))

            def group_norm(n, g0, g1):
                c = slice(4 * g0, 4 * g1)
                dve.wait_ge(sem("grs_ready"), n)
                Dv.fence()
                newton(gms[:, c], gy[:, c], gtmp[:, c], gms[:, c], sem("group_ready"))

            for i in range(KT + 2):
                if i < KT:
                    qk_evac(i, 0)
                else:
                    gate_evac(2 * (i - KT))
                if i >= 2:
                    pt_copy(i - 2, 1)
                if 1 <= i <= KT:
                    maxima(i - 1, 0)
                if i >= 2:
                    attn_out(i - 2, 1)
                if i < KT:
                    qk_ms(i, 0)
                split_lo(U_QK2 + 2 * i + LOOK)
                if 1 <= i <= KT:
                    weigh(i - 1, 0)
                if i < KT:
                    qk_evac(i, 1)
                if i == KT:
                    gate_evac(1)
                    group_ms(0, 2)
                if 1 <= i <= KT:
                    pt_copy(i - 1, 0)
                if i < KT:
                    qk_norm(i, 0)
                if 1 <= i <= KT:
                    maxima(i - 1, 1)
                    attn_out(i - 1, 0)
                if i < KT:
                    qk_ms(i, 1)
                    qk_norm(i, 1)
                if i <= KT:
                    split_lo(U_QK2 + 2 * i + 1 + LOOK)
                if i == KT:
                    group_norm(1, 0, 2)
                if 1 <= i <= KT:
                    weigh(i - 1, 1)

            group_ms(2, 3)
            group_norm(2, 2, 3)
            Dv.fence()
            a, b = GROUPS[2]
            for t in range(4):
                ts(yq[:, t, a:b], yq[:, t, a:b], gms[:, 8 + t:9 + t], 0.0, M, A_, sem("dil_scaled"))
            for m in range(KT):
                dve.wait_ge(sem("yt_mm"), m + 1)
                src = PS[:, 2 + m % 6, :]
                if m in FOX_TILES:
                    dve.wait_ge(sem("sgf_ready"), 3)
                    stt(qr[m % 2][:, :], src, col("out_gain", m), sgf[:, m - FOX_TILES[0], :], M, M, sem("yfox_pre"))
                    dve.wait_ge(sem("y2_hi"), m + 1)
                    tt(hlo[:, m, 0:SEQ], qr[m % 2][:, :], f32(hhi[:, m, 0:SEQ]), S_, sem("y2_lo"))
                else:
                    dve.wait_ge(sem("y2_hi"), m + 1)
                    stt(hlo[:, m, 0:SEQ], src, col("out_gain", m), f32(hhi[:, m, 0:SEQ]), M, S_, sem("y2_lo"))
            for m in range(KT):
                n = U_OUT2 + m
                split_lo(n + LOOK)
                dve.wait_ge(unit_done, n + 1)
                tt(x[:, m, META:T1], x[:, m, META:T1], PS[:, n % 2, :], A_, evacuated)
            for m in range(KT):
                dve.wait_ge(sem("h4_hi"), m + 1)
                stt(hlo[:, m, 0:SEQ], x[:, m, META:T1], col("mlp_norm", m), f32(hhi[:, m, 0:SEQ]), M, S_, sem("h4_lo"))

            def mlp_up(s, r, f, rf, fl):
                p = f % 2
                split_lo(s + LOOK, r)
                dve.wait_ge(sem("relu_ready"), rf + (f + 1))
                if not isinstance(rf, int) or f >= 2:
                    dve.wait_ge(sem("ma_lo"), rf + (f - 1))
                stt(r2[p][:, :], PS[:, s % 2, :], 0.0, rl[p][:, :], ALU.max, M, evacuated)
                dve.wait_ge(sem("ma_hi"), rf + (f + 1))
                tt(malo[:, fl, :], r2[p][:, :], f32(mahi[:, fl, :]), S_, sem("ma_lo"))

            def mlp_down(s, r, m):
                split_lo(s + LOOK, r)
                dve.wait_ge(unit_done, r + (s + 1))
                if isinstance(r, int) and s < U_MLP + 2 * KT:
                    Dv.do(v.tensor_copy(ysum[:, m, 0:SEQ], PS[:, s % 2, :]), evacuated)
                else:
                    tt(ysum[:, m, 0:SEQ], ysum[:, m, 0:SEQ], PS[:, s % 2, :], A_, evacuated)

            for f in range(KT):
                mlp_up(U_MLP + f, 0, f, 0, f)
                if f == 0:
                    rstd(5, SEQ)
                    tt(rs[:, 0:SEQ], rs[:, 0:SEQ], rs[:, 0:SEQ], M)
            for m in range(KT):
                mlp_down(U_MLP + KT + m, 0, m)
            with Dv.loop(2, {lo_ready: 16, evacuated: 16, sem("ma_lo"): 8}) as c:
                for f in range(KT):
                    mlp_up(U_MLP + 2 * KT + f, c * 16, KT + f, c * 8, f)
                for m in range(KT):
                    mlp_down(U_MLP + 3 * KT + m, c * 16, m)
            for f in range(KT):
                mlp_up(U_MLP + 6 * KT + f, 0, 3 * KT + f, 0, f)
            for m in range(KT):
                s = U_MLP + 7 * KT + m
                split_lo(s + LOOK)
                dve.wait_ge(unit_done, s + 1)
                tt(ysum[:, m, 0:SEQ], ysum[:, m, 0:SEQ], PS[:, s % 2, :], A_, evacuated)
                Dv.fence()
                tt(ysum[:, m, 0:SEQ], ysum[:, m, 0:SEQ], rs[:, 0:SEQ], M)
                Dv.fence()
                if m >= 2:
                    dve.wait_ge(sem(f"out_done{m % 2}"), 16 * (m // 2))
                tt(ot[m % 2][:, :], ysum[:, m, 0:SEQ], x[:, m, META:T1], A_, sem("out_ready"))

        @block.gpsimd
        def _(pool):
            Po = Order(pool, pool_steps)
            g = nc.gpsimd
            g_ts = g.tensor_scalar
            M, A_, S_ = ALU.mult, ALU.add, ALU.subtract

            def tt(o, a, b, op, s=None):
                Po.do(g.tensor_tensor(o, a, b, op), s)

            def post_norm(norm, n):
                for m in range(1, KT - 1):
                    pool.wait_ge(sem("sq_ready"), KT * POST.index(norm) + m + 1)
                    Po.fence()
                    tt(acc[:, 0:n], acc[:, 0:n], sq[m % 2][:, 0:n], A_, sem("sq_added"))
                pool.wait_ge(sem("rs_ready"), norm + 1)
                for m in range(OWN_SCALED, KT):
                    tt(ysum[:, m, 0:n], ysum[:, m, 0:n], rs[:, 0:n], M, sem("y_scaled"))

            pool.wait_ge(sem("lam_dve"), 2)
            pr, pi = ph[:, 0, :, :], ph[:, 1, :, :]
            Po.do(g.tensor_copy(pr[:, :, 0:1], sm("p4r").unsqueeze(2)))
            Po.do(g.tensor_copy(pi[:, :, 0:1], sm("p4i").unsqueeze(2)))
            m = 1
            while m < SEG:
                k = min(m, SEG - m)
                br, bi = (q[:, :, m - 1:m].to_broadcast([P, PAIRS, k]) for q in (pr, pi))
                t4 = [t[:, 0:PAIRS * k].rearrange("p (a b) -> p a b", a=PAIRS) for t in c_t]
                Po.fence()
                tt(t4[0], pr[:, :, 0:k], br, M)
                tt(t4[1], pi[:, :, 0:k], bi, M)
                tt(t4[2], pr[:, :, 0:k], bi, M)
                tt(t4[3], pi[:, :, 0:k], br, M)
                Po.fence()
                tt(pr[:, :, m:m + k], t4[0], t4[1], S_)
                tt(pi[:, :, m:m + k], t4[2], t4[3], A_)
                m += k
            pool.wait_ge(sem("ssm_c_in"), 16)
            Po.fence()
            Po.do(g.tensor_scalar(c_pow[:, 1, :, 0, :], c_pow[:, 1, :, 0, :], -1.0, None, M), sem("ssm_tables"))
            wr, wi = (sm(k).unsqueeze(2).to_broadcast([P, PAIRS, 32]) for k in ("ar", "ai"))
            for j in range(STEP):
                cr, cn = (c_pow[:, k, :, j, :] for k in range(2))
                t3 = [t[:, :].rearrange("p (a b) -> p a b", b=32) for t in c_t]
                Po.fence()
                tt(t3[0], cr, wr, M)
                tt(t3[1], cn, wi, M)
                tt(t3[2], cn, wr, M)
                tt(t3[3], cr, wi, M)
                Po.fence()
                tt(c_pow[:, 0, :, j + 1, :], t3[0], t3[1], A_)
                tt(c_pow[:, 1, :, j + 1, :], t3[2], t3[3], S_, sem("ssm_tables") if j == STEP - 1 else None)

            pool.wait_ge(sem("bt_mm"), 2 * STEP)
            Po.do(g.memset(kblk[:, :, :, :], 0.0), sem("kz"))
            for m in range(2 * HEADS1):
                for k in range(1, 4):
                    pool.wait_ge(sem("tap_ready"), 3 * m + k)
                    Po.fence()
                    tt(qk[:, m, :], qk[:, m, :], vT[k % 2][:, :], A_, sem("tap_added"))
                if m == 4:
                    pool.wait_ge(sem("k_mm"), 1)
                    Po.do(g.memset(vs[:, 4, :], 0.0), sem("vz"))
            pool.wait_ge(sem("ya_lo"), CT)
            Po.do(g.memset(Wm[:, S_OFF[4]:S_OFF[4] + 16], 0.0))
            for h in range(HEADS1):
                pool.wait_ge(sem("bc_done"), h + 1)
                if h:
                    pool.wait_ge(sem("nd_mm"), h)
                Po.fence()
                for j in range(5):
                    k = min(P, S_LEN[j])
                    tt(Wm[0:k, S_OFF[j]:S_OFF[j] + k], sq[0][0:k, P * j:P * j + k], mask_st[0:k, 0:k], A_, sem("diag_done"))
            post_norm(1, T1)

            s0, f = U_FFN, 0
            for tiles in FFN_CHUNKS:
                for q in range(tiles):
                    src, dst = gp[f % 2], cg[f % 2]
                    w = [col("ffn_conv", 4 * f + k) for k in range(4)]
                    pool.wait_ge(evacuated, s0 + 2 * q + 1)
                    if f >= 2:
                        pool.wait_ge(sem("fa_pre"), f - 1)
                    Po.do(g.tensor_scalar(dst[:, :], src[:, META:META + SEQ], w[0], w[3], M, A_))
                    for k in (1, 2):
                        Po.fence()
                        Po.do(g.tensor_scalar(ctmp[:, :], src[:, META + k:META + k + SEQ], w[k], 0.0, M, A_))
                        Po.fence()
                        tt(dst[:, :], dst[:, :], ctmp[:, :], A_, sem("conv2_ready") if k == 2 else None)
                    f += 1
                s0 += 2 * tiles + KT
            post_norm(3, SEQ)
            pool.wait_ge(sem("yb_lo"), HEADS1)
            pool.dma_start(dil[:, :, :], dil_in.rearrange("p (a b) -> p a b", a=2)).then_inc(sem("dil_in"), 16)
            pool.wait_ge(sem("fox_ready"), 1)
            for i in range(KT):
                if i >= 2:
                    pool.wait_ge(sem("qk_mm"), 2 * (i - 1))
                for hh in range(2):
                    h = 2 * i + hh
                    if N_MOBA <= h < N_MOBA + N_FOX:
                        src = fox[0][h - N_MOBA:h - N_MOBA + 1, :]
                    else:
                        src = alibi_in[h:h + 1, :]
                    pool.dma_start(ka[i % 2][64:65, hh, :], src).then_inc(sem(f"bias_in{i % 2}"), 16)
            pool.wait_ge(sem("group_ready"), 1)
            for g in range(2):
                a, b = GROUPS[g]
                for t in range(4):
                    Po.do(g_ts(yq[:, t, a:b], yq[:, t, a:b], gms[:, 4 * g + t:4 * g + t + 1], 0.0, M, A_), sem("yn_ready"))

        @block.tensor
        def _(pe):
            mm = nc.tensor.matmul

            def unit(s, r, xhi, xlo, outs, ready=None, base=0, blocks=None, last_of_unit=True, after=None):
                blocks = blocks or [(k, k) for k in range(KT)]
                for b, (kw, kx) in enumerate(blocks):
                    if ready is not None:
                        pe.wait_ge(ready, base + kx + 1)
                    w = slice(kw * P, kw * P + P)
                    for a, (wt, xt) in enumerate(((whi, xhi), (whi, xlo), (wlo, xhi))):
                        for o, c0, n in outs:
                            ins = mm(o, wt[:, s % RING, w], xt[:, kx, c0:c0 + n], start=(b == 0 and a == 0),
                                     stop=(b == len(blocks) - 1 and a == 2))
                    if last_of_unit and b == len(blocks) - 1:
                        ins.then_inc(unit_done, 1)
                    if after is not None:
                        after(b)

            def begin(s, r=0):
                pe.wait_ge(lo_ready, r + (s + 1))
                if s >= 2:
                    pe.wait_ge(evacuated, r + (s - 1))

            def halves(s, b0=None):
                b = 2 * (s % 2) if b0 is None else b0
                return [(PS[:, b + h, 0:HALF], HALF * h, HALF) for h in range(2)]

            def column_sums(n, src, start, stop):
                outs = [(4, 0, HALF), (5, HALF, HALF)] if n == T1 else [(4, 0, SEQ)]
                for b, c0, k in outs:
                    ins = mm(PS[:, b, 0:k], ones, src[:, c0:c0 + k], start=start, stop=stop)
                return ins

            def post_stat(norm, n):
                pe.wait_ge(sem("sq_added"), 6 * (POST.index(norm) + 1))
                column_sums(n, acc, True, False)
                pe.wait_ge(sem("sq_ready"), KT * (POST.index(norm) + 1))
                column_sums(n, sq[1], False, True).then_inc(sem("stat_mm"), 1)

            def tile_sum(norm, n, m):
                pe.wait_ge(sem("tile_sq"), KT * PRE.index(norm) + m + 1)
                column_sums(n, sq[m % 2], m == 0, m == KT - 1).then_inc(sem("tile_summed" if m < KT - 1 else "stat_mm"), 1)

            def b_transposes(ri):
                pe.wait_ge(sem("b_ready"), STEP)
                if ri == 0:
                    pe.wait_ge(sem("ms_ready"), 1)
                for s in range(STEP):
                    if ri:
                        pe.wait_ge(sem("bt_copied"), s + 1)
                    for t in range(CT):
                        ins = nc.tensor.transpose(PS[:, 4 + s, P * t:P * t + P], b_pow[s][:, ri, P * t:P * t + P], ident)
                    ins.then_inc(sem("bt_mm"), 1)

            def gate_transposes():
                pe.wait_ge(sem("bt_copied"), 2 * STEP)
                pe.wait_ge(sem("rows_ready"), 1)
                for j in range(5):
                    k = min(P, T1 - P * j)
                    ins = nc.tensor.transpose(PS[0:k, 4, 4 * j:4 * j + 4], sq[0][0:4, P * j:P * j + k], ident[0:4, 0:4])
                ins.then_inc(sem("r2_mm"), 1)

            def ssm_in(t):
                pe.wait_ge(sem("u_ready"), t + 1)
                if t == 0:
                    pe.wait_ge(sem("r2c_ready"), 1)
                else:
                    pe.wait_ge(sem("k_ready"), STEP)
                    pe.wait_ge(sem("e_used"), t)
                if t >= 2:
                    pe.wait_ge(sem("ya_ready"), t - 1)
                for g in range(4):
                    for ri in range(2):
                        ins = mm(PS[:, 4 + g, CHUNKS * ri:CHUNKS * ri + CHUNKS], bT[:, ri, t, g, :], u[:, t, g, :],
                                 start=True, stop=True)
                ins.then_inc(sem("e_mm"), 1)

            def ssm_kernel():
                pe.wait_ge(sem("ssm_tables"), 2)
                pe.wait_ge(sem("d_ready"), CT)
                pe.wait_ge(sem("e_used"), 1)
                for t in range(CT):
                    for g in range(4):
                        q = slice(32 * g, 32 * g + 32)
                        c = slice(32 * (4 * t + g), 32 * (4 * t + g) + 32)
                        mm(PS[q, 4, P * t:P * t + 32], ident[:, q], dmat[:, t, :], start=True, stop=True,
                           tile_position=(0, 32 * g))
                        for ri in range(2):
                            ins = mm(PS[q, 4, P * t:P * t + P], b_pow[0][:, ri, c],
                                     c_pow[:, ri, 4 * t + g, 0:STEP, :].rearrange("p s c -> p (s c)"), start=False,
                                     stop=(ri == 1), skip_group_check=True, tile_position=(0, 32 * g))
                ins.then_inc(sem("k_mm"), 1)

            def ssm_out(t):
                pe.wait_ge(sem("x_ready"), t + 1)
                pe.wait_ge(sem("e_used"), min(t + 2, CT))
                if t == CT - 1:
                    pe.wait_ge(sem("ya_ready"), t)
                X = xst[t % 2]
                for g in range(4):
                    y = PS[:, 4 + g // 2, CHUNKS * (g % 2):CHUNKS * (g % 2) + CHUNKS]
                    mm(y, kblk[:, t, g, :], u[:, t, g, :], start=True, stop=False)
                    for ri in range(2):
                        ins = mm(y, c_pow[:, ri, 4 * t + g, 1:STEP + 1, :].rearrange("p s c -> p (s c)"), X[:, ri, g, 0:CHUNKS], start=False, stop=(ri == 1))
                ins.then_inc(sem("y_mm"), 1)

            def v_transposes(j):
                b = VT_BANK[j]
                pe.wait_ge(evacuated, U_V + j + 1)
                if j in (0, 1):
                    pe.wait_ge(sem("e_used"), CT)
                if j in (1, 3):
                    pe.wait_ge(sem("vs_ready"), j if j == 1 else 2)
                if j == 2:
                    pe.wait_ge(sem("ya_ready"), CT)
                for k in range(4):
                    nc.tensor.transpose(PS[:, b, P * k:P * k + P], vT[j % 2][:, P * k:P * k + P], ident)
                nc.tensor.transpose(PS[0:16, b + 1, 0:P], vT[j % 2][:, 512:T1], ident).then_inc(sem("vt_mm"), 1)

            def mlstm_broadcast(h):
                pe.wait_ge(sem("sel_in"), 16)
                pe.wait_ge(sem("vs_ready"), 4)
                if h:
                    pe.wait_ge(sem("z_ready"), h)
                    pe.wait_ge(sem("den_used"), h)
                for p0, b in ((0, 4), (32, 6)):
                    for k in range(2):
                        ins = mm(PS[:, b + k, 0:HALF], sel[p0:p0 + 4, h, :], rows[p0:p0 + 4, HALF * k:HALF * k + HALF],
                                 start=True, stop=True, tile_position=(p0, 0))
                ins.then_inc(sem("bc_mm"), 1)

            def mlstm_scores(h):
                pe.wait_ge(sem("bc_done"), h + 1)
                pe.wait_ge(sem("qk_ready"), 2 * HEADS1)
                for k in range(2):
                    mm(PS[:, 6 + k, 0:HALF], qk[:, 4 + h, 0:P], qk[:, h, HALF * k:HALF * k + HALF], start=True, stop=True)
                for j, (bank, c) in {1: (5, 0), 2: (4, 0), 3: (4, 272), 4: (4, 416)}.items():
                    k = min(P, S_LEN[j])
                    ins = mm(PS[0:k, bank, c:c + S_LEN[j]], qk[:, 4 + h, P * j:P * j + k], qk[:, h, P * j:T1],
                             start=True, stop=True)
                ins.then_inc(sem("s_mm"), 1)

            def mlstm_values(h):
                pe.wait_ge(sem("p_ready"), h + 1)
                for b, lhs in ((4, lambda j: vs[:, j, P * h:P * h + P]), (6, lambda j: ones)):
                    for k in range(2):
                        js = [j for j in range(5) if P * j < HALF * (k + 1)]
                        for j in js:
                            t0 = max(P * j, HALF * k)
                            n = HALF * (k + 1) - t0
                            o = S_OFF[j] + t0 - P * j
                            ins = mm(PS[:, b + k, t0 - HALF * k:HALF], lhs(j), Wm[:, o:o + n], start=(j == 0),
                                     stop=(j == js[-1]), skip_group_check=True)
                ins.then_inc(sem("nd_mm"), 1)

            def mlstm_norm(h):
                pe.wait_ge(sem("numsq_ready"), h + 1)
                for k in range(2):
                    ins = mm(PS[:, 4 + k, 0:HALF], ones, sq[0][:, HALF * k:HALF * k + HALF], start=True, stop=True)
                ins.then_inc(sem("ss_mm"), 1)

            pe.wait_ge(sem("consts_in"), 16)
            for n in range(U_GLU):
                begin(n)
                if n == 0:
                    unit(n, 0, hhi, hlo, halves(n), sem("h1_lo"), after=lambda b: tile_sum(0, T1, b))
                else:
                    unit(n, 0, hhi, hlo, halves(n))
                if n in (4, 5):
                    b_transposes(n - 4)
                if n == 6:
                    gate_transposes()
                if n == 8:
                    ssm_kernel()
                if n in Y_AFTER:
                    ssm_out(Y_AFTER.index(n))
                if n in E_AFTER:
                    ssm_in(E_AFTER.index(n))
                if U_V + 1 <= n < U_V + 5:
                    v_transposes(n - U_V - 1)
                if n >= U_GA - 1:
                    h, k = divmod(n - (U_GA - 1), 4)
                    if h < HEADS1:
                        (mlstm_broadcast, mlstm_scores, mlstm_values, mlstm_norm)[k](h)

            pe.wait_ge(sem("z_ready"), HEADS1)
            pe.wait_ge(sem("den_used"), HEADS1)
            pe.wait_ge(sem("ya_lo"), CT)
            for n in range(U_GLU, U_MERGE):
                begin(n)
                unit(n, 0, yahi, yalo, halves(n), None, 0, [(k, k) for k in range(4)], False)
                unit(n, 0, yahi, yalo, halves(n, 4 + 2 * (n % 2)), None, 0, [(4 + k, k) for k in range(4)])
            pe.wait_ge(sem("yb_lo"), HEADS1)

            def branch(s, b):
                if b:
                    unit(s, 0, ybhi, yblo, halves(s, 4 + 2 * (s % 2)), None, 0, [(4 + k, k) for k in range(4)], False)
                else:
                    unit(s, 0, yahi, yalo, halves(s), None, 0, [(k, k) for k in range(4)])

            for s in (U_MERGE, U_MERGE + 1):
                begin(s)
                branch(s, 1)
            pe.wait_ge(sem("ya2_lo"), CT)
            for s in (U_MERGE, U_MERGE + 1):
                branch(s, 0)
            for s in range(U_MERGE + 2, U_OUT):
                begin(s)
                branch(s, 1)
                branch(s, 0)
            begin(U_OUT)
            unit(U_OUT, 0, hhi, hlo, halves(U_OUT), sem("mg_lo"))
            for n in range(U_OUT + 1, U_OUT + 4):
                begin(n)
                unit(n, 0, hhi, hlo, halves(n))
            for n in range(U_OUT + 4, U_FFN):
                begin(n)
                unit(n, 0, hhi, hlo, halves(n))
            post_stat(1, T1)

            def ffn_gate(s, r):
                begin(s, r)
                if isinstance(r, int) and s == U_FFN:
                    unit(s, r, hhi, hlo, halves(s), sem("h2_lo"), after=lambda b: tile_sum(2, T1, b))
                else:
                    unit(s, r, hhi, hlo, halves(s))

            def ffn_up(s, r):
                begin(s, r)
                unit(s, r, hhi, hlo, [(PS[:, 2 * (s % 2), :], META, SEQ)])

            def down(s, r, xhi, xlo, o, ready=None, base=0, tiles=KT):
                begin(s, r)
                unit(s, r, xhi, xlo, [(o, 0, SEQ)], ready, base, [(k, k) for k in range(tiles)])

            s0, f0 = U_FFN, 0
            for c, tiles in enumerate(FFN_CHUNKS):
                for q in range(2):
                    ffn_gate(s0 + 2 * q, 0)
                    ffn_up(s0 + 2 * q + 1, 0)
                with pe.Fori(0, tiles // 2 - 1) as i:
                    for q in range(2, 4):
                        ffn_gate(s0 + 2 * q, i * 4)
                        ffn_up(s0 + 2 * q + 1, i * 4)
                s0 += 2 * tiles
                with pe.Fori(0, 2) as i:
                    for j in range(4):
                        down(s0 + j, i * 4, fahi, falo, PS[:, 2 * ((s0 + j) % 2), :], sem("fa_lo") if j == 0 else None,
                             f0, tiles)
                f0 += tiles
                s0 += KT
            post_stat(3, SEQ)

            def v2_transposes(j):
                pe.wait_ge(evacuated, U_V2 + j + 1)
                if j >= 2:
                    pe.wait_ge(sem("v2_ready"), j - 1)
                for t in range(4):
                    ins = nc.tensor.transpose(PS[:, 2 + j % 2, P * t:P * t + P], vT2[j % 2][:, P * t:P * t + P], ident)
                ins.then_inc(sem("v2t_mm"), 1)

            def wide(s, r=0, ready=None, norm=None):
                begin(s, r)
                unit(s, r, hhi, hlo, [(PS[:, s % 2, :], 0, SEQ)], ready,
                     after=(lambda b: tile_sum(norm, SEQ, b)) if norm else None)

            pe.wait_ge(evacuated, U_V2)
            wide(U_V2, 0, sem("h3_lo"), 4)
            for n in range(U_V2 + 1, U_QK2):
                wide(n)
                if n <= U_F2:
                    v2_transposes(n - 1 - U_V2)

            def qk_stat(i, w):
                pe.wait_ge(sem("qsq_ready"), 2 * i + w + 1)
                mm(PS[:, (U_QK2 + w) % 2, :], blk64, sq[w][:, 0:SEQ], start=True, stop=True).then_inc(sem("qstat_mm"), 1)

            def scores(i, hh):
                h = 2 * i + hh
                b = 2 + 3 * hh
                q, k = qa[i % 2], ka[i % 2]
                pe.wait_ge(sem("aug_ready"), 4 * i + 4)
                pe.wait_ge(sem("qa_ones"), 2)
                pe.wait_ge(sem(f"bias_in{i % 2}"), 32 * (i // 2 + 1))
                if i:
                    pe.wait_ge(sem("attn_done"), h - 1)
                pe.wait_ge(sem("masks_ready"), 3)
                for t in range(4):
                    bank, c = QB[t]
                    w = P * (t + 1)
                    if h < N_MOBA + N_FOX:
                        mm(PS[:, b + bank, c + w - P:c + w], identr[:, :], maskr[:, :], start=True, stop=True)
                    else:
                        mm(PS[:, b + bank, c:c + w], identr[:, :], dilr[:, P * (3 - t):SEQ], start=True, stop=True)
                    ins = mm(PS[:, b + bank, c:c + w], q[0:65, hh, P * t:P * t + P], k[0:65, hh, 0:w], start=False,
                             stop=True, skip_group_check=True)
                ins.then_inc(sem("qk_mm"), 1)

            def p_transposes(i, hh):
                h = 2 * i + hh
                b = 2 + 3 * hh
                for t in range(4):
                    bank, c = QB[t]
                    pe.wait_ge(sem("p2_ready"), 4 * h + BANK_DONE[t])
                    if h >= N_MOBA + N_FOX:
                        pe.wait_ge(sem("weighed"), 4 * (h - N_MOBA - N_FOX) + BANK_DONE[t])
                    for k in range(t + 1):
                        ins = nc.tensor.transpose(PS[:, b + bank, c + P * k:c + P * k + P],
                                                  Pb[hh][:, bank, c + P * k:c + P * k + P], ident)
                ins.then_inc(sem("pt_mm"), 1)

            def values(i, hh):
                h = 2 * i + hh
                pe.wait_ge(sem("pt_act"), h + 1)
                pe.wait_ge(sem("pt_dve"), h + 1)
                if h == 0:
                    pe.wait_ge(sem("v2_ready"), KT)
                for t in range(4):
                    bank, c = QB[t]
                    for k in range(t + 1):
                        ins = mm(PS[:, 2 + 3 * hh, HD * t:HD * t + HD], Pb[hh][:, bank, c + P * k:c + P * k + P],
                                 V[:, k, HD * h:HD * h + HD], start=(k == 0), stop=(k == t))
                ins.then_inc(sem("pv_mm"), 1)

            for i in range(KT + 2):
                n = U_QK2 + 2 * i
                if 1 <= i <= KT:
                    pe.wait_ge(sem("qms_ready"), 2 * i - 1)
                wide(n)
                if i >= 2:
                    p_transposes(i - 2, 1)
                if 1 <= i <= KT:
                    scores(i - 1, 0)
                if i >= 2:
                    values(i - 2, 1)
                if i < KT:
                    qk_stat(i, 0)
                if i <= KT:
                    if i:
                        pe.wait_ge(sem("qms_ready"), 2 * i)
                    wide(n + 1)
                if 1 <= i <= KT:
                    p_transposes(i - 1, 0)
                    scores(i - 1, 1)
                    values(i - 1, 0)
                if i < KT:
                    qk_stat(i, 1)

            for m in range(KT):
                if m == 0:
                    pe.wait_ge(sem("attn_done"), HEADS2 - 1)
                    pe.wait_ge(sem("yn_ready"), 8)
                if m == 3:
                    pe.wait_ge(sem("attn_done"), HEADS2)
                if m == GROUPS[2][0] // P:
                    pe.wait_ge(sem("dil_scaled"), 4)
                if m >= 6:
                    pe.wait_ge(sem("y2_lo"), m - 5)
                for t in range(4):
                    ins = nc.tensor.transpose(PS[:, 2 + m % 6, P * t:P * t + P], yq[:, t, P * m:P * m + P], ident)
                ins.then_inc(sem("yt_mm"), 1)
            pe.wait_ge(sem("qms_ready"), 2 * KT)
            for m in range(KT):
                wide(U_OUT2 + m, 0, sem("y2_lo") if m == 0 else None)

            pe.wait_ge(sem("y2_lo"), KT)
            for f in range(KT):
                wide(U_MLP + f, 0, *((sem("h4_lo"), 5) if f == 0 else ()))
            for m in range(KT):
                s = U_MLP + KT + m
                down(s, 0, mahi, malo, PS[:, s % 2, :], sem("ma_lo") if m == 0 else None, 0)
            with pe.Fori(0, 2) as c:
                for f in range(KT):
                    wide(U_MLP + 2 * KT + f, c * 16)
                for m in range(KT):
                    s = U_MLP + 3 * KT + m
                    down(s, c * 16, mahi, malo, PS[:, s % 2, :], sem("ma_lo") if m == 0 else None, c * 8 + KT)
            for f in range(KT):
                wide(U_MLP + 6 * KT + f)
            for m in range(KT):
                s = U_MLP + 7 * KT + m
                down(s, 0, mahi, malo, PS[:, s % 2, :], sem("ma_lo") if m == 0 else None, 3 * KT)
    return locals()


def kernel(x, meta_tokens, g_mix_pre, g_mix_post, w_in, b_gates, ssm_lambda_re, ssm_lambda_im, ssm_b_re, ssm_b_im,
           ssm_c_re, ssm_c_im, ssm_d, ssm_log_dt, w_ssm_glu, w_qk_conv, b_qk_conv, g_head_norm, w_branch_ssm,
           w_branch_mlstm, w_out, g_ffn_pre, g_ffn_post, w_ffn_gate, w_ffn_up, w_ffn_conv, b_ffn_conv, w_ffn_down,
           attn_norm_2, w_in_2, b_forget_2, q_gain_2, k_gain_2, out_gain_2, w_out_2, mlp_norm_2, w_up_2, w_down_2):
    import concourse.bacc as bacc
    from concourse.bass_utils import run_bass_kernel_spmd

    def unit(w, m, k0=0, n=KT):
        t = np.zeros((P, KT, P), np.float32)
        t[:, :n] = w[P * k0:P * (k0 + n), P * m:P * m + P].reshape(n, P, P).transpose(1, 0, 2)
        return t.reshape(P, KT * P)

    w1, w2 = np.asarray(w_in)[0], np.asarray(w_in_2)[0]
    c0 = SSM_W + 4 * 512
    gates = np.zeros((D_MODEL, P), np.float32)
    gates[:, 0:HEADS1] = w1[:, c0:c0 + HEADS1]
    gates[:, 32:32 + HEADS1] = w1[:, c0 + HEADS1:c0 + 2 * HEADS1]
    units = [unit(w1, m) for m in range(CT)] + [unit(gates, 0)]
    units += [unit(w1[:, SSM_W:], m) for m in range(16)]
    units += [unit(w1[:, c0 + 2 * HEADS1:], m) for m in range(2 * KT)]
    glu = np.asarray(w_ssm_glu)[0]
    units += [np.concatenate([unit(glu, 2 * j, 0, CT)[:, :512], unit(glu, 2 * j + 1, 0, CT)[:, :512]], 1)
              for j in range(2)]
    wa, wb = np.asarray(w_branch_ssm)[0], np.asarray(w_branch_mlstm)[0]
    units += [np.concatenate([unit(wa, m, 0, CT)[:, :512], unit(wb, m, 0, CT)[:, :512]], 1) for m in range(KT)]
    units += [unit(np.asarray(w_out)[0], m) for m in range(KT)]
    wg, wu, wd = np.asarray(w_ffn_gate)[0], np.asarray(w_ffn_up)[0], np.asarray(w_ffn_down)[0]
    f0 = 0
    for tiles in FFN_CHUNKS:
        for f in range(f0, f0 + tiles):
            units += [unit(wg, f), unit(wu, f)]
        units += [unit(wd, m, f0, tiles) for m in range(KT)]
        f0 += tiles
    v0, f2 = 2 * D_MODEL, 3 * D_MODEL
    units += [unit(w2[:, v0:], m) for m in range(KT)] + [unit(w2[:, f2:], 0)]
    for i in range(KT):
        units += [unit(w2, i), unit(w2, KT + i)]
    units += [unit(w2[:, f2 + N_FOX:], m) for m in range(3)]
    units += [unit(np.asarray(w_out_2)[0], m) for m in range(KT)]
    wup, wdn = np.asarray(w_up_2)[0], np.asarray(w_down_2)[0]
    for c in range(MLP_CHUNKS):
        units += [unit(wup, KT * c + f) for f in range(KT)] + [unit(wdn, m, KT * c) for m in range(KT)]
    w_units = np.stack(units)
    assert w_units.shape[0] == UNITS

    tokens = np.concatenate([np.asarray(meta_tokens), np.asarray(x)[0]], 0)
    x_t = np.ascontiguousarray(tokens.T.reshape(KT, P, T1).transpose(1, 0, 2)).reshape(P, KT * T1)

    def feats(a):
        return np.asarray(a).reshape(-1, P).T

    def top(a):
        t = np.zeros((P, 1), np.float32)
        t[:len(a), 0] = a
        return t

    def pairs(a):
        return np.asarray(a).reshape(PAIRS, P).T

    parts = {
        "g_mix_pre": feats(g_mix_pre[0]), "g_mix_post": feats(g_mix_post[0]), "g_ffn_pre": feats(g_ffn_pre[0]),
        "g_ffn_post": feats(g_ffn_post[0]), "b_qk": feats(b_qk_conv[0]),
        "w_qk": np.concatenate([feats(w_qk_conv[0][k]) for k in range(4)], 1),
        "g_head": feats(g_head_norm[0]), "ssm_d": feats(ssm_d[0]), "attn_norm": feats(attn_norm_2[0]),
        "mlp_norm": feats(mlp_norm_2[0]), "out_gain": feats(out_gain_2[0]), "q_gain": feats(q_gain_2[0]),
        "k_gain": feats(k_gain_2[0]),
        "ffn_conv": np.stack([feats(w_ffn_conv[0][k]) for k in range(3)] + [feats(b_ffn_conv[0])], 2).reshape(P, -1),
        "lam_re": pairs(ssm_lambda_re[0]), "lam_im": pairs(ssm_lambda_im[0]),
        "log_dt": pairs(np.repeat(np.asarray(ssm_log_dt)[0][:, None], SSM_STATE, 1)),
        "b_i": top(np.asarray(b_gates)[0][:HEADS1]), "b_f": top(np.asarray(b_gates)[0][HEADS1:]),
        "b_forget": top(np.asarray(b_forget_2)[0]),
    }
    cols = np.concatenate([parts[name] for name, _ in _COLS], 1).astype(np.float32)

    p, f = np.arange(P)[:, None], np.arange(P)[None, :]
    consts = np.concatenate([p == f, np.ones((P, P)), p // HD == f // HD, np.where(p > f, NEG, 0.0),
                             np.where(f > p, NEG, 0.0)], 1).astype(np.float32)
    sel = np.zeros((36, HEADS1, P), np.float32)
    for h in range(HEADS1):
        sel[h, h] = sel[32 + h, h] = 1.0
    n_alibi = HEADS2 - N_FOX
    slopes = np.exp2(-8.0 * np.arange(1, n_alibi + 1, dtype=np.float32) / n_alibi).astype(np.float32)
    alibi = np.zeros((HEADS2, SEQ), np.float32)
    n_dil = n_alibi - N_MOBA
    for h in range(N_MOBA):
        alibi[h] = slopes[n_dil + h] * np.arange(SEQ, dtype=np.float32)
    for h in range(n_dil):
        alibi[N_MOBA + N_FOX + h] = slopes[h] * np.arange(SEQ, dtype=np.float32)
    d = p + 3 * P - np.arange(SEQ)[None, :]
    count = (d >= 0) * ((d <= 128) * 1 + ((d % 4 == 0) & (d <= 512)) + ((d % 16 == 0) & (d <= 2048)))
    dil = np.concatenate([np.where(count > 0, 0.0, NEG), count], 1).astype(np.float32)

    def diagonal(re, im):
        t = np.zeros((2, SSM_STATE, 2, PAIRS, 2, SSM_GROUP), np.float32)
        for k, a in enumerate((re, im)):
            for g in range(2):
                t[g, :, k, :, g, :] = a.reshape(PAIRS, 2, SSM_STATE, SSM_GROUP)[:, g].transpose(1, 0, 2)
        return t.reshape(P, -1)

    ssm_b = diagonal(np.asarray(ssm_b_re)[0], np.asarray(ssm_b_im)[0])
    ssm_c = diagonal(*(np.ascontiguousarray(np.asarray(a)[0].transpose(0, 2, 1)) for a in (ssm_c_re, ssm_c_im)))

    arrays = {"w_units": w_units, "x_t": x_t, "cols": cols, "consts": consts, "sel": sel.reshape(36, -1),
              "ssm_b": ssm_b, "ssm_c": ssm_c, "alibi": alibi, "dil": dil}
    nc = bacc.Bacc("TRN2", target_bir_lowering=False, num_devices=1)
    aps = [nc.dram_tensor(name, a.shape, mybir.dt.float32, kind="ExternalInput").ap() for name, a in arrays.items()]
    out = nc.dram_tensor("out", (P, KT * SEQ), mybir.dt.float32, kind="ExternalOutput").ap()
    build(nc, *aps, out)
    r = run_bass_kernel_spmd(nc, [{name: np.ascontiguousarray(a) for name, a in arrays.items()}], core_ids=[0])
    res = np.asarray(r.results[0]["out"]).reshape(P, KT, SEQ)
    return res.transpose(2, 1, 0).reshape(1, SEQ, D_MODEL)
```
